# Optimizing a Trainium2 kernel written in Bass

```python
import math
import jax, jax.numpy as jnp
from jax import lax
import numpy as np

D_MODEL = 1024
BATCH = 1
SEQ = 512
DEPTH = 2

GRID_W = 64
CTX_LEN = 256
D_MIX = D_MODEL
F_GROUPS = 4
F_GROUP_DIM = 64
F_WIDTH = F_GROUPS * F_GROUP_DIM
MLA_HEADS = 8
QK_NOPE_DIM = 64
QK_ROPE_DIM = 32
V_HEAD_DIM = 64
MLA_WIDTH = MLA_HEADS * V_HEAD_DIM
Q_LORA_RANK = 256
KV_LORA_RANK = 128
CONV_WIDTH = D_MIX - F_WIDTH - MLA_WIDTH
CONV_KERNEL = 31
D_IN = F_WIDTH + Q_LORA_RANK + KV_LORA_RANK + QK_ROPE_DIM + 2 * CONV_WIDTH
SPLITS = (F_WIDTH,
          F_WIDTH + Q_LORA_RANK,
          F_WIDTH + Q_LORA_RANK + KV_LORA_RANK,
          F_WIDTH + Q_LORA_RANK + KV_LORA_RANK + QK_ROPE_DIM)
D_FF = 4 * D_MODEL
N_MOD = 6
ROPE_BASE = 10000.0
ROPE_AXIS_DIM = QK_ROPE_DIM // 2
ATTN_SCALE = (QK_NOPE_DIM + QK_ROPE_DIM) ** -0.5
Q_BLOCK = 128
EPS = 1e-6


def rms_norm(x, g):
    xf = x.astype(jnp.float32)
    y = xf * lax.rsqrt(jnp.mean(jnp.square(xf), axis=-1, keepdims=True) + EPS)
    return (y * g.astype(jnp.float32)).astype(x.dtype)

def layer_norm(x, g, b):
    xf = x.astype(jnp.float32)
    mu = jnp.mean(xf, axis=-1, keepdims=True)
    xc = xf - mu
    var = jnp.mean(jnp.square(xc), axis=-1, keepdims=True)
    y = xc * lax.rsqrt(var + EPS) * g.astype(jnp.float32) + b.astype(jnp.float32)
    return y.astype(x.dtype)

def modulate(h, shift, scale):
    return h * (1 + scale) + shift

def axial_rope_angles(n_tokens):
    rows = n_tokens // GRID_W
    t = jnp.arange(rows * GRID_W)
    row = (t // GRID_W).astype(jnp.float32)
    col = (t % GRID_W).astype(jnp.float32)
    inv = ROPE_BASE ** (-jnp.arange(0, ROPE_AXIS_DIM, 2, dtype=jnp.float32) / ROPE_AXIS_DIM)
    ang = jnp.concatenate([row[:, None] * inv, col[:, None] * inv], axis=-1)
    return jnp.cos(ang), jnp.sin(ang)

def apply_rope(x, cos, sin):
    half = QK_ROPE_DIM // 2
    x1, x2 = x[..., :half], x[..., half:]
    cos = cos.astype(x.dtype)
    sin = sin.astype(x.dtype)
    return jnp.concatenate([x1 * cos - x2 * sin, x1 * sin + x2 * cos], axis=-1)

def fourier_mix(zf, w_f):
    B, N, _ = zf.shape
    u = zf.reshape(B, N, F_GROUPS, F_GROUP_DIM).astype(jnp.float32)
    y = jnp.fft.fftn(u, axes=(1, 3), norm="ortho").real
    return y.reshape(B, N, F_WIDTH).astype(zf.dtype) @ w_f

def conformer_conv(zg, w_dw, b_dw, ln_g, ln_b, w_pw2):
    a, g = jnp.split(zg, 2, axis=-1)
    u = a * jax.nn.sigmoid(g)
    pad = CONV_KERNEL // 2
    u = lax.conv_general_dilated(u, w_dw[:, None, :], window_strides=(1,),
                                 padding=((pad, pad),),
                                 dimension_numbers=("NWC", "WIO", "NWC"),
                                 feature_group_count=CONV_WIDTH) + b_dw
    u = jax.nn.silu(layer_norm(u, ln_g, ln_b))
    return u @ w_pw2

def mla_queries(cq, q_g, w_uq):
    B, N, _ = cq.shape
    q = (rms_norm(cq, q_g) @ w_uq).reshape(B, N, MLA_HEADS, QK_NOPE_DIM + QK_ROPE_DIM)
    return q[..., :QK_NOPE_DIM], q[..., QK_NOPE_DIM:]

def mla_keys_values(ckv, kv_g, w_ukv):
    B, N, _ = ckv.shape
    kv = (rms_norm(ckv, kv_g) @ w_ukv).reshape(B, N, MLA_HEADS, QK_NOPE_DIM + V_HEAD_DIM)
    return kv[..., :QK_NOPE_DIM], kv[..., QK_NOPE_DIM:]

def mla_attend(qn, qr, kn, kr, v):
    s = jnp.einsum("bqhd,bkhd->bhqk", qn, kn) + jnp.einsum("bqhr,bkr->bhqk", qr, kr)
    p = jax.nn.softmax(s.astype(jnp.float32) * ATTN_SCALE, axis=-1).astype(v.dtype)
    return jnp.einsum("bhqk,bkhd->bqhd", p, v)

def blocked_mla_attend(qn, qr, kn, kr, v):
    B, N, H, _ = qn.shape
    nblk = N // Q_BLOCK

    def to_blocks(q):
        return q.reshape(B, nblk, Q_BLOCK, H, q.shape[-1]).transpose(1, 0, 2, 3, 4)

    out = lax.map(lambda qs: mla_attend(qs[0], qs[1], kn, kr, v), (to_blocks(qn), to_blocks(qr)))
    return out.transpose(1, 0, 2, 3, 4).reshape(B, N, H * V_HEAD_DIM)

def first_inputs(seed: int = 0) -> dict:
    key = jax.random.key(seed)
    ks = jax.random.split(key, 24)
    f32 = jnp.float32
    L = DEPTH

    def nrm(k, shape, scale):
        return jax.random.normal(k, shape, f32) * scale

    return {
        "x": nrm(ks[0], (BATCH, SEQ, D_MODEL), 1.0),
        "c": nrm(ks[1], (BATCH, D_MODEL), 1.0),
        "ctx": nrm(ks[2], (BATCH, CTX_LEN, D_MODEL), 1.0),
        "c_ctx": nrm(ks[3], (D_MODEL,), 1.0),
        "w_mod": nrm(ks[4], (L, D_MODEL, N_MOD * D_MODEL), 0.5 * D_MODEL ** -0.5),
        "b_mod": nrm(ks[5], (L, N_MOD * D_MODEL), 0.01),
        "norm1_g": 1.0 + nrm(ks[6], (L, D_MODEL), 0.05),
        "w_in": nrm(ks[7], (L, D_MODEL, D_IN), D_MODEL ** -0.5),
        "q_norm_g": 1.0 + nrm(ks[8], (L, Q_LORA_RANK), 0.05),
        "w_uq": nrm(ks[9], (L, Q_LORA_RANK, MLA_HEADS * (QK_NOPE_DIM + QK_ROPE_DIM)), Q_LORA_RANK ** -0.5),
        "kv_norm_g": 1.0 + nrm(ks[10], (L, KV_LORA_RANK), 0.05),
        "w_ukv": nrm(ks[11], (L, KV_LORA_RANK, MLA_HEADS * (QK_NOPE_DIM + V_HEAD_DIM)), KV_LORA_RANK ** -0.5),
        "w_fourier": nrm(ks[12], (L, F_WIDTH, F_WIDTH), F_WIDTH ** -0.5),
        "w_dw": nrm(ks[13], (L, CONV_KERNEL, CONV_WIDTH), CONV_KERNEL ** -0.5),
        "b_dw": nrm(ks[14], (L, CONV_WIDTH), 0.01),
        "conv_ln_g": 1.0 + nrm(ks[15], (L, CONV_WIDTH), 0.05),
        "conv_ln_b": nrm(ks[16], (L, CONV_WIDTH), 0.01),
        "w_pw2": nrm(ks[17], (L, CONV_WIDTH, CONV_WIDTH), CONV_WIDTH ** -0.5),
        "w_o": nrm(ks[18], (L, D_MIX, D_MODEL), D_MIX ** -0.5),
        "norm2_g": 1.0 + nrm(ks[19], (L, D_MODEL), 0.05),
        "w_mlp1": nrm(ks[20], (L, D_MODEL, D_FF), D_MODEL ** -0.5),
        "w_mlp2": nrm(ks[21], (L, D_FF, D_MODEL), D_FF ** -0.5),
        "final_norm_g": 1.0 + nrm(ks[22], (D_MODEL,), 0.05),
    }

def first_block(x, c, ctx, c_ctx, w_mod, b_mod, norm1_g, w_in, q_norm_g, w_uq, kv_norm_g, w_ukv,
              w_fourier, w_dw, b_dw, conv_ln_g, conv_ln_b, w_pw2, w_o, norm2_g, w_mlp1, w_mlp2,
              final_norm_g):
    B, S, D = x.shape
    cos, sin = axial_rope_angles(S)
    silu_c = jax.nn.silu(c)
    silu_cc = jax.nn.silu(c_ctx)

    def mixer_rest(zf, zg, attn_out, l):
        y_f = fourier_mix(zf, w_fourier[l])
        y_c = conformer_conv(zg, w_dw[l], b_dw[l], conv_ln_g[l], conv_ln_b[l], w_pw2[l])
        return jnp.concatenate([y_f, attn_out, y_c], axis=-1) @ w_o[l]

    def channel_mlp(h, l):
        return jnp.square(jax.nn.relu(h @ w_mlp1[l])) @ w_mlp2[l]

    for l in range(DEPTH):
        last = l == DEPTH - 1
        mx = jnp.split((silu_c @ w_mod[l] + b_mod[l])[:, None, :], N_MOD, axis=-1)
        mc = jnp.split(silu_cc @ w_mod[l] + b_mod[l], N_MOD, axis=-1)

        zx = modulate(rms_norm(x, norm1_g[l]), mx[0], mx[1]) @ w_in[l]
        zc = modulate(rms_norm(ctx, norm1_g[l]), mc[0], mc[1]) @ w_in[l]
        fx, cqx, ckvx, krx, gx = jnp.split(zx, SPLITS, axis=-1)
        fc, cqc, ckvc, krc, gc = jnp.split(zc, SPLITS, axis=-1)

        kn_c, v_c = mla_keys_values(ckvc, kv_norm_g[l], w_ukv[l])
        kn_x, v_x = mla_keys_values(ckvx, kv_norm_g[l], w_ukv[l])
        kr_x = apply_rope(krx, cos, sin)
        qn_x, qr_x = mla_queries(cqx, q_norm_g[l], w_uq[l])
        qr_x = apply_rope(qr_x, cos[:, None, :], sin[:, None, :])

        kn_all = jnp.concatenate([kn_c, kn_x], axis=1)
        kr_all = jnp.concatenate([krc, kr_x], axis=1)
        v_all = jnp.concatenate([v_c, v_x], axis=1)
        attn_x = blocked_mla_attend(qn_x, qr_x, kn_all, kr_all, v_all)

        if not last:
            qn_c, qr_c = mla_queries(cqc, q_norm_g[l], w_uq[l])
            attn_c = mla_attend(qn_c, qr_c, kn_c, krc, v_c).reshape(B, ctx.shape[1], MLA_WIDTH)
            ctx = ctx + mc[2] * mixer_rest(fc, gc, attn_c, l)
            hc = modulate(rms_norm(ctx, norm2_g[l]), mc[3], mc[4])
            ctx = ctx + mc[5] * channel_mlp(hc, l)

        x = x + mx[2] * mixer_rest(fx, gx, attn_x, l)
        hx = modulate(rms_norm(x, norm2_g[l]), mx[3], mx[4])
        x = x + mx[5] * channel_mlp(hx, l)

    return rms_norm(x, final_norm_g)


HEAD_DIM = 64
ROPE_THETA = 10000.0
DIFF_HEADS = 4
DIFF_QK_DIM = HEAD_DIM
DIFF_V_DIM = 2 * HEAD_DIM
GQA_Q_HEADS = 8
GQA_KV_HEADS = 2
GQA_GROUP = GQA_Q_HEADS // GQA_KV_HEADS
ATTN_IN = DIFF_HEADS * (4 * DIFF_QK_DIM + DIFF_V_DIM) + (GQA_Q_HEADS + 2 * GQA_KV_HEADS) * HEAD_DIM
ATTN_OUT = DIFF_HEADS * DIFF_V_DIM + GQA_Q_HEADS * HEAD_DIM
SGU_DIM = D_MODEL
SGU_GROUPS = 4
SGU_CHUNK = 128
FFN_DIM = 2816
CONV_W = 3
N_EVEN = (DEPTH + 1) // 2
N_ODD = DEPTH // 2


def rms_norm_2(x, g):
    xf = x.astype(jnp.float32)
    y = xf * lax.rsqrt(jnp.mean(xf * xf, axis=-1, keepdims=True) + EPS)
    return (y * g.astype(jnp.float32)).astype(x.dtype)

def modulate_2(h, shift, scale):
    return h * (1 + scale) + shift

def axial_rope_tables(rows):
    n_freq = HEAD_DIM // 4
    inv = ROPE_THETA ** (-jnp.arange(n_freq, dtype=jnp.float32) / n_freq)
    row = jnp.repeat(jnp.arange(rows, dtype=jnp.float32), GRID_W)
    col = jnp.tile(jnp.arange(GRID_W, dtype=jnp.float32), rows)
    ang = jnp.concatenate([row[:, None] * inv, col[:, None] * inv], axis=-1)
    return jnp.cos(ang), jnp.sin(ang)

def apply_rope_2(x, cos, sin):
    xf = x.astype(jnp.float32).reshape(x.shape[:-1] + (x.shape[-1] // 2, 2))
    x0, x1 = xf[..., 0], xf[..., 1]
    c = cos[None, :, None, :]
    s = sin[None, :, None, :]
    out = jnp.stack([x0 * c - x1 * s, x0 * s + x1 * c], axis=-1).reshape(x.shape)
    return out.astype(x.dtype)

def attn_project(h, w_in, q_norm, k_norm, rope):
    B, S, _ = h.shape
    qk_a = DIFF_HEADS * DIFF_QK_DIM
    sizes = [qk_a, qk_a, qk_a, qk_a, DIFF_HEADS * DIFF_V_DIM,
             GQA_Q_HEADS * HEAD_DIM, GQA_KV_HEADS * HEAD_DIM, GQA_KV_HEADS * HEAD_DIM]
    splits = [int(v) for v in np.cumsum(sizes)[:-1]]
    q1, q2, k1, k2, va, qb, kb, vb = jnp.split(h @ w_in, splits, axis=-1)
    heads = lambda t, n: t.reshape(B, S, n, -1)
    q1, q2, k1, k2, va = (heads(t, DIFF_HEADS) for t in (q1, q2, k1, k2, va))
    qb = rms_norm_2(heads(qb, GQA_Q_HEADS), q_norm)
    kb = rms_norm_2(heads(kb, GQA_KV_HEADS), k_norm)
    vb = heads(vb, GQA_KV_HEADS)
    if rope is not None:
        cos, sin = rope
        q1, q2, k1, k2, qb, kb = (apply_rope_2(t, cos, sin) for t in (q1, q2, k1, k2, qb, kb))
    return q1, q2, qb, k1, k2, va, kb, vb

def diff_attend(q1, q2, k1, k2, v, lam):
    scale = DIFF_QK_DIM ** -0.5
    p1 = jax.nn.softmax(jnp.einsum('bqhd,bkhd->bhqk', q1, k1).astype(jnp.float32) * scale, axis=-1)
    p2 = jax.nn.softmax(jnp.einsum('bqhd,bkhd->bhqk', q2, k2).astype(jnp.float32) * scale, axis=-1)
    p = (p1 - lam * p2).astype(v.dtype)
    return jnp.einsum('bhqk,bkhv->bqhv', p, v)

def gqa_attend(q, k, v):
    B, Q, H, d = q.shape
    qg = q.reshape(B, Q, GQA_KV_HEADS, GQA_GROUP, d)
    s = jnp.einsum('bqgrd,bkgd->bgrqk', qg, k).astype(jnp.float32) * (d ** -0.5)
    p = jax.nn.softmax(s, axis=-1).astype(v.dtype)
    return jnp.einsum('bgrqk,bkgd->bqgrd', p, v).reshape(B, Q, H, d)

def attn_heads(q1, q2, qb, k1, k2, va, kb, vb, lam, lam_init, subln):
    B, Q = q1.shape[:2]
    oa = rms_norm_2(diff_attend(q1, q2, k1, k2, va, lam), subln) * (1 - lam_init)
    ob = gqa_attend(qb, kb, vb)
    return jnp.concatenate([oa.reshape(B, Q, -1), ob.reshape(B, Q, -1)], axis=-1)

def sweep_query_blocks(fn, qs):
    B, S = qs[0].shape[:2]
    nb = S // Q_BLOCK
    blocks = tuple(jnp.moveaxis(q.reshape((B, nb, Q_BLOCK) + q.shape[2:]), 1, 0) for q in qs)
    out = lax.map(lambda qb: fn(*qb), blocks)
    return jnp.moveaxis(out, 0, 1).reshape(B, S, out.shape[-1])

def attention_mixer(h_lat, h_ctx, w_in, w_out, lq1, lk1, lq2, lk2, subln, q_norm, k_norm,
                    lam_init, rope, with_ctx_out):
    lat = attn_project(h_lat, w_in, q_norm, k_norm, rope)
    ctx = attn_project(h_ctx, w_in, q_norm, k_norm, None)
    lam = (jnp.exp(jnp.sum(lq1.astype(jnp.float32) * lk1.astype(jnp.float32)))
           - jnp.exp(jnp.sum(lq2.astype(jnp.float32) * lk2.astype(jnp.float32))) + lam_init)
    K1, K2, VA, KB, VB = (jnp.concatenate([ctx[i], lat[i]], axis=1) for i in range(3, 8))
    lat_fn = lambda q1b, q2b, qbb: attn_heads(q1b, q2b, qbb, K1, K2, VA, KB, VB, lam, lam_init, subln)
    y_lat = sweep_query_blocks(lat_fn, lat[:3]) @ w_out
    y_ctx = None
    if with_ctx_out:
        y_ctx = attn_heads(*ctx, lam, lam_init, subln) @ w_out
    return y_lat, y_ctx

def sgu_mixer(h, w_in, v_norm, w_s, b_s, w_out):
    B, S, _ = h.shape
    z = jax.nn.gelu(h @ w_in, approximate=False)
    u, v = jnp.split(z, 2, axis=-1)
    v = rms_norm_2(v, v_norm)
    n = S // SGU_CHUNK
    vg = v.reshape(B, n, SGU_CHUNK, SGU_GROUPS, SGU_DIM // SGU_GROUPS)
    mixed = jnp.einsum('gpq,bnqgc->bnpgc', w_s, vg) + b_s.T[:, :, None]
    return (u * mixed.reshape(B, S, SGU_DIM)) @ w_out

def conv_ffn(h, w_up, conv_w, conv_b, w_down):
    S = h.shape[1]
    z = h @ w_up
    zp = jnp.pad(z, ((0, 0), (1, 1), (0, 0)))
    z = conv_w[0] * zp[:, :S] + conv_w[1] * zp[:, 1:S + 1] + conv_w[2] * zp[:, 2:] + conv_b
    g, u = jnp.split(z, 2, axis=-1)
    return (jax.nn.silu(g) * u) @ w_down

def second_inputs(seed: int = 0) -> dict:
    key = jax.random.key(seed)
    ks = iter(jax.random.split(key, 32))
    D = D_MODEL
    nrm = lambda shape, s: jax.random.normal(next(ks), shape, jnp.float32) * s
    return {
        "x": nrm((BATCH, SEQ, D), 1.0),
        "c": nrm((BATCH, D), 1.0),
        "ctx": nrm((BATCH, CTX_LEN, D), 1.0),
        "c_ctx": nrm((D,), 1.0),
        "ada_w": nrm((DEPTH, D, N_MOD * D), 0.5 * D ** -0.5),
        "ada_b": nrm((DEPTH, N_MOD * D), 0.02),
        "mix_norm": 1.0 + nrm((DEPTH, D), 0.1),
        "ffn_norm": 1.0 + nrm((DEPTH, D), 0.1),
        "final_norm": 1.0 + nrm((D,), 0.1),
        "attn_w_in": nrm((N_EVEN, D, ATTN_IN), D ** -0.5),
        "attn_w_out": nrm((N_EVEN, ATTN_OUT, D), ATTN_OUT ** -0.5),
        "diff_lq1": nrm((N_EVEN, DIFF_QK_DIM), 0.1),
        "diff_lk1": nrm((N_EVEN, DIFF_QK_DIM), 0.1),
        "diff_lq2": nrm((N_EVEN, DIFF_QK_DIM), 0.1),
        "diff_lk2": nrm((N_EVEN, DIFF_QK_DIM), 0.1),
        "diff_subln": 1.0 + nrm((N_EVEN, DIFF_V_DIM), 0.1),
        "gqa_q_norm": 1.0 + nrm((N_EVEN, HEAD_DIM), 0.1),
        "gqa_k_norm": 1.0 + nrm((N_EVEN, HEAD_DIM), 0.1),
        "sgu_w_in": nrm((N_ODD, D, 2 * SGU_DIM), D ** -0.5),
        "sgu_v_norm": 1.0 + nrm((N_ODD, SGU_DIM), 0.1),
        "sgu_w_s": nrm((N_ODD, SGU_GROUPS, SGU_CHUNK, SGU_CHUNK), SGU_CHUNK ** -0.5),
        "sgu_b_s": 1.0 + nrm((N_ODD, SGU_GROUPS, SGU_CHUNK), 0.1),
        "sgu_w_out": nrm((N_ODD, SGU_DIM, D), SGU_DIM ** -0.5),
        "ffn_w_up": nrm((DEPTH, D, 2 * FFN_DIM), D ** -0.5),
        "ffn_conv_w": nrm((DEPTH, CONV_W, 2 * FFN_DIM), CONV_W ** -0.5),
        "ffn_conv_b": nrm((DEPTH, 2 * FFN_DIM), 0.02),
        "ffn_w_down": nrm((DEPTH, FFN_DIM, D), FFN_DIM ** -0.5),
    }

def second_block(x, c, ctx, c_ctx, ada_w, ada_b, mix_norm, ffn_norm, final_norm,
              attn_w_in, attn_w_out, diff_lq1, diff_lk1, diff_lq2, diff_lk2, diff_subln,
              gqa_q_norm, gqa_k_norm, sgu_w_in, sgu_v_norm, sgu_w_s, sgu_b_s, sgu_w_out,
              ffn_w_up, ffn_conv_w, ffn_conv_b, ffn_w_down):
    rows = x.shape[1] // GRID_W
    rope = axial_rope_tables(rows)
    last_attn = (DEPTH - 1) // 2 * 2
    s_c = jax.nn.silu(c)
    s_cc = jax.nn.silu(c_ctx)
    for l in range(DEPTH):
        i = l // 2
        is_attn = l % 2 == 0
        update_ctx = l < last_attn
        m_lat = (s_c @ ada_w[l] + ada_b[l])[:, None, :]
        sh1, sc1, g1, sh2, sc2, g2 = jnp.split(m_lat, N_MOD, axis=-1)
        h_lat = modulate_2(rms_norm_2(x, mix_norm[l]), sh1, sc1)
        if is_attn or update_ctx:
            m_ctx = s_cc @ ada_w[l] + ada_b[l]
            csh1, csc1, cg1, csh2, csc2, cg2 = jnp.split(m_ctx, N_MOD, axis=-1)
            h_ctx = modulate_2(rms_norm_2(ctx, mix_norm[l]), csh1, csc1)
        if is_attn:
            lam_init = 0.8 - 0.6 * math.exp(-0.3 * l)
            y_lat, y_ctx = attention_mixer(h_lat, h_ctx, attn_w_in[i], attn_w_out[i],
                                           diff_lq1[i], diff_lk1[i], diff_lq2[i], diff_lk2[i],
                                           diff_subln[i], gqa_q_norm[i], gqa_k_norm[i],
                                           lam_init, rope, update_ctx)
        else:
            y_lat = sgu_mixer(h_lat, sgu_w_in[i], sgu_v_norm[i], sgu_w_s[i], sgu_b_s[i], sgu_w_out[i])
            if update_ctx:
                y_ctx = sgu_mixer(h_ctx, sgu_w_in[i], sgu_v_norm[i], sgu_w_s[i], sgu_b_s[i], sgu_w_out[i])
        x = x + g1 * y_lat
        x = x + g2 * conv_ffn(modulate_2(rms_norm_2(x, ffn_norm[l]), sh2, sc2),
                              ffn_w_up[l], ffn_conv_w[l], ffn_conv_b[l], ffn_w_down[l])
        if update_ctx:
            ctx = ctx + cg1 * y_ctx
            ctx = ctx + cg2 * conv_ffn(modulate_2(rms_norm_2(ctx, ffn_norm[l]), csh2, csc2),
                                       ffn_w_up[l], ffn_conv_w[l], ffn_conv_b[l], ffn_w_down[l])
    return rms_norm_2(x, final_norm)


def setup_inputs(seed=0):
    out = dict(first_inputs(seed))
    for name, value in second_inputs(seed + 1).items():
        if name != "x":
            out[name + "_2"] = value
    return out


def reference(
    x, c, ctx, c_ctx, w_mod, b_mod, norm1_g, w_in, q_norm_g, w_uq, kv_norm_g, w_ukv, w_fourier,
    w_dw, b_dw, conv_ln_g, conv_ln_b, w_pw2, w_o, norm2_g, w_mlp1, w_mlp2, final_norm_g, c_2,
    ctx_2, c_ctx_2, ada_w_2, ada_b_2, mix_norm_2, ffn_norm_2, final_norm_2, attn_w_in_2,
    attn_w_out_2, diff_lq1_2, diff_lk1_2, diff_lq2_2, diff_lk2_2, diff_subln_2, gqa_q_norm_2,
    gqa_k_norm_2, sgu_w_in_2, sgu_v_norm_2, sgu_w_s_2, sgu_b_s_2, sgu_w_out_2, ffn_w_up_2,
    ffn_conv_w_2, ffn_conv_b_2, ffn_w_down_2,
):
    x = first_block(
        x, c, ctx, c_ctx, w_mod, b_mod, norm1_g, w_in, q_norm_g, w_uq, kv_norm_g, w_ukv,
        w_fourier, w_dw, b_dw, conv_ln_g, conv_ln_b, w_pw2, w_o, norm2_g, w_mlp1, w_mlp2,
        final_norm_g,
    )
    return second_block(
        x, c_2, ctx_2, c_ctx_2, ada_w_2, ada_b_2, mix_norm_2, ffn_norm_2, final_norm_2,
        attn_w_in_2, attn_w_out_2, diff_lq1_2, diff_lk1_2, diff_lq2_2, diff_lk2_2, diff_subln_2,
        gqa_q_norm_2, gqa_k_norm_2, sgu_w_in_2, sgu_v_norm_2, sgu_w_s_2, sgu_b_s_2, sgu_w_out_2,
        ffn_w_up_2, ffn_conv_w_2, ffn_conv_b_2, ffn_w_down_2,
    )


_drawn_inputs = setup_inputs


def setup_inputs(seed=0):
    import zlib

    import numpy as np

    out = dict(_drawn_inputs(seed))
    spreads = {}
    factors = {'ctx': 4.949,
     'norm1_g': 4.986,
     'q_norm_g': 8.0,
     'kv_norm_g': 8.0,
     'b_dw': 8.0,
     'conv_ln_g': 6.729,
     'conv_ln_b': 8.0,
     'diff_lq1_2': 2.945,
     'diff_lk1_2': 2.75,
     'diff_lq2_2': 3.609,
     'diff_lk2_2': 3.099,
     'diff_subln_2': 4.478,
     'gqa_q_norm_2': 8.0,
     'gqa_k_norm_2': 8.0,
     'sgu_b_s_2': 2.717,
     'ffn_conv_b_2': 7.018,
     'sgu_v_norm_2': 3.3}
    for name, (base, spread) in spreads.items():
        noise = np.random.default_rng([zlib.crc32(name.encode()), seed]).standard_normal(out[name].shape)
        drawn = base * np.exp(spread * noise) if base else spread * noise
        out[name] = __import__('jax').numpy.asarray(drawn.astype(out[name].dtype))
    for name, factor in factors.items():
        out[name] = (out[name] * factor).astype(out[name].dtype)
    return out
```

```python
from contextlib import ExitStack

import numpy as np

import concourse.bass as bass
from concourse import mybir

F32 = mybir.dt.float32
F32R = mybir.dt.float32r
ACT = mybir.ActivationFunctionType
ALU = mybir.AluOpType
AX = mybir.AxisListType

P = 128
D = 1024
KD = D // P
NC_, NX = 256, 512
T = NC_ + NX
CTX, LAT, ALL = (0, NC_), (NC_, T), (0, T)
EPS = 1e-6
GRID_W = 64
CH = 6 * KD
TAPS = 31
PAD = TAPS // 2
UW = PAD + NC_ + PAD + NX + PAD
CW = NC_ + PAD + NX
HEADS, NOPE, ROPE = 8, 64, 32
MLA_SCALE = (NOPE + ROPE) ** -0.5
HD = 64
GQA_SCALE = HD ** -0.5
QUARTERS, QK = 4, 8
FFN_T = 22
FFN_PARTS = (12, 10)
LAM_INIT = 0.2

VEC_SIZES = [("bias", 4 * CH), ("norm1", 16), ("norm2", 16), ("fin1", 8), ("qn", 4), ("kvn", 2),
             ("dw", 4 * TAPS), ("bdw", 4), ("lng", 4), ("lnb", 4), ("mixn", 16), ("ffnn", 16),
             ("fin2", 8), ("subln", 1), ("gq", 1), ("gk", 1), ("vn", 8), ("lam", 4),
             ("fcw", 2 * 3 * 44), ("fcb", 2 * 44)]
VEC, _at = {}, 0
for _name, _size in VEC_SIZES:
    VEC[_name] = _at
    _at += _size
NVEC = _at

IN_TILES, OUT_TILES = 10, 8
MLP_STEPS = 16
QK_TILES, V_TILES = 13, 5
SGU_U, SGU_V = 8, 8
N_IN = [0, IN_TILES + OUT_TILES + QUARTERS * MLP_STEPS]
N_BLOCK2 = 2 * N_IN[1]
N_FFN = [N_BLOCK2 + QK_TILES + V_TILES + OUT_TILES]
FFN_TILES = sum(2 * k + k for k in FFN_PARTS)
N_SGU = N_FFN[0] + FFN_TILES
N_FFN.append(N_SGU + SGU_U + SGU_V + OUT_TILES)
N_TILES = N_FFN[1] + FFN_TILES
MOD_TILES = 4 * CH
RAW = 4
QK_ORDER = ([("q", 4 + i) for i in range(4)] + [("k", 4)] + [("q", i) for i in range(4)]
            + [("k", i) for i in range(4)])
N_NORMED = 5
NORMS = 10
MOD_AFTER = [{3: 1, 7: 1, 11: 1}, {1: 1, 3: 1, 5: 1, 7: 1, 9: 1, 11: 1}]


def two_towers(nc, a):
    ctx = ExitStack()
    with ctx:
        base = nc.sbuf_base
        base += -base % 32
        cursor = [base]

        def at(name, cols, dt=F32, offset=None):
            if offset is None:
                offset = cursor[0]
                cursor[0] += -(-4 * cols // 32) * 32
            return nc.alloc_sbuf_tensor_at(name, [P, cols], dt, offset=offset), offset

        res, _ = at("residual", KD * T)
        hi_f, o_hi = at("in_hi", KD * T, F32R)
        lo_f, o_lo = at("in_lo", KD * T, F32R)
        hid_hi_f, o_c = at("hidden_hi", QK * T, F32R)
        hid_lo_f, o_c2 = at("hidden_lo", QK * T, F32R)
        raw, _ = at("w_raw", RAW * 1024)
        whi, _ = at("w_hi", 2 * 1024, F32R)
        wlo, _ = at("w_lo", 2 * 1024, F32R)
        mod_w, _ = at("mod_w", 4 * 1024)
        small_w, o_sw = at("small_w", 4096)
        vec, _ = at("vectors", NVEC)
        mod, _ = at("modulation", 2 * MOD_TILES)
        cvec, _ = at("conditions", 4 * KD)
        scvec, _ = at("silu_conditions", 4 * KD)
        coef, _ = at("coefficients", 64)
        ident, _ = at("identity", P)
        ones, _ = at("ones", P)
        halves, _ = at("half_ones", P)
        swap, _ = at("pair_swap", P)
        chan_dft, _ = at("channel_dft", 256)
        rstd, _ = at("rstd", T)
        tmp, o_tmp = at("scratch", 2 * T)
        rope, _ = at("rope", 2 * NX)
        rtmp, _ = at("rope_scratch", NX)
        tiny, _ = at("tiny", 64)
        cbuf, _ = at("mixer_space", 2 * QK * T, F32, o_c)
        h_f, _ = at("in_hi_space", KD * T, F32, o_hi)
        l_f, _ = at("in_lo_space", KD * T, F32, o_lo)

        res3 = res[:, :].rearrange("p (k t) -> p k t", k=KD)
        hi3 = hi_f[:, :].rearrange("p (k t) -> p k t", k=KD)
        lo3 = lo_f[:, :].rearrange("p (k t) -> p k t", k=KD)
        hid_hi3 = hid_hi_f[:, :].rearrange("p (k t) -> p k t", k=QK)
        hid_lo3 = hid_lo_f[:, :].rearrange("p (k t) -> p k t", k=QK)
        tmp2 = tmp[:, :].rearrange("p (s t) -> p s t", s=2)
        raw3 = raw[:, :].rearrange("p (s n) -> p s n", s=RAW)
        whi3 = whi[:, :].rearrange("p (s k m) -> p s k m", s=2, k=8)
        wlo3 = wlo[:, :].rearrange("p (s k m) -> p s k m", s=2, k=8)
        mod_w3 = mod_w[:, :].rearrange("p (s k m) -> p s k m", s=4, k=8)
        mod3 = mod[:, :].rearrange("p (m v) -> p m v", v=2)
        rope3 = rope[:, :].rearrange("p (s t) -> p s t", s=2)
        uq = small_w[:, 0:2048].rearrange("p (h k m) -> p h k m", h=8, k=2)
        uk = small_w[:, 2048:2560].rearrange("p (h m) -> p h m", h=8)
        uv = small_w[:, 2560:3072]
        wf = small_w[:, 3072:3584].rearrange("p (m k c) -> p m k c", m=2, k=2)
        wp = small_w[:, 3584:4096].rearrange("p (m k c) -> p m k c", m=2, k=2)

        def region(first, k, width):
            return cbuf[:, first:first + k * width].rearrange("p (k t) -> p k t", k=k)

        cq = region(0, 2, T)
        ckv = region(1536, 1, T)
        u_pad = region(2304, 2, UW)
        conv = region(3930, 2, CW)
        sgate = region(3930, 2, T)
        v1 = region(5496, 6, 512)
        qbuf = region(8568, 2, T)
        kbuf = region(10104, 2, T)
        zf = qbuf
        dft_x = h_f[:, 1536:1536 + 4096].rearrange("p (s k n) -> p s k n", s=2, k=4)
        dft_c = l_f[:, 4608:4608 + 1024].rearrange("p (s k n) -> p s k n", s=2, k=2)
        ab = l_f[:, 1536:1536 + 3072].rearrange("p (k n) -> p k n", k=6)
        pt1 = [h_f[:, 6 * T:8 * T].rearrange("p (k q) -> p k q", k=6),
               l_f[:, 6 * T:8 * T].rearrange("p (k q) -> p k q", k=6)]
        q2 = region(0, 8, NX)
        k2 = region(4096, 5, T)
        v2 = region(4096 + 3840, 6, 640)
        mix_hi = hi_f[:, 0:8 * NX].rearrange("p (k t) -> p k t", k=8)
        mix_lo = lo_f[:, 0:8 * NX].rearrange("p (k t) -> p k t", k=8)
        pt2 = [h_f[:, 8 * NX:8 * NX + 1536].rearrange("p (k q) -> p k q", k=6),
               l_f[:, 8 * NX:8 * NX + 1536].rearrange("p (k q) -> p k q", k=6)]
        diff_out = small_w[:, 0:2048].rearrange("p (k t) -> p k t", k=4)
        more_p = small_w[:, 2048:2048 + 2 * T].rearrange("p (s t) -> p s t", s=2)
        su = region(0, 8, NX)
        sv = region(4096, 4, 1024)
        ws = small_w[:, 0:512].rearrange("p (g c) -> p g c", g=4)
        bs = small_w[:, 512:1024].rearrange("p (g c) -> p g c", g=4)
        fh_hi = hid_hi_f[:, :].rearrange("p (k t) -> p k t", t=NX)
        fh_lo = hid_lo_f[:, :].rearrange("p (k t) -> p k t", t=NX)
        gates = small_w[:, 1024:2048].rearrange("p (s t) -> p s t", s=2)
        ups = small_w[:, 2048:3072].rearrange("p (s t) -> p s t", s=2)
        prods = tmp[:, 0:1024].rearrange("p (s t) -> p s t", s=2)

        psum = ctx.enter_context(nc.psum_tensor("psum", [P, 8, 512], F32))

        def bank(b, r0=0, r1=P, c0=0, c1=512):
            return psum[r0:r1, b, c0:c1]

        def V(name, i=0, n=1):
            return vec[:, VEC[name] + i:VEC[name] + i + n]

        def M(block, chunk, k, which):
            return mod3[:, block * CH + chunk * KD + k, which:which + 1]

        def both(layer_segs):
            return [(CTX, 0), (LAT, 1)] if layer_segs == ALL else [(LAT, 1)]

        def w(t):
            return t[1] - t[0]

        def sem(name):
            return ctx.enter_context(nc.semaphore(name))

        loaded = sem("constants_loaded")
        late = {n: sem(f"{n}_loaded") for n in ("dft", "small_w", "rope2", "context2", "sgu")}
        w_landed = [sem(f"w_landed{i}") for i in range(RAW)]
        m_landed = [sem(f"m_landed{i}") for i in range(4)]
        hi_ready = sem("w_hi_ready")
        lo_ready = sem("w_lo_ready")
        tile_done = sem("tile_done")
        drained = [sem("drained_even"), sem("drained_odd")]
        mod_done = sem("mod_done")
        mod_drained = sem("mod_drained")
        silu_ready = sem("silu_ready")
        const_ready = sem("const_ready")
        sq_ready = sem("norm_squares")
        sum_ready = sem("norm_sums")
        rstd_ready = sem("rstd_ready")
        scaled = sem("norm_scaled")
        norm_hi = sem("norm_hi")
        norm_out = sem("norm_out")
        squared = sem("hid_squared")
        hid_hi = sem("hid_hi")
        hid_ready = sem("hid_ready")
        a_chain, d_chain, p_chain = sem("act_chain"), sem("dve_chain"), sem("pe_chain")
        out_done = sem("out_done")

        class Chain:

            def __init__(self, eng, s):
                self.eng, self.s, self.n, self.plus = eng, s, 0, 0

            def mark(self, ins):
                ins.then_inc(self.s, 1)
                self.n += 1
                return self.n

            def wait(self, n=None):
                self.eng.wait_ge(self.s, (self.n if n is None else n) + self.plus)

        def per_layer(names):
            return [{n: sem(f"{n}_{i}") for n in names} for i in (0, 1)]

        m1 = per_layer(["ckv_in", "ckv_sum", "lora_sums", "lora_ready", "v_mm", "v_cp",
                        "ab_mm", "ab_cp", "y_mm", "y_cp", "f_mm", "f_hi", "f_lo",
                        "u_ready", "post"])
        att_names = ["scores", "maxed", "exped", "p_ready", "tA", "tB", "evA", "evB",
                     "pv", "pv_hi", "pv_lo", "proj", "proj_act", "proj_dve"]
        att = [{n: sem(f"att{i}_{n}") for n in att_names} for i in range(3)]
        s2 = {n: sem("b2_" + n) for n in ["raw", "sq", "sum", "normed", "perm", "roped",
                                          "sub_sq", "sub_sum", "sub_r", "mixed", "mix_t", "mix_hi",
                                          "mix_lo", "g_ready", "prod", "f_hi", "f_lo", "sv",
                                          "lam"]}

        def mla_plan(layer):
            steps, units = [], []
            for h in range(HEADS):
                chunks = ([(0, NC_)] if layer == 0 else []) + [(NC_, T), (NC_ + 256, T)]
                for q0, nk in chunks:
                    u = len(units)
                    units.append(dict(nk=nk, h=h, q0=q0, rows=(64 * (h % 2), 64 * (h % 2) + 64),
                                      lo=True))
                    for j in range(2):
                        steps.append(dict(unit=u, half=j, nk=nk, h=h, post="plain",
                                          q=qbuf[0:96, h % 2, q0 + j * P:q0 + (j + 1) * P],
                                          k=kbuf[0:96, h % 2, :], p=len(steps) % 2))
            return steps, units

        def gqa_plan():
            steps, units = [], []
            for h in range(4):
                for q0 in (0, 256):
                    u = len(units)
                    units.append(dict(nk=T, h=h, q0=q0, rows=(0, P), lo=False, kind="diff"))
                    r = 64 * (h % 2)
                    for j in range(2):
                        for i, post in enumerate(("first", "second")):
                            qs = q2[r:r + 64, 2 * i + h // 2, q0 + j * P:q0 + (j + 1) * P]
                            steps.append(dict(unit=u, half=j, nk=T, h=h, post=post, q=qs,
                                              k=k2[r:r + 64, 2 * i + h // 2, :], p=len(steps) % 4))
            for h in range(8):
                for q0 in (0, 256):
                    u = len(units)
                    r = 64 * (h % 2)
                    units.append(dict(nk=T, h=h, q0=q0, rows=(r, r + 64), lo=True, kind="gqa"))
                    for j in range(2):
                        steps.append(dict(unit=u, half=j, nk=T, h=h, post="plain",
                                          q=q2[r:r + 64, 4 + h // 2, q0 + j * P:q0 + (j + 1) * P],
                                          k=k2[r:r + 64, 4, :], p=len(steps) % 4))
            return steps, units

        def index(steps, units):
            t = b = 0
            for s in steps:
                s["t"] = s["b"] = None
                s["t_before"], s["b_before"] = t, b
                if s["post"] != "first":
                    s["t"] = t
                    t += 1
                    if s["nk"] > 384:
                        s["b"] = b
                        b += 1
            lo = 0
            for u in units:
                u["lo_before"] = lo
                lo += u["lo"]
            for n, u in enumerate(units):
                last = [s for s in steps if s["unit"] == n][-1]
                u["t_end"] = last["t"] + 1
                u["b_end"] = last["b_before"] + (last["b"] is not None)

        plans = [mla_plan(0), mla_plan(1), gqa_plan()]
        for pl in plans:
            index(*pl)

        def pieces_of(layer, h):
            base_ = [("q", LAT), ("k", (0, 384)), ("k", (384, T))]
            return base_ + ([("q", CTX)] if layer == 0 else [])

        def p_slot(i):
            return tmp2[:, i, :] if i < 2 else more_p[:, i - 2, :]

        def ffn_marks():
            marks, count = {}, 0
            for layer in (0, 1):
                for part, kk in enumerate(FFN_PARTS):
                    for m in range(8):
                        if (m + 1) * kk % 8:
                            count += 1
                            marks[layer, part, m] = count
            return marks

        marks = ffn_marks()
        block = ctx.enter_context(nc.Block())

        @block.sync
        def _(sp):
            stream, mods = a["stream"], a["mods"]

            def w_load(n, j):
                tile = stream[n:n + 1] if isinstance(n, int) else stream[bass.ds(n, 1)]
                sp.dma_start(raw3[:, j, :], tile.rearrange("a p n -> p (a n)"))\
                  .then_inc(w_landed[j], 16)

            def w_step(n, j):
                sp.wait_ge(lo_ready, n + 1)
                w_load(n + RAW, j)

            def w_steps(n0, count):
                count = min(count, N_TILES - RAW - n0)
                if count >= 8:
                    with sp.Fori(0, count // 4) as i:
                        for j in range(4):
                            w_step(i * 4 + (n0 + j), (n0 + j) % 4)
                for n in range(n0 + (count // 4 * 4 if count >= 8 else 0), n0 + count):
                    w_step(n, n % 4)

            def m_group(g):
                for j in range(4):
                    sp.wait_ge(mod_done, g * 4 + (j + 1))
                    m = g * 4 + (4 + j)
                    tile = mods[m:m + 1] if isinstance(m, int) else mods[bass.ds(m, 1)]
                    sp.dma_start(mod_w[:, j * 1024:(j + 1) * 1024], tile.rearrange("a p n -> p (a n)"))\
                      .then_inc(m_landed[j], 16)

            for j in range(4):
                sp.dma_start(mod_w[:, j * 1024:(j + 1) * 1024], mods[j]).then_inc(m_landed[j], 16)
            for n in range(RAW):
                w_load(n, n)
            with sp.Fori(0, CH // 4) as g:
                m_group(g)
            groups = CH // 4
            for layer in (0, 1):
                n0 = N_IN[layer]
                w_steps(n0, IN_TILES)
                sp.wait_ge(tile_done, n0 + IN_TILES)
                sp.dma_start(h_f[:, 1536:1536 + 4096], a["dft_x"]).then_inc(late["dft"], 16)
                sp.dma_start(l_f[:, 4608:4608 + 1024], a["dft_c"]).then_inc(late["dft"], 16)
                w_steps(n0 + IN_TILES, OUT_TILES)
                sp.wait_ge(tile_done, n0 + IN_TILES + 1)
                if layer == 0:
                    sp.dma_start(small_w[:, :], a["small_w"][1]).then_inc(late["small_w"], 16)
                else:
                    sp.dma_start(rope[:, :], a["rope2"]).then_inc(late["rope2"], 16)
                n1 = n0 + IN_TILES + OUT_TILES
                after = MOD_AFTER[layer]
                per = len(after)
                last_groups = layer == 1

                def quarter(i, ends=False):
                    seen = 0
                    for j in range(MLP_STEPS):
                        w_step(i * MLP_STEPS + (n1 + j), (n1 + j) % 4)
                        if j in after:
                            seen += 1
                            if not (ends and seen == per):
                                m_group(i * per + (groups + seen - 1))

                with sp.Fori(0, QUARTERS - last_groups) as i:
                    quarter(i)
                if last_groups:
                    quarter(QUARTERS - 1, ends=True)
                groups += QUARTERS * per
            w_steps(N_BLOCK2, N_SGU - N_BLOCK2)
            sp.wait_ge(tile_done, N_FFN[0])
            sp.dma_start(small_w[:, 0:512], a["w_s"]).then_inc(late["sgu"], 16)
            sp.dma_start(small_w[:, 512:1024], a["b_s"]).then_inc(late["sgu"], 16)
            w_steps(N_SGU, N_TILES - N_SGU)
            sp.wait_ge(norm_out, KD * NORMS)
            sp.dma_start(a["out"], res3[:, :, NC_:T]).then_inc(out_done, 16)
            sp.wait_ge(out_done, 16)

        @block.gpsimd
        def _(pool):
            def w_low(n, j, free):
                pool.wait_ge(hi_ready, n + 1)
                if free:
                    pool.wait_ge(tile_done, n - 1)
                nc.gpsimd.tensor_tensor(wlo[:, (j % 2) * 1024:(j % 2 + 1) * 1024], raw3[:, j, :],
                                        whi[:, (j % 2) * 1024:(j % 2 + 1) * 1024].bitcast(F32),
                                        ALU.subtract).then_inc(lo_ready, 1)

            for n in range(4):
                w_low(n, n, n >= 2)
            with pool.Fori(0, (N_TILES - 4) // 4) as i:
                for j in range(4):
                    w_low(i * 4 + (4 + j), j, True)
            for n in range(N_TILES // 4 * 4, N_TILES):
                w_low(n, n % 4, True)

        @block.scalar
        def _(act):
            chain = Chain(act, a_chain)

            def split(n, shift=0):
                j = n % 4
                act.wait_ge(w_landed[j], shift * 4 + 16 * (n // 4 + 1))
                if n >= 2:
                    act.wait_ge(tile_done, shift + (n - 1))
                nc.scalar.activation(whi[:, (j % 2) * 1024:(j % 2 + 1) * 1024], raw3[:, j, :],
                                     ACT.Copy).then_inc(hi_ready, 1)

            def ahead(n, shift=0):
                if n + 2 < N_TILES:
                    split(n + 2, shift)

            def square(k, c0, c1, slot):
                return nc.scalar.activation(tmp2[:, slot, c0:c1], res3[:, k, c0:c1], ACT.Square)

            def inv_sqrt(dst, src, n, rows=P):
                chain.mark(nc.scalar.activation(dst, src, ACT.Ln, bias=tiny[0:rows, 0:1], scale=1.0 / n))
                chain.wait()
                return nc.scalar.activation(dst, dst, ACT.Exp, scale=-0.5)

            def norm(v, cols, wait_res, shifts):
                segs = both(cols)
                c0, c1 = cols
                wait_res()
                for k in range(KD):
                    if k >= 2:
                        act.wait_ge(sum_ready, 8 * v + k - 1)
                    square(k, c0, c1, k % 2).then_inc(sq_ready, 1)
                act.wait_ge(sum_ready, 8 * v + 8)
                for (s0, s1), b in segs:
                    last = inv_sqrt(rstd[:, s0:s1], bank(4 + b, c1=s1 - s0), D)
                last.then_inc(rstd_ready, 1)
                if shifts is None:
                    return
                for k in range(KD):
                    act.wait_ge(scaled, 8 * hi_v[0] + k + 1)
                    for (s0, s1), b in segs:
                        last = nc.scalar.activation(hi3[:, k, s0:s1], tmp2[:, k % 2, s0:s1],
                                                    ACT.Identity, bias=shifts(k, 1 - b))
                    last.then_inc(norm_hi, 1)
                hi_v[0] += 1

            hi_v = [0]

            def copy_out(t, dst, cols, func=ACT.Copy):
                segs = both(cols)
                for (s0, s1), b in segs:
                    last = nc.scalar.activation(dst(s0, s1), bank(2 * (t % 2) + b, c1=s1 - s0), func)
                last.then_inc(drained[t % 2], 1)

            def attention(s, plan, scale, hooks):
                steps, units = plan

                def exp(i):
                    st = steps[i]
                    nk, sl = st["nk"], i % 2
                    act.wait_ge(s["maxed"], i + 1)
                    back = 2 if len({x["p"] for x in steps}) == 2 else 4
                    if i >= back:
                        nt = steps[i - back]["t_before"] + 1
                        tdone(nt)
                    if nk > 384:
                        src = psum[:, 2 * sl:2 * sl + 2, 0:384]
                        dst = p_slot(st["p"])[:, 0:nk].rearrange("p (b c) -> p b c", b=2)
                    else:
                        src, dst = bank(2 * sl, c1=nk), p_slot(st["p"])[:, 0:nk]
                    nc.scalar.activation(dst, src, ACT.Exp, bias=tiny[:, 4 + i % 4:5 + i % 4],
                                         scale=scale, accum_out=tiny[:, 8 + i % 4:9 + i % 4])\
                      .then_inc(s["exped"], 1)

                def tdone(n):
                    act.wait_ge(s["tA"], n)
                    nb = sum(1 for x in steps if x["b"] is not None and x["t"] < n)
                    if nb:
                        act.wait_ge(s["tB"], nb)

                def ev_a(i):
                    st = steps[i]
                    if st["t"] is None:
                        return
                    act.wait_ge(s["tA"], st["t"] + 1)
                    if st["unit"] >= 2:
                        act.wait_ge(s["pv"], st["unit"] - 1)
                    n = min(3, st["nk"] // P)
                    pt = hooks["pt"][st["unit"] % 2]
                    nc.scalar.activation(pt[:, 0:n, st["half"] * P:(st["half"] + 1) * P],
                                         bank(4, c1=n * P).rearrange("p (k q) -> p k q", k=n),
                                         ACT.Copy).then_inc(s["evA"], 1)

                def pv_hi(u):
                    un = units[u]
                    r0, r1 = un["rows"]
                    act.wait_ge(s["pv"], u + 1)
                    nc.scalar.activation(hooks["hi"](un), bank(6, r0, r1, 0, 256), ACT.Copy)\
                      .then_inc(s["pv_hi"], 1)

                exp(0)
                for i, st in enumerate(steps):
                    if i + 1 < len(steps):
                        exp(i + 1)
                    ev_a(i)
                    if st["t"] is not None and st["half"] == 0 and st["unit"] >= 1:
                        pv_hi(st["unit"] - 1)
                    hooks["act"](i)
                pv_hi(len(units) - 1)

            act.dma_start(vec[:, :], a["vectors"]).then_inc(loaded, 16)
            act.dma_start(cvec[:, :], a["conditions"]).then_inc(loaded, 16)
            act.dma_start(res3, a["tokens"]).then_inc(loaded, 16)
            act.dma_start(ident[:, :], a["identity"]).then_inc(loaded, 16)
            act.dma_start(swap[:, :], a["pair_swap"]).then_inc(loaded, 16)
            act.dma_start(halves[:, :], a["half_ones"]).then_inc(loaded, 16)
            act.dma_start(chan_dft[:, :], a["channel_dft"]).then_inc(loaded, 16)
            act.dma_start(small_w[:, :], a["small_w"][0]).then_inc(loaded, 16)
            act.dma_start(rope[:, 0:NX], a["rope1"]).then_inc(loaded, 16)
            act.wait_ge(loaded, 16 * 9)
            nc.scalar.activation(scvec[:, :], cvec[:, :], ACT.Silu).then_inc(silu_ready, 1)
            act.wait_ge(const_ready, 1)
            split(0)
            split(1)
            v = 0
            for layer in (0, 1):
                s = m1[layer]
                n0 = N_IN[layer]
                t0 = layer * (IN_TILES + OUT_TILES + 64)
                cols = ALL if layer == 0 else LAT
                norm(v, ALL, lambda: [act.wait_ge(drained[i], t0 // 2) for i in (0, 1)] if t0 else None,
                     lambda k, which: M(layer, 0, k, which))
                v += 1

                def at_step(j):
                    ahead(n0 + j)
                    act.wait_ge(tile_done, n0 + j + 1)

                at_step(0)
                copy_out(t0, lambda x, y: ckv[:, 0, x:y], ALL)
                at_step(1)
                for k in range(2):
                    at_step(2 + k)
                    copy_out(t0 + 2 + k, lambda x, y: cq[:, k, x:y], cols)
                act.wait_ge(drained[0], (t0 + 2) // 2)
                act.wait_ge(norm_out, 8 * (2 * layer + 1))
                nc.scalar.activation(tmp2[:, 0, :], ckv[:, 0, :], ACT.Square).then_inc(s["ckv_in"], 1)
                for k in range(2):
                    at_step(4 + k)
                    copy_out(t0 + 4 + k, lambda x, y: zf[:, k, x:y], cols)
                act.wait_ge(s["ckv_sum"], 1)
                for seg, b in both(ALL):
                    last = inv_sqrt(rstd[:, seg[0]:seg[1]], bank(4 + b, c1=w(seg)), P)
                last.then_inc(s["lora_sums"], 1)
                act.wait_ge(s["lora_ready"], 1)
                act.wait_ge(drained[1], (t0 + 4) // 2)
                for k in range(2):
                    nc.scalar.activation(tmp2[:, k, cols[0]:cols[1]], cq[:, k, cols[0]:cols[1]],
                                         ACT.Square).then_inc(s["ckv_in"], 1)
                for k in range(2):
                    at_step(6 + k)
                    copy_out(t0 + 6 + k, lambda x, y: sgate[:, k, x:y], cols, ACT.Sigmoid)
                act.wait_ge(s["ckv_sum"], 2)
                for seg, b in both(cols):
                    last = inv_sqrt(rstd[:, seg[0]:seg[1]], bank(4 + b, c1=w(seg)), 2 * P)
                last.then_inc(s["lora_sums"], 1)
                at_step(8)
                at_step(9)
                for c in range(2):
                    act.wait_ge(s["y_mm"], c + 1)
                    for seg, b in both(cols):
                        last = nc.scalar.activation(zf[:, c, seg[0]:seg[1]],
                                                    bank(2 + c if b else 4 + c, c1=w(seg)), ACT.Copy)
                    last.then_inc(s["y_cp"], 1)
                for m in range(2):
                    act.wait_ge(s["f_mm"], m + 1)
                    for seg, b in both(cols):
                        last = nc.scalar.activation(hi3[:, m, seg[0]:seg[1]],
                                                    bank(m if b else 6 + m, c1=w(seg)), ACT.Copy)
                    last.then_inc(s["f_hi"], 1)

                sa = att[layer]
                plan = plans[layer]
                per = len(plan[0]) // HEADS
                npc = len(pieces_of(layer, 0))

                def proj_ev(h, i):
                    kind, (x, y) = pieces_of(layer, h)[i]
                    act.wait_ge(sa["proj"], npc * h + i + 1)
                    r = 96 if (kind, (x, y)) == ("q", CTX) else 64
                    dst = (qbuf if kind == "q" else kbuf)[0:r, h % 2, x:y]
                    nc.scalar.activation(dst, bank(7, 0, r, 0, y - x), ACT.Copy)\
                      .then_inc(sa["proj_act"], 1)

                for i in range(npc):
                    proj_ev(0, i)

                def act_hook(i):
                    h, j = divmod(i, per)
                    if h + 1 < HEADS and j < npc:
                        proj_ev(h + 1, j)

                attention(sa, plan, MLA_SCALE, dict(
                    pt=pt1, act=act_hook,
                    hi=lambda un: hi3[un["rows"][0]:un["rows"][1], 2 + un["h"] // 2,
                                      un["q0"]:un["q0"] + 256]))

                act.wait_ge(s["post"], 1)
                for c in range(2):
                    for seg, b in both(cols):
                        o = 0 if seg == CTX else NC_ + PAD
                        last = nc.scalar.activation(tmp2[:, c, seg[0]:seg[1]],
                                                    conv[:, c, o:o + w(seg)], ACT.Square)
                last.then_inc(s["post"], 1)
                act.wait_ge(s["post"], 3)
                for seg, b in both(cols):
                    last = inv_sqrt(rstd[:, seg[0]:seg[1]], bank(4 + b, c1=w(seg)), 2 * P)
                last.then_inc(s["post"], 1)
                act.wait_ge(s["post"], 5)
                for c in range(2):
                    nc.scalar.activation(qbuf[:, c, cols[0]:cols[1]], tmp2[:, c, cols[0]:cols[1]],
                                         ACT.Silu, bias=V("lnb", 2 * layer + c)).then_inc(s["post"], 1)
                for m in range(2):
                    act.wait_ge(s["post"], 8 + 3 * m)
                    for seg, b in both(cols):
                        last = nc.scalar.activation(hi3[:, 6 + m, seg[0]:seg[1]],
                                                    bank(2 * m + b, c1=w(seg)), ACT.Copy)
                    last.then_inc(s["post"], 1)
                    act.wait_ge(s["post"], 10 + 3 * m)
                for j in range(OUT_TILES):
                    ahead(n0 + IN_TILES + j)
                n1, t1 = n0 + IN_TILES + OUT_TILES, t0 + IN_TILES + OUT_TILES
                norm(v, cols, lambda: [act.wait_ge(drained[i], t1 // 2) for i in (0, 1)],
                     lambda k, which: M(layer, 3, k, which))
                v += 1
                e0 = 32 * layer
                c0, c1 = cols
                with act.Fori(0, QUARTERS) as i:
                    for j in range(MLP_STEPS):
                        ahead(n1 + j, i * MLP_STEPS)
                        if j < 8:
                            t = t1 + j
                            act.wait_ge(tile_done, i * MLP_STEPS + (n1 + j + 1))
                            if j >= 2:
                                act.wait_ge(hid_ready, i * 8 + (e0 + j - 1))
                            for (s0, s1), b in both(cols):
                                last = nc.scalar.activation(tmp2[:, j % 2, s0:s1],
                                                            bank(2 * (t % 2) + b, c1=s1 - s0), ACT.Relu)
                            last.then_inc(drained[t % 2], 1)
                            act.wait_ge(squared, i * 8 + (e0 + j + 1))
                            nc.scalar.activation(hid_hi3[:, j, c0:c1], tmp2[:, j % 2, c0:c1], ACT.Copy)\
                              .then_inc(hid_hi, 1)
            t2 = 2 * (IN_TILES + OUT_TILES + 64)
            norm(v, LAT, lambda: [act.wait_ge(drained[i], t2 // 2) for i in (0, 1)], None)
            v += 1
            act.dma_start(res3[:, :, 0:NC_], a["context2"]).then_inc(late["context2"], 16)
            act.wait_ge(late["context2"], 16)

            n0 = N_BLOCK2
            norm(v, ALL, lambda: act.wait_ge(norm_out, 8 * 5), lambda k, which: M(2, 0, k, which))
            v += 1
            for j in range(QK_TILES):
                ahead(n0 + j)
                act.wait_ge(tile_done, n0 + j + 1)
                name, idx = QK_ORDER[j]
                if name == "q":
                    nc.scalar.activation(q2[:, idx, :], bank(2 * ((t2 + j) % 2) + 1), ACT.Copy)\
                      .then_inc(drained[(t2 + j) % 2], 1)
                else:
                    copy_out(t2 + j, lambda x, y: k2[:, idx, x:y], ALL)
                if 1 <= j <= N_NORMED:
                    act.wait_ge(s2["sum"], j)
                    if j >= 2:
                        act.wait_ge(s2["normed"], j - 1)
                    for sg, b in both(LAT if QK_ORDER[j - 1][0] == "q" else ALL):
                        last = inv_sqrt(rstd[:, sg[0]:sg[1]], bank(4 + b, c1=w(sg)), HD)
                    last.then_inc(s2["sub_r"], 1)
                if j < N_NORMED:
                    seg = LAT if name == "q" else ALL
                    act.wait_ge(drained[(t2 + j) % 2], (t2 + j) // 2 + 1)
                    src = q2[:, idx, :] if name == "q" else k2[:, idx, :]
                    nc.scalar.activation(tmp2[:, 0, seg[0]:seg[1]], src, ACT.Square)\
                      .then_inc(s2["sq"], 1)
            for c in range(V_TILES):
                j = QK_TILES + c
                ahead(n0 + j)
                act.wait_ge(tile_done, n0 + j + 1)
                t = t2 + j
                nc.scalar.activation(v2[:, :, c * P:(c + 1) * P].rearrange("p (b k) c -> p b k c", b=2),
                                     psum[:, 2 * (t % 2):2 * (t % 2) + 2, 0:384]
                                     .rearrange("p b (k c) -> p b k c", k=3),
                                     ACT.Copy).then_inc(drained[t % 2], 1)
            act.wait_ge(s2["lam"], 2)
            nc.scalar.activation(coef[:, 0:2], bank(7, c1=2), ACT.Exp).then_inc(s2["lam"], 1)

            def gqa_hi(un):
                if un["kind"] == "diff":
                    return diff_out[:, un["h"], un["q0"]:un["q0"] + 256]
                return mix_hi[un["rows"][0]:un["rows"][1], 4 + un["h"] // 2, un["q0"]:un["q0"] + 256]

            attention(att[2], plans[2], GQA_SCALE, dict(pt=pt2, act=lambda i: None, hi=gqa_hi))
            for h in range(4):
                if h >= 2:
                    act.wait_ge(s2["sub_sum"], h - 1)
                if h == 0:
                    act.wait_ge(s2["sub_sq"], 1)
                act.wait_ge(att[2]["pv_hi"], 8)
                nc.scalar.activation(tmp2[:, h % 2, 0:NX], diff_out[:, h, :], ACT.Square)\
                  .then_inc(s2["sub_sq"], 1)
            act.wait_ge(s2["sub_sum"], 4)
            for h in range(4):
                if h >= 1:
                    act.wait_ge(s2["mix_t"], h)
                inv_sqrt(rstd[:, 0:NX], bank(h), P).then_inc(s2["sub_r"], 1)
                act.wait_ge(s2["mix_t"], h + 1)
                nc.scalar.activation(mix_hi[:, h, :], tmp2[:, h % 2, 0:NX], ACT.Copy)\
                  .then_inc(s2["mix_hi"], 1)
            for j in range(OUT_TILES):
                ahead(n0 + QK_TILES + V_TILES + j)
            t3 = t2 + QK_TILES + V_TILES + OUT_TILES

            def ffn(layer, tb):
                nf = N_FFN[layer]
                pair0 = 0
                for part, kk in enumerate(FFN_PARTS):
                    nb = nf + sum(3 * x for x in FFN_PARTS[:part])
                    tb_part = tb + sum(2 * x + 8 for x in FFN_PARTS[:part])
                    e0 = layer * FFN_T + pair0
                    with act.Fori(0, kk // 2) as i:
                        for j in range(4):
                            ahead(nb + j, i * 4)
                            q, is_up = j // 2, j % 2
                            dst = (ups if is_up else gates)[:, q, :]
                            t = tb_part + j
                            col = layer * 44 * 3 + 44 + 2 * pair0 + j
                            act.wait_ge(tile_done, i * 4 + (nb + j + 1))
                            act.wait_ge(loaded, 16 * 9)
                            nc.scalar.activation(dst, bank(2 * (t % 2) + 1), ACT.Identity,
                                                 bias=vec[:, bass.ds(i * 4 + (VEC["fcb"] + layer * 44 + 2 * pair0 + j), 1)],
                                                 scale=vec[:, bass.ds(i * 4 + (VEC["fcw"] + col), 1)])\
                              .then_inc(s2["g_ready"], 1)
                            if is_up:
                                act.wait_ge(drained[(t - 1) % 2], i * 2 + ((t - 1) // 2 + 1))
                                nc.scalar.activation(gates[:, q, :], gates[:, q, :], ACT.Silu)\
                                  .then_inc(s2["f_hi"], 1)
                                act.wait_ge(s2["prod"], i * 2 + (e0 + q + 1))
                                act.wait_ge(loaded, 16 * 9)
                                nc.scalar.activation(
                                    hid_hi_f[:, bass.ds(i * 2 * NX + q * NX, NX)],
                                    prods[:, q, :], ACT.Copy).then_inc(hid_hi, 1)
                    for j in range(kk):
                        ahead(nb + 2 * kk + j)
                    pair0 += kk

            norm(v, LAT, lambda: [act.wait_ge(drained[i], t3 // 2) for i in (0, 1)],
                 lambda k, which: M(2, 3, k, which))
            v += 1
            ffn(0, t3)
            t4 = t3 + 2 * FFN_T + 16
            norm(v, LAT, lambda: [act.wait_ge(drained[i], t4 // 2) for i in (0, 1)],
                 lambda k, which: M(3, 0, k, which))
            v += 1
            for j in range(SGU_U + SGU_V):
                ahead(N_SGU + j)
                act.wait_ge(tile_done, N_SGU + j + 1)
                t = t4 + j
                if j < SGU_U:
                    dst, src = su[:, j, :], bank(2 * (t % 2) + 1)
                else:
                    c = j - SGU_U
                    dst = sv[:, :, c * P:(c + 1) * P]
                    src = bank(2 * (t % 2) + 1).rearrange("p (k c) -> p k c", k=4)
                nc.scalar.activation(dst, src, ACT.Gelu).then_inc(drained[t % 2], 1)
            t5 = t4 + SGU_U + SGU_V
            for i in (0, 1):
                act.wait_ge(drained[i], t5 // 2)
            for k in range(4):
                chain.mark(nc.scalar.activation(h_f[:, 5120:6144], sv[:, k, :], ACT.Square,
                                                accum_out=tiny[:, 16 + k:17 + k]))
                chain.wait()
            inv_sqrt(tiny[:, 20:24], tiny[:, 16:20], D).then_inc(s2["sv"], 1)
            for c in range(8):
                act.wait_ge(s2["mix_t"], 4 + c + 1)
                nc.scalar.activation(mix_hi[:, c, :], tmp2[:, c % 2, 0:NX], ACT.Copy)\
                  .then_inc(s2["mix_hi"], 1)
            for j in range(OUT_TILES):
                ahead(N_SGU + SGU_U + SGU_V + j)
            t6 = t5 + OUT_TILES
            norm(v, LAT, lambda: [act.wait_ge(drained[i], t6 // 2) for i in (0, 1)],
                 lambda k, which: M(3, 3, k, which))
            v += 1
            ffn(1, t6)
            t7 = t6 + 2 * FFN_T + 16
            norm(v, LAT, lambda: [act.wait_ge(drained[i], t7 // 2) for i in (0, 1)], None)

        @block.tensor
        def _(pe):
            def tile(n, j, t, cols, rhs_hi, rhs_lo, per_k=None, first=True):
                pe.wait_ge(lo_ready, n + 1)
                if first:
                    slot_free(t)
                for k in range(8):
                    if per_k:
                        per_k(k)
                    for wt, x in ((whi3, rhs_hi), (whi3, rhs_lo), (wlo3, rhs_hi)):
                        for (s0, s1), b in both(cols):
                            mm = pe.matmul(bank(2 * (t % 2) + b, c1=s1 - s0), wt[:, j % 2, k, :],
                                           x(k, s0, s1), start=(k == 0 and wt is whi3 and x is rhs_hi),
                                           stop=(k == 7 and wt is wlo3))
                mm.then_inc(tile_done, 1)

            def slot_free(t):
                if t >= 2:
                    pe.wait_ge(drained[t % 2], t // 2)

            def norm(v, cols):
                for k in range(KD):
                    pe.wait_ge(sq_ready, 8 * v + k + 1)
                    for (s0, s1), b in both(cols):
                        mm = pe.matmul(bank(4 + b, c1=s1 - s0), ones[:, :], tmp2[:, k % 2, s0:s1],
                                       start=(k == 0), stop=(k == KD - 1))
                    mm.then_inc(sum_ready, 1)

            def in_hi(k, x, y):
                return hi3[:, k, x:y]

            def in_lo(k, x, y):
                return lo3[:, k, x:y]

            def mod_group(g, first=False):
                if not first:
                    pe.wait_ge(mod_drained, g)
                for j in range(4):
                    pe.wait_ge(m_landed[j], g * 16 + 16)
                    for k in range(KD):
                        mm = pe.matmul(bank(6, c0=2 * j, c1=2 * j + 2), mod_w3[:, j, k, :], cond(k),
                                       start=(k == 0), stop=(k == KD - 1))
                    mm.then_inc(mod_done, 1)

            tower = [0]

            def cond(k):
                return scvec[:, tower[0] * 2 * KD + 2 * k:tower[0] * 2 * KD + 2 * k + 2]

            def attention(s, plan, hooks):
                steps, units = plan

                def scores(i):
                    st = steps[i]
                    if i >= 2:
                        pe.wait_ge(s["exped"], i - 1)
                    hooks["ready"](i)
                    for b in range(0, st["nk"], 384):
                        e = min(st["nk"], b + 384)
                        mm = pe.matmul(bank(2 * (i % 2) + b // 384, c1=e - b), st["q"], st["k"][:, b:e],
                                       start=True, stop=True)
                    mm.then_inc(s["scores"], 1)

                def turn(i):
                    st = steps[i]
                    pe.wait_ge(s["p_ready"], i + 1)
                    if st["t"]:
                        pe.wait_ge(s["evA"], st["t"])
                    if st["b"]:
                        pe.wait_ge(s["evB"], st["b"])
                    p = p_slot(st["p"])
                    n = st["nk"] // P
                    for k in range(n):
                        mm = pe.transpose(bank(4 + k // 3, c0=(k % 3) * P, c1=(k % 3 + 1) * P),
                                          p[:, k * P:(k + 1) * P], ident[:, :])
                        if k == min(n, 3) - 1:
                            mm.then_inc(s["tA"], 1)
                    if n > 3:
                        mm.then_inc(s["tB"], 1)

                def pv(u):
                    un = units[u]
                    r0, r1 = un["rows"]
                    pe.wait_ge(s["evA"], un["t_end"])
                    if un["b_end"]:
                        pe.wait_ge(s["evB"], un["b_end"])
                    if u:
                        pe.wait_ge(s["pv_hi"], u)
                        if un["lo_before"]:
                            pe.wait_ge(s["pv_lo"], un["lo_before"])
                    n = un["nk"] // P
                    for k in range(n):
                        mm = pe.matmul(bank(6, r0, r1, 0, 256), hooks["v"](un, k),
                                       hooks["pt"][u % 2][:, k, :], start=(k == 0), stop=(k == n - 1))
                    mm.then_inc(s["pv"], 1)

                scores(0)
                for i, st in enumerate(steps):
                    if i + 1 < len(steps):
                        scores(i + 1)
                    hooks["pe"](i)
                    if st["t"] is not None:
                        turn(i)
                        if st["half"] == 0 and st["unit"] >= 1:
                            pv(st["unit"] - 1)
                pv(len(units) - 1)

            pe.wait_ge(silu_ready, 1)
            mod_group(0, first=True)
            with pe.Fori(1, CH // 4) as g:
                mod_group(g)
            pe.wait_ge(const_ready, 2)
            groups = CH // 4
            v = 0
            for layer in (0, 1):
                s = m1[layer]
                n0 = N_IN[layer]
                t0 = layer * (IN_TILES + OUT_TILES + 64)
                cols = ALL if layer == 0 else LAT
                norm(v, ALL)
                out_at = 8 * 2 * layer
                v += 1
                for j in range(IN_TILES):
                    tile(n0 + j, (n0 + j) % 4, t0 + j, ALL if j < 2 else cols, in_hi, in_lo,
                         per_k=(lambda k: pe.wait_ge(norm_out, out_at + k + 1)) if j == 0 else None)
                    if j == 4:
                        pe.wait_ge(s["ckv_in"], 1)
                        for seg, b in both(ALL):
                            mm = pe.matmul(bank(4 + b, c1=w(seg)), ones[:, :], tmp2[:, 0, seg[0]:seg[1]],
                                           start=True, stop=True)
                        mm.then_inc(s["ckv_sum"], 1)
                    if j == 6:
                        pe.wait_ge(s["ckv_in"], 3)
                        for k in range(2):
                            for seg, b in both(cols):
                                mm = pe.matmul(bank(4 + b, c1=w(seg)), ones[:, :],
                                               tmp2[:, k, seg[0]:seg[1]], start=(k == 0), stop=(k == 1))
                        mm.then_inc(s["ckv_sum"], 1)
                pe.wait_ge(s["lora_ready"], 1)
                if layer:
                    pe.wait_ge(late["small_w"], 16)
                for k in range(6):
                    if k >= 2:
                        pe.wait_ge(s["v_cp"], k - 1)
                    pe.matmul(bank(6 + k % 2), ckv[:, 0, k * P:(k + 1) * P], uv, start=True, stop=True)\
                      .then_inc(s["v_mm"], 1)
                toks = range(0 if layer == 0 else 2, 6)
                pe.wait_ge(drained[0], (t0 + 10) // 2)
                pe.wait_ge(drained[1], (t0 + 10) // 2)
                for i, k in enumerate(toks):
                    if i >= 2:
                        pe.wait_ge(s["ab_cp"], i - 1)
                    for c in range(2):
                        mm = pe.matmul(bank(i % 2, c0=256 * c, c1=256 * c + 256),
                                       zf[:, c, k * P:(k + 1) * P], chan_dft[:, :], start=True, stop=True)
                    mm.then_inc(s["ab_mm"], 1)
                pe.wait_ge(s["lora_ready"], 3)
                pe.wait_ge(s["ab_cp"], len(toks))
                pe.wait_ge(late["dft"], 32 * (layer + 1))
                for c in range(2):
                    for seg, b in both(cols):
                        first, table = (0, dft_c) if seg == CTX else (2, dft_x)
                        nk = w(seg) // P
                        for k in range(nk):
                            for part in range(2):
                                mm = pe.matmul(bank(2 + c if b else 4 + c, c1=w(seg)),
                                               ab[:, first + k, 256 * c + 128 * part:
                                                  256 * c + 128 * part + 128],
                                               table[:, part, k, :], start=(k == 0 and part == 0),
                                               stop=(k == nk - 1 and part == 1))
                    mm.then_inc(s["y_mm"], 1)
                pe.wait_ge(s["y_cp"], 2)
                pe.wait_ge(s["v_cp"], 6)
                for m in range(2):
                    for seg, b in both(cols):
                        for c in range(2):
                            mm = pe.matmul(bank(m if b else 6 + m, c1=w(seg)), wf[:, m, c, :],
                                           zf[:, c, seg[0]:seg[1]], start=(c == 0), stop=(c == 1))
                    mm.then_inc(s["f_mm"], 1)
                pe.wait_ge(s["f_lo"], 2)
                sa = att[layer]
                plan = plans[layer]
                per = len(plan[0]) // HEADS
                pcs = pieces_of(layer, 0)
                npc = len(pcs)
                pe.wait_ge(s["lora_ready"], 3)

                def project(h, i):
                    kind, (x, y) = pcs[i]
                    p = npc * h + i
                    if p:
                        pe.wait_ge(sa["proj_act"], p)
                        roped = h + (i > 0)
                        if roped:
                            pe.wait_ge(sa["proj_dve"], roped)
                    if kind == "q":
                        for k in range(2):
                            mm = pe.matmul(bank(7, c1=y - x), uq[:, h, k, :], cq[:, k, x:y],
                                           start=(k == 0), stop=(k == 1))
                    else:
                        mm = pe.matmul(bank(7, 0, 64, 0, y - x), uk[:, h, :], ckv[:, 0, x:y],
                                       start=True, stop=True)
                    mm.then_inc(sa["proj"], 1)

                for i in range(npc):
                    project(0, i)

                def pe_hook(i):
                    h, j = divmod(i, per)
                    if h + 1 < HEADS and j < npc:
                        project(h + 1, j)

                def head_ready(i):
                    h, j = divmod(i, per)
                    if j == 0:
                        pe.wait_ge(sa["proj_act"], npc * (h + 1))
                        pe.wait_ge(sa["proj_dve"], h + 1)

                attention(sa, plan, dict(pe=pe_hook, ready=head_ready, pt=pt1,
                                         v=lambda un, k: v1[:, k, 64 * un["h"]:64 * un["h"] + 64]))
                pe.wait_ge(s["u_ready"], 2)
                for c in range(2):
                    for seg, b in both(cols):
                        o = 0 if seg == CTX else NC_ + PAD
                        mm = pe.matmul(bank(4 + b, c1=w(seg)), ones[:, :], conv[:, c, o:o + w(seg)],
                                       start=(c == 0), stop=(c == 1))
                mm.then_inc(s["u_ready"], 1)
                pe.wait_ge(s["post"], 2)
                for c in range(2):
                    for seg, b in both(cols):
                        mm = pe.matmul(bank(4 + b, c1=w(seg)), ones[:, :], tmp2[:, c, seg[0]:seg[1]],
                                       start=(c == 0), stop=(c == 1))
                mm.then_inc(s["post"], 1)
                pe.wait_ge(s["post"], 7)
                for m in range(2):
                    if m:
                        pe.wait_ge(s["post"], 10)
                    for seg, b in both(cols):
                        for c in range(2):
                            mm = pe.matmul(bank(2 * m + b, c1=w(seg)), wp[:, m, c, :],
                                           qbuf[:, c, seg[0]:seg[1]], start=(c == 0), stop=(c == 1))
                    mm.then_inc(s["post"], 1)
                pe.wait_ge(s["post"], 13)
                for j in range(OUT_TILES):
                    n = n0 + IN_TILES + j
                    tile(n, n % 4, t0 + IN_TILES + j, cols, in_hi, in_lo)
                n1, t1 = n0 + IN_TILES + OUT_TILES, t0 + IN_TILES + OUT_TILES
                norm(v, cols)
                v += 1
                after = MOD_AFTER[layer]
                e0 = 32 * layer
                with pe.Fori(0, QUARTERS) as i:
                    seen = 0
                    for j in range(MLP_STEPS):
                        n, t = n1 + j, t1 + j
                        pe.wait_ge(lo_ready, i * MLP_STEPS + (n + 1))
                        pe.wait_ge(drained[t % 2], i * 8 + t // 2)
                        hi_, lo_ = (hi3, lo3) if j < 8 else (hid_hi3, hid_lo3)
                        for k in range(8):
                            if j == 0:
                                pe.wait_ge(norm_out, 8 * (2 * layer + 1) + k + 1)
                            if j == 8:
                                pe.wait_ge(hid_ready, i * 8 + (e0 + k + 1))
                            for q, (wt, x) in enumerate(((whi3, hi_), (whi3, lo_), (wlo3, hi_))):
                                for (s0, s1), b in both(cols):
                                    mm = pe.matmul(bank(2 * (t % 2) + b, c1=s1 - s0), wt[:, n % 2, k, :],
                                                   x[:, k, s0:s1], start=(k == 0 and q == 0),
                                                   stop=(k == 7 and q == 2))
                        mm.then_inc(tile_done, 1)
                        if j in after:
                            tower[0] = layer
                            mod_group(i * len(after) + (groups + seen))
                            seen += 1
                groups += QUARTERS * len(after)

            norm(v, LAT)
            v += 1
            norm(v, ALL)
            v += 1
            n0 = N_BLOCK2
            t2 = 2 * (IN_TILES + OUT_TILES + 64)

            def block_sum(j):
                name, idx = QK_ORDER[j]
                pe.wait_ge(s2["sq"], j + 1)
                for seg, b in both(LAT if name == "q" else ALL):
                    mm = pe.matmul(bank(4 + b, c1=w(seg)), halves[:, :], tmp2[:, 0, seg[0]:seg[1]],
                                   start=True, stop=True)
                mm.then_inc(s2["sum"], 1)

            def swap_pairs(j):
                name, idx = QK_ORDER[j]
                if j < N_NORMED:
                    pe.wait_ge(s2["normed"], j + 1)
                else:
                    t = t2 + j
                    pe.wait_ge(drained[t % 2], t // 2 + 1)
                if j >= 2:
                    pe.wait_ge(s2["roped"], j - 1)
                src = q2[:, idx, :] if name == "q" else k2[:, idx, NC_:T]
                pe.matmul(bank(6 + j % 2), swap[:, :], src, start=True, stop=True)\
                  .then_inc(s2["perm"], 1)

            for j in range(QK_TILES):
                name, idx = QK_ORDER[j]
                tile(n0 + j, (n0 + j) % 4, t2 + j, LAT if name == "q" else ALL, in_hi, in_lo,
                     per_k=(lambda k: pe.wait_ge(norm_out, 8 * 5 + k + 1)) if j == 0 else None)
                if 1 <= j <= N_NORMED:
                    block_sum(j - 1)
                if j >= 2:
                    swap_pairs(j - 2)
            for c in range(V_TILES):
                n, t = n0 + QK_TILES + c, t2 + QK_TILES + c
                if c < 2:
                    swap_pairs(QK_TILES - 2 + c)
                value_tile = [(k, (2 * (t % 2) + k // 3, (k % 3) * P)) for k in range(6)]
                pe.wait_ge(lo_ready, n + 1)
                slot_free(t)
                for tok, (b, c0) in value_tile:
                    for k in range(8):
                        for q, (x, wt) in enumerate(((hi3, whi3), (lo3, whi3), (hi3, wlo3))):
                            mm = pe.matmul(bank(b, c0=c0, c1=c0 + P), x[:, k, tok * P:(tok + 1) * P],
                                           wt[:, n % 2, k, :], start=(k == 0 and q == 0),
                                           stop=(k == 7 and q == 2))
                mm.then_inc(tile_done, 1)
            pe.wait_ge(s2["lam"], 1)
            pe.wait_ge(s2["roped"], QK_TILES)
            pe.matmul(bank(7, c1=2), ones[0:HD, :], coef[0:HD, 2:4], start=True, stop=True)\
              .then_inc(s2["lam"], 1)
            for i in (0, 1):
                pe.wait_ge(drained[i], (t2 + QK_TILES + V_TILES) // 2)
            pe.wait_ge(s2["lam"], 4)

            def gqa_v(un, k):
                if un["kind"] == "diff":
                    return v2[:, k, un["h"] * P:(un["h"] + 1) * P]
                g = un["h"] % 2
                return v2[:, k, 512 + 64 * g:512 + 64 * g + 64]

            attention(att[2], plans[2], dict(pe=lambda i: None, ready=lambda i: None, pt=pt2, v=gqa_v))
            for h in range(4):
                pe.wait_ge(s2["sub_sq"], h + 2)
                pe.matmul(bank(h), ones[:, :], tmp2[:, h % 2, 0:NX], start=True, stop=True)\
                  .then_inc(s2["sub_sum"], 1)
            t3 = t2 + QK_TILES + V_TILES + OUT_TILES

            def mixed(lo_count):
                def per_k(k):
                    pe.wait_ge(s2["mix_lo"], lo_count(k))
                return per_k

            for j in range(OUT_TILES):
                n = n0 + QK_TILES + V_TILES + j
                if j == 0:
                    pe.wait_ge(s2["mix_lo"], 4)
                    pe.wait_ge(att[2]["pv_lo"], 16)
                tile(n, n % 4, t3 - OUT_TILES + j, LAT, lambda k, x, y: mix_hi[:, k, :],
                     lambda k, x, y: mix_lo[:, k, :])
            norm(v, LAT)
            v += 1

            def ffn(layer, tb, norm_at):
                nf = N_FFN[layer]
                pair0 = 0
                for part, kk in enumerate(FFN_PARTS):
                    nb = nf + sum(3 * x for x in FFN_PARTS[:part])
                    tb_part = tb + sum(2 * x + 8 for x in FFN_PARTS[:part])
                    with pe.Fori(0, kk // 2) as i:
                        for j in range(4):
                            n, t = nb + j, tb_part + j
                            pe.wait_ge(lo_ready, i * 4 + (n + 1))
                            pe.wait_ge(drained[t % 2], i * 2 + t // 2)
                            for k in range(8):
                                if j == 0 and part == 0:
                                    pe.wait_ge(norm_out, norm_at + k + 1)
                                for q, (wt, x) in enumerate(((whi3, hi3), (whi3, lo3), (wlo3, hi3))):
                                    mm = pe.matmul(bank(2 * (t % 2) + 1), wt[:, n % 2, k, :],
                                                   x[:, k, NC_:T], start=(k == 0 and q == 0),
                                                   stop=(k == 7 and q == 2))
                            mm.then_inc(tile_done, 1)
                    n = nb + 2 * kk
                    block_no = 0
                    for m in range(8):
                        t = tb_part + 2 * kk + m
                        slot_free(t)
                        for k in range(kk):
                            if block_no % 8 == 0:
                                pe.wait_ge(lo_ready, n + 1)
                            if m == 0:
                                pe.wait_ge(hid_ready, 64 + layer * FFN_T + pair0 + k + 1)
                            for q, (wt, x) in enumerate(((whi3, fh_hi), (whi3, fh_lo), (wlo3, fh_hi))):
                                mm = pe.matmul(bank(2 * (t % 2) + 1), wt[:, n % 2, block_no % 8, :],
                                               x[:, k, :], start=(k == 0 and q == 0),
                                               stop=(k == kk - 1 and q == 2))
                            block_no += 1
                            if block_no % 8 == 0:
                                mm.then_inc(tile_done, 1)
                                n += 1
                            elif k == kk - 1:
                                pass
                        if block_no % 8:
                            mm.then_inc(p_chain, 1)
                    pair0 += kk

            ffn(0, t3, 8 * 6)
            t4 = t3 + 2 * FFN_T + 16
            norm(v, LAT)
            v += 1
            for j in range(SGU_U):
                tile(N_SGU + j, (N_SGU + j) % 4, t4 + j, LAT, in_hi, in_lo,
                     per_k=(lambda k: pe.wait_ge(norm_out, 8 * 7 + k + 1)) if j == 0 else None)
            for c in range(SGU_V):
                n, t = N_SGU + SGU_U + c, t4 + SGU_U + c
                pe.wait_ge(lo_ready, n + 1)
                slot_free(t)
                for tok in range(4):
                    for k in range(8):
                        for q, (x, wt) in enumerate(((hi3, whi3), (lo3, whi3), (hi3, wlo3))):
                            mm = pe.matmul(bank(2 * (t % 2) + 1, c0=tok * P, c1=(tok + 1) * P),
                                           x[:, k, NC_ + tok * P:NC_ + (tok + 1) * P],
                                           wt[:, n % 2, k, :], start=(k == 0 and q == 0),
                                           stop=(k == 7 and q == 2))
                mm.then_inc(tile_done, 1)
            pe.wait_ge(s2["sv"], 2)
            pe.wait_ge(late["sgu"], 32)
            for c in range(8):
                if c >= 2:
                    pe.wait_ge(s2["mix_t"], 4 + c - 1)
                for n in range(4):
                    mm = pe.matmul(bank(4 + c % 2, c0=n * P, c1=(n + 1) * P),
                                   sv[:, n, c * P:(c + 1) * P], ws[:, c // 2, :], start=True, stop=True)
                mm.then_inc(s2["mixed"], 1)
            t5 = t4 + SGU_U + SGU_V
            for j in range(OUT_TILES):
                n = N_SGU + SGU_U + SGU_V + j
                tile(n, n % 4, t5 + j, LAT, lambda k, x, y: mix_hi[:, k, :],
                     lambda k, x, y: mix_lo[:, k, :],
                     per_k=(lambda k: pe.wait_ge(s2["mix_lo"], 4 + k + 1)) if j == 0 else None)
            norm(v, LAT)
            v += 1
            ffn(1, t5 + OUT_TILES, 8 * 8)
            norm(v, LAT)

        @block.vector
        def _(dve):
            chain = Chain(dve, d_chain)
            out_v = [0]

            def norm(v, cols, gains, shifts):
                segs = both(cols)
                o = out_v[0]
                dve.wait_ge(rstd_ready, v + 1)

                def low(k):
                    dve.wait_ge(norm_hi, 8 * o + k + 1)
                    for (s0, s1), b in segs:
                        last = nc.vector.scalar_tensor_tensor(
                            lo3[:, k, s0:s1], tmp2[:, k % 2, s0:s1], shifts(k, 1 - b),
                            hi3[:, k, s0:s1].bitcast(F32), ALU.add, ALU.subtract)
                    last.then_inc(norm_out, 1)

                for k in range(KD):
                    if k >= 2:
                        dve.wait_ge(norm_out, 8 * v + k - 1)
                    for (s0, s1), b in segs:
                        last = nc.vector.scalar_tensor_tensor(
                            tmp2[:, k % 2, s0:s1], res3[:, k, s0:s1], gains(k, 1 - b),
                            rstd[:, s0:s1], ALU.mult, ALU.mult)
                    last.then_inc(scaled, 1)
                    if k:
                        low(k - 1)
                low(KD - 1)
                out_v[0] += 1

            def final_norm(v, name):
                dve.wait_ge(rstd_ready, v + 1)
                for k in range(KD):
                    nc.vector.scalar_tensor_tensor(
                        res3[:, k, NC_:T], res3[:, k, NC_:T], V(name, k), rstd[:, NC_:T],
                        ALU.mult, ALU.mult).then_inc(norm_out, 1)

            def gain_table(dst, name, i, block_, chunk, w_):
                for which in range(w_):
                    last = nc.vector.scalar_tensor_tensor(
                        coef[:, dst + 8 * which:dst + 8 * which + 8],
                        mod3[:, block_ * CH + chunk * KD:block_ * CH + chunk * KD + KD, which],
                        1.0, V(name, i, KD), ALU.add, ALU.mult)
                    chain.mark(last)
                chain.wait()

            def add_residual(t, m, cols, block_, chunk, shift=None, wait=True):
                for (s0, s1), b in both(cols):
                    last = nc.vector.scalar_tensor_tensor(
                        res3[:, m, s0:s1], bank(2 * (t % 2) + b, c1=s1 - s0),
                        M(block_, chunk, m, 1 - b), res3[:, m, s0:s1], ALU.mult, ALU.add)
                last.then_inc(drained[t % 2], 1)

            def mod_out(g):
                dve.wait_ge(mod_done, g * 4 + 4)
                for which in range(2):
                    last = nc.vector.tensor_tensor(
                        mod[:, bass.ds(g * 8, 8)].rearrange("p (m v) -> p m v", v=2)[:, :, which],
                        bank(6, c1=8).rearrange("p (m v) -> p m v", v=2)[:, :, which],
                        vec[:, bass.ds(g * 4 + VEC["bias"], 4)], ALU.add)
                last.then_inc(mod_drained, 1)

            def attention(s, plan, scale, hooks):
                steps, units = plan

                def maximum(i):
                    st = steps[i]
                    dve.wait_ge(s["scores"], i + 1)
                    c = tiny[:, 12 + i % 4:13 + i % 4]
                    if st["nk"] > 384:
                        last = nc.vector.tensor_reduce(c, psum[:, 2 * (i % 2):2 * (i % 2) + 2, 0:384],
                                                       AX.XY, ALU.max)
                    else:
                        last = nc.vector.tensor_reduce(c, bank(2 * (i % 2), c1=st["nk"]), AX.X, ALU.max)
                    chain.mark(last)
                    chain.wait()
                    nc.vector.tensor_scalar(tiny[:, 4 + i % 4:5 + i % 4], c, -scale, None, ALU.mult)\
                      .then_inc(s["maxed"], 1)

                def weigh(i):
                    st = steps[i]
                    dve.wait_ge(s["exped"], i + 1)
                    r = tiny[:, 24 + i % 4:25 + i % 4]
                    chain.mark(nc.vector.reciprocal(r, tiny[:, 8 + i % 4:9 + i % 4]))
                    chain.wait()
                    p = p_slot(st["p"])[:, 0:st["nk"]]
                    if st["post"] == "second":
                        chain.mark(nc.vector.tensor_tensor(r, r, coef[:, 4:5], ALU.mult))
                        chain.wait()
                        nc.vector.scalar_tensor_tensor(p, p, r, p_slot(steps[i - 1]["p"])[:, 0:st["nk"]],
                                                       ALU.mult, ALU.add).then_inc(s["p_ready"], 1)
                    else:
                        nc.vector.tensor_scalar(p, p, r, None, ALU.mult).then_inc(s["p_ready"], 1)
                        if st["post"] == "first":
                            dve.wait_ge(s["p_ready"], i + 1)

                def ev_b(i):
                    st = steps[i]
                    if st["b"] is None:
                        return
                    dve.wait_ge(s["tB"], st["b"] + 1)
                    if st["unit"] >= 2:
                        dve.wait_ge(s["pv"], st["unit"] - 1)
                    pt = hooks["pt"][st["unit"] % 2]
                    nc.vector.tensor_copy(pt[:, 3:6, st["half"] * P:(st["half"] + 1) * P],
                                          bank(5, c1=384).rearrange("p (k q) -> p k q", k=3))\
                      .then_inc(s["evB"], 1)

                def pv_lo(u):
                    un = units[u]
                    if not un["lo"]:
                        return
                    r0, r1 = un["rows"]
                    dve.wait_ge(s["pv_hi"], u + 1)
                    nc.vector.tensor_tensor(hooks["lo"](un), bank(6, r0, r1, 0, 256),
                                            hooks["hi"](un).bitcast(F32), ALU.subtract)\
                      .then_inc(s["pv_lo"], 1)

                maximum(0)
                for i, st in enumerate(steps):
                    if i + 1 < len(steps):
                        maximum(i + 1)
                    weigh(i)
                    hooks["dve"](i)
                    ev_b(i)
                    if st["t"] is not None and st["half"] == 0 and st["unit"] >= 1:
                        pv_lo(st["unit"] - 1)
                pv_lo(len(units) - 1)

            nc.vector.memset(tiny[:, 0:1], EPS).then_inc(const_ready, 1)
            nc.vector.memset(ones[:, :], 1.0).then_inc(const_ready, 1)
            dve.wait_ge(loaded, 16 * 9)
            with dve.Fori(0, CH // 4) as g:
                mod_out(g)
            groups = CH // 4
            dve.wait_ge(mod_drained, groups)
            v = 0
            for layer in (0, 1):
                s = m1[layer]
                n0 = N_IN[layer]
                t0 = layer * (IN_TILES + OUT_TILES + 64)
                cols = ALL if layer == 0 else LAT
                dve.wait_ge(mod_drained, groups)
                if layer:
                    for i in (0, 1):
                        dve.wait_ge(drained[i], t0 // 2)
                gain_table(8, "norm1", 8 * layer, layer, 1, 2)
                norm(v, ALL, lambda k, which: coef[:, 8 + 8 * which + k:9 + 8 * which + k],
                     lambda k, which: M(layer, 0, k, which))
                v += 1
                t = t0 + 1
                dve.wait_ge(tile_done, n0 + 2)
                b = 2 * (t % 2)
                kx = kbuf[64:96, 0, NC_:T]
                chain.mark(nc.vector.tensor_tensor(kx, bank(b + 1, 0, 32), rope3[0:32, 0, :], ALU.mult))
                chain.mark(nc.vector.tensor_tensor(rtmp[64:96, :], bank(b + 1, 32, 64), rope3[32:64, 0, :],
                                                   ALU.mult))
                nc.vector.tensor_copy(kbuf[64:96, 0, 0:NC_], bank(b, 0, 32, 0, NC_))\
                  .then_inc(drained[t % 2], 1)
                chain.wait()
                dve.wait_ge(drained[t % 2], t // 2 + 1)
                chain.mark(nc.vector.tensor_tensor(kx, kx, rtmp[64:96, :], ALU.add))
                chain.wait()
                chain.mark(nc.vector.tensor_copy(kbuf[64:96, 1, :], kbuf[64:96, 0, :]))
                chain.mark(nc.vector.memset(u_pad, 0.0))
                dve.wait_ge(s["lora_sums"], 1)
                nc.vector.scalar_tensor_tensor(ckv[:, 0, :], ckv[:, 0, :], V("kvn", layer), rstd[:, :],
                                               ALU.mult, ALU.mult).then_inc(s["lora_ready"], 1)
                dve.wait_ge(s["lora_sums"], 2)
                c0, c1 = cols
                for k in range(2):
                    nc.vector.scalar_tensor_tensor(cq[:, k, c0:c1], cq[:, k, c0:c1],
                                                   V("qn", 2 * layer + k), rstd[:, c0:c1],
                                                   ALU.mult, ALU.mult).then_inc(s["lora_ready"], 1)
                chain.wait()
                for k in range(2):
                    t = t0 + 8 + k
                    dve.wait_ge(tile_done, n0 + 9 + k)
                    dve.wait_ge(drained[t % 2], t // 2)
                    for seg, b in both(cols):
                        o = PAD if seg == CTX else PAD + NC_ + PAD
                        last = nc.vector.tensor_tensor(u_pad[:, k, o:o + w(seg)],
                                                       bank(2 * (t % 2) + b, c1=w(seg)),
                                                       sgate[:, k, seg[0]:seg[1]], ALU.mult)
                    last.then_inc(drained[t % 2], 1)
                for k in range(6):
                    dve.wait_ge(s["v_mm"], k + 1)
                    nc.vector.tensor_copy(v1[:, k, :], bank(6 + k % 2)).then_inc(s["v_cp"], 1)
                toks = range(0 if layer == 0 else 2, 6)
                for i, k in enumerate(toks):
                    dve.wait_ge(s["ab_mm"], i + 1)
                    nc.vector.tensor_copy(ab[:, k, :], bank(i % 2)).then_inc(s["ab_cp"], 1)
                for m in range(2):
                    dve.wait_ge(s["f_hi"], m + 1)
                    for seg, b in both(cols):
                        last = nc.vector.tensor_tensor(lo3[:, m, seg[0]:seg[1]],
                                                       bank(m if b else 6 + m, c1=w(seg)),
                                                       hi3[:, m, seg[0]:seg[1]].bitcast(F32),
                                                       ALU.subtract)
                    last.then_inc(s["f_lo"], 1)

                sa = att[layer]
                plan = plans[layer]
                per = len(plan[0]) // HEADS
                npc = len(pieces_of(layer, 0))

                def rope_q(h):
                    dve.wait_ge(sa["proj_act"], npc * h + 1)
                    q = qbuf[64:96, h % 2, NC_:T]
                    chain.mark(nc.vector.tensor_tensor(q, bank(7, 64, 96), rope3[64:96, 0, :], ALU.mult))
                    chain.mark(nc.vector.tensor_tensor(rtmp[64:96, :], bank(7, 96, 128),
                                                       rope3[96:128, 0, :], ALU.mult))
                    chain.wait()
                    nc.vector.tensor_tensor(q, q, rtmp[64:96, :], ALU.add).then_inc(sa["proj_dve"], 1)

                rope_q(0)
                x0 = 0 if layer == 0 else NC_ + PAD
                last_tap = [None, None]

                def tap(c, k):
                    if last_tap[c] is not None:
                        chain.wait(last_tap[c])
                    dst = conv[:, c, x0:CW]
                    src = u_pad[:, c, x0 + k:CW + k]
                    wt = V("dw", (2 * layer + c) * TAPS + k)
                    if k == 0:
                        ins = nc.vector.tensor_scalar(dst, src, wt, V("bdw", 2 * layer + c),
                                                      ALU.mult, ALU.add)
                    else:
                        ins = nc.vector.scalar_tensor_tensor(dst, src, wt, dst, ALU.mult, ALU.add)
                    if k == TAPS - 1:
                        ins.then_inc(s["u_ready"], 1)
                    else:
                        last_tap[c] = chain.mark(ins)

                for i in (0, 1):
                    dve.wait_ge(drained[i], (t0 + 10) // 2)

                def dve_hook(i):
                    h, j = divmod(i, per)
                    if h + 1 < HEADS and j == 0:
                        rope_q(h + 1)
                    if i < TAPS:
                        for c in range(2):
                            tap(c, i)

                attention(sa, plan, MLA_SCALE, dict(
                    pt=pt1, dve=dve_hook,
                    hi=lambda un: hi3[un["rows"][0]:un["rows"][1], 2 + un["h"] // 2,
                                      un["q0"]:un["q0"] + 256],
                    lo=lambda un: lo3[un["rows"][0]:un["rows"][1], 2 + un["h"] // 2,
                                      un["q0"]:un["q0"] + 256]))
                dve.wait_ge(s["u_ready"], 3)
                for c in range(2):
                    for seg, b in both(cols):
                        o = 0 if seg == CTX else NC_ + PAD
                        last = nc.vector.scalar_tensor_tensor(
                            conv[:, c, o:o + w(seg)], bank(4 + b, c1=w(seg)), -1.0 / (2 * P),
                            conv[:, c, o:o + w(seg)], ALU.mult, ALU.add)
                last.then_inc(s["post"], 1)
                dve.wait_ge(s["post"], 4)
                for c in range(2):
                    for seg, b in both(cols):
                        o = 0 if seg == CTX else NC_ + PAD
                        last = nc.vector.scalar_tensor_tensor(
                            tmp2[:, c, seg[0]:seg[1]], conv[:, c, o:o + w(seg)],
                            V("lng", 2 * layer + c), rstd[:, seg[0]:seg[1]], ALU.mult, ALU.mult)
                last.then_inc(s["post"], 1)
                for m in range(2):
                    dve.wait_ge(s["post"], 9 + 3 * m)
                    for seg, b in both(cols):
                        last = nc.vector.tensor_tensor(lo3[:, 6 + m, seg[0]:seg[1]],
                                                       bank(2 * m + b, c1=w(seg)),
                                                       hi3[:, 6 + m, seg[0]:seg[1]].bitcast(F32),
                                                       ALU.subtract)
                    last.then_inc(s["post"], 1)
                for j in range(OUT_TILES):
                    dve.wait_ge(tile_done, n0 + IN_TILES + j + 1)
                    add_residual(t0 + IN_TILES + j, j, cols, layer, 2)
                n1, t1 = n0 + IN_TILES + OUT_TILES, t0 + IN_TILES + OUT_TILES
                for i in (0, 1):
                    dve.wait_ge(drained[i], t1 // 2)
                gain_table(8, "norm2", 8 * layer, layer, 4, 2)
                norm(v, cols, lambda k, which: coef[:, 8 + 8 * which + k:9 + 8 * which + k],
                     lambda k, which: M(layer, 3, k, which))
                v += 1
                after = MOD_AFTER[layer]
                e0 = 32 * layer
                with dve.Fori(0, QUARTERS) as i:
                    seen = 0

                    def low(j):
                        dve.wait_ge(hid_hi, i * 8 + (e0 + j + 1))
                        nc.vector.tensor_tensor(hid_lo3[:, j, c0:c1], tmp2[:, j % 2, c0:c1],
                                                hid_hi3[:, j, c0:c1].bitcast(F32), ALU.subtract)\
                          .then_inc(hid_ready, 1)

                    for j in range(MLP_STEPS):
                        t = t1 + j
                        if j == 8:
                            low(7)
                        dve.wait_ge(tile_done, i * MLP_STEPS + (n1 + j + 1))
                        if j < 8:
                            dve.wait_ge(drained[t % 2], i * 8 + (t // 2 + 1))
                            x = tmp2[:, j % 2, c0:c1]
                            nc.vector.tensor_tensor(x, x, x, ALU.mult).then_inc(squared, 1)
                            if j:
                                low(j - 1)
                        else:
                            dve.wait_ge(drained[t % 2], i * 8 + (t // 2 - 3))
                            add_residual(t, j - 8, cols, layer, 5)
                        if j in after:
                            mod_out(i * len(after) + (groups + seen))
                            seen += 1
                groups += QUARTERS * len(after)

            t2 = 2 * (IN_TILES + OUT_TILES + 64)
            for i in (0, 1):
                dve.wait_ge(drained[i], t2 // 2)
            final_norm(v, "fin1")
            v += 1
            dve.wait_ge(norm_out, 8 * 5)
            dve.wait_ge(mod_drained, groups)
            dve.wait_ge(late["context2"], 16)
            gain_table(8, "mixn", 0, 2, 1, 2)
            n0 = N_BLOCK2
            norm(v, ALL, lambda k, which: coef[:, 8 + 8 * which + k:9 + 8 * which + k],
                 lambda k, which: M(2, 0, k, which))
            v += 1
            nc.vector.tensor_tensor(coef[0:HD, 2:4], vec[0:HD, VEC["lam"]:VEC["lam"] + 2],
                                    vec[0:HD, VEC["lam"] + 2:VEC["lam"] + 4], ALU.mult)\
              .then_inc(s2["lam"], 1)

            def scale_heads(j):
                name, idx = QK_ORDER[j]
                dve.wait_ge(s2["sub_r"], j + 1)
                if name == "q":
                    x, r, g = q2[:, idx, :], rstd[:, NC_:T], V("gq")
                else:
                    x, r, g = k2[:, idx, :], rstd[:, :], V("gk")
                nc.vector.scalar_tensor_tensor(x, x, g, r, ALU.mult, ALU.mult).then_inc(s2["normed"], 1)

            def rope_tile(j):
                name, idx = QK_ORDER[j]
                dve.wait_ge(s2["perm"], j + 1)
                if j:
                    dve.wait_ge(s2["roped"], j)
                x = q2[:, idx, :] if name == "q" else k2[:, idx, NC_:T]
                chain.mark(nc.vector.tensor_tensor(rtmp[:, :], bank(6 + j % 2), rope3[:, 1, :], ALU.mult))
                chain.mark(nc.vector.tensor_tensor(x, x, rope3[:, 0, :], ALU.mult))
                chain.wait()
                nc.vector.tensor_tensor(x, x, rtmp[:, :], ALU.add).then_inc(s2["roped"], 1)

            dve.wait_ge(late["rope2"], 16)
            for j in range(QK_TILES):
                if 1 <= j <= N_NORMED:
                    scale_heads(j - 1)
                if j >= 2:
                    rope_tile(j - 2)
            rope_tile(QK_TILES - 2)
            rope_tile(QK_TILES - 1)
            dve.wait_ge(s2["lam"], 3)
            chain.mark(nc.vector.tensor_tensor(coef[:, 5:6], coef[:, 1:2], coef[:, 0:1], ALU.subtract))
            chain.wait()
            nc.vector.tensor_scalar(coef[:, 4:5], coef[:, 5:6], -LAM_INIT, None, ALU.add)\
              .then_inc(s2["lam"], 1)
            dve.wait_ge(s2["lam"], 4)
            chain.mark(nc.vector.tensor_scalar(coef[:, 6:7], V("subln"), 1.0 - LAM_INIT, None, ALU.mult))
            chain.wait()
            attention(att[2], plans[2], GQA_SCALE, dict(
                pt=pt2, dve=lambda i: None,
                hi=lambda un: mix_hi[un["rows"][0]:un["rows"][1], 4 + un["h"] // 2,
                                     un["q0"]:un["q0"] + 256],
                lo=lambda un: mix_lo[un["rows"][0]:un["rows"][1], 4 + un["h"] // 2,
                                     un["q0"]:un["q0"] + 256]))
            nc.vector.tensor_copy(tiny[:, 28:29], tiny[:, 12:13]).then_inc(s2["sub_sq"], 1)
            for h in range(4):
                dve.wait_ge(s2["sub_r"], N_NORMED + h + 1)
                if h >= 2:
                    dve.wait_ge(s2["mix_lo"], h - 1)
                nc.vector.scalar_tensor_tensor(tmp2[:, h % 2, 0:NX], diff_out[:, h, :], coef[:, 6:7],
                                               rstd[:, 0:NX], ALU.mult, ALU.mult)\
                  .then_inc(s2["mix_t"], 1)
                dve.wait_ge(s2["mix_hi"], h + 1)
                nc.vector.tensor_tensor(mix_lo[:, h, :], tmp2[:, h % 2, 0:NX],
                                        mix_hi[:, h, :].bitcast(F32), ALU.subtract)\
                  .then_inc(s2["mix_lo"], 1)
            t3 = t2 + QK_TILES + V_TILES + OUT_TILES
            for j in range(OUT_TILES):
                dve.wait_ge(tile_done, n0 + QK_TILES + V_TILES + j + 1)
                add_residual(t3 - OUT_TILES + j, j, LAT, 2, 2)
            for i in (0, 1):
                dve.wait_ge(drained[i], t3 // 2)
            gain_table(8, "ffnn", 0, 2, 4, 1)

            def norm_b(v, block_, chunk):
                norm(v, LAT, lambda k, which: coef[:, 8 + 8 * which + k:9 + 8 * which + k],
                     lambda k, which: M(block_, chunk, k, which))

            norm_b(v, 2, 3)
            v += 1

            def ffn(layer, tb):
                nf = N_FFN[layer]
                pair0 = 0
                for part, kk in enumerate(FFN_PARTS):
                    nb = nf + sum(3 * x for x in FFN_PARTS[:part])
                    tb_part = tb + sum(2 * x + 8 for x in FFN_PARTS[:part])
                    e0 = layer * FFN_T + pair0
                    with dve.Fori(0, kk // 2) as i:
                        for j in range(4):
                            q, is_up = j // 2, j % 2
                            x = (ups if is_up else gates)[:, q, :]
                            t = tb_part + j
                            col = VEC["fcw"] + layer * 132 + 2 * pair0 + j
                            dve.wait_ge(s2["g_ready"], i * 4 + (2 * e0 + j + 1))
                            chain_l = nc.vector.scalar_tensor_tensor(
                                x[:, 1:NX], bank(2 * (t % 2) + 1, c1=NX - 1),
                                vec[:, bass.ds(i * 4 + col, 1)], x[:, 1:NX], ALU.mult, ALU.add)
                            chain_l.then_inc(s2["f_lo"], 1)
                            dve.wait_ge(s2["f_lo"], i * 4 + (2 * e0 + j + 1))
                            nc.vector.scalar_tensor_tensor(
                                x[:, 0:NX - 1], bank(2 * (t % 2) + 1, c0=1, c1=NX),
                                vec[:, bass.ds(i * 4 + (col + 88), 1)], x[:, 0:NX - 1],
                                ALU.mult, ALU.add).then_inc(drained[t % 2], 1)
                            if is_up:
                                dve.wait_ge(s2["f_hi"], i * 2 + (e0 + q + 1))
                                dve.wait_ge(drained[t % 2], i * 2 + (t // 2 + 1))
                                nc.vector.tensor_tensor(prods[:, q, :], gates[:, q, :], ups[:, q, :],
                                                        ALU.mult).then_inc(s2["prod"], 1)
                                dve.wait_ge(hid_hi, i * 2 + (64 + e0 + q + 1))
                                nc.vector.tensor_tensor(
                                    hid_lo_f[:, bass.ds(i * 2 * NX + q * NX, NX)], prods[:, q, :],
                                    hid_hi_f[:, bass.ds(i * 2 * NX + q * NX, NX)].bitcast(F32),
                                    ALU.subtract).then_inc(hid_ready, 1)
                    for m in range(8):
                        t = tb_part + 2 * kk + m
                        end = (m + 1) * kk
                        if end % 8:
                            dve.wait_ge(p_chain, marks[layer, part, m])
                        else:
                            dve.wait_ge(tile_done, nb + 2 * kk + end // 8)
                        if part:
                            dve.wait_ge(drained[t % 2], t // 2 - 3)
                        add_residual(t, m, LAT, 2 + layer, 5)
                    pair0 += kk

            ffn(0, t3)
            t4 = t3 + 2 * FFN_T + 16
            for i in (0, 1):
                dve.wait_ge(drained[i], t4 // 2)
            gain_table(8, "mixn", 8, 3, 1, 1)
            norm_b(v, 3, 0)
            v += 1
            t5 = t4 + SGU_U + SGU_V
            dve.wait_ge(s2["sv"], 1)
            for k in range(4):
                last = nc.vector.tensor_scalar(sv[:, k, :], sv[:, k, :], tiny[:, 20 + k:21 + k], None,
                                               ALU.mult)
                if k < 3:
                    chain.mark(last)
            last.then_inc(s2["sv"], 1)
            dve.wait_ge(late["sgu"], 32)

            def mix_low(c):
                dve.wait_ge(s2["mix_hi"], 4 + c + 1)
                nc.vector.tensor_tensor(mix_lo[:, c, :], tmp2[:, c % 2, 0:NX],
                                        mix_hi[:, c, :].bitcast(F32), ALU.subtract)\
                  .then_inc(s2["mix_lo"], 1)

            for c in range(8):
                dve.wait_ge(s2["mixed"], c + 1)
                if c >= 2:
                    dve.wait_ge(s2["mix_lo"], 4 + c - 1)
                for n in range(4):
                    chain.mark(nc.vector.scalar_tensor_tensor(
                        tmp2[:, c % 2, n * P:(n + 1) * P], bank(4 + c % 2, c0=n * P, c1=(n + 1) * P),
                        V("vn", c), bs[:, c // 2, :], ALU.mult, ALU.add))
                chain.wait()
                nc.vector.tensor_tensor(tmp2[:, c % 2, 0:NX], tmp2[:, c % 2, 0:NX], su[:, c, :],
                                        ALU.mult).then_inc(s2["mix_t"], 1)
                if c:
                    mix_low(c - 1)
            mix_low(7)
            for j in range(OUT_TILES):
                dve.wait_ge(tile_done, N_SGU + SGU_U + SGU_V + j + 1)
                add_residual(t5 + j, j, LAT, 3, 2)
            t6 = t5 + OUT_TILES
            for i in (0, 1):
                dve.wait_ge(drained[i], t6 // 2)
            gain_table(8, "ffnn", 8, 3, 4, 1)
            norm_b(v, 3, 3)
            v += 1
            ffn(1, t6)
            t7 = t6 + 2 * FFN_T + 16
            for i in (0, 1):
                dve.wait_ge(drained[i], t7 // 2)
            final_norm(v, "fin2")


def blocks(wt, ks, cols):
    return wt.reshape(-1, P, wt.shape[1])[np.asarray(ks)][:, :, np.asarray(cols)].transpose(1, 0, 2)


def columns(v):
    return v.reshape(-1, P).T


def stream_tiles(i):
    k8 = range(8)
    m = lambda c: range(c * P, (c + 1) * P)
    for l in (0, 1):
        wi = i["w_in"][l]
        f, q, kv, r = 256, 512, 640, 672
        kr = list(range(kv, r))
        turned = kr[16:] + kr[:16]
        for c in ([range(q, kv), kr + turned + kr + turned, range(f, f + P), range(f + P, q), m(0), m(1)]
                  + [range(r + o, r + o + P) for o in (256, 384, 0, 128)]):
            yield blocks(wi, k8, list(c))
        for c in range(8):
            yield blocks(i["w_o"][l], k8, list(m(c)))
        for part in range(QUARTERS):
            for c in range(8):
                yield blocks(i["w_mlp1"][l], k8, list(m(8 * part + c)))
            for c in range(8):
                yield blocks(i["w_mlp2"][l], range(8 * part, 8 * part + 8), list(m(c)))
    wi = i["attn_w_in_2"][0]
    pairs = lambda o: [o + 2 * x for x in range(32)] + [o + 2 * x + 1 for x in range(32)]
    q1, q2, k1, k2, va, qb, kb, vb = 0, 256, 512, 768, 1024, 1536, 2048, 2176
    for c in range(4):
        yield blocks(wi, k8, pairs(qb + 64 * c) + pairs(qb + 64 * (c + 4)))
    yield blocks(wi, k8, pairs(kb) + pairs(kb + 64))
    for o in (q1, q2, k1, k2):
        for c in range(2):
            yield blocks(wi, k8, pairs(o + 128 * c) + pairs(o + 128 * c + 64))
    for c in range(4):
        yield blocks(wi, k8, list(range(va + P * c, va + P * (c + 1))))
    yield blocks(wi, k8, list(range(vb, vb + P)))
    wo = i["attn_w_out_2"][0]
    rows = list(range(512)) + [512 + 64 * h + x for c in range(4) for h in (c, c + 4) for x in range(64)]
    for c in range(8):
        yield blocks(wo[rows], k8, list(m(c)))

    def ffn(l):
        up, down = i["ffn_w_up_2"][l], i["ffn_w_down_2"][l]
        first = 0
        for kk in FFN_PARTS:
            for c in range(first, first + kk):
                yield blocks(up, k8, list(m(c)))
                yield blocks(up, k8, list(m(FFN_T + c)))
            flat = np.concatenate([blocks(down, range(first, first + kk), list(m(c))) for c in range(8)], 1)
            for b in range(0, 8 * kk, 8):
                yield flat[:, b:b + 8]
            first += kk

    yield from ffn(0)
    for c in range(16):
        yield blocks(i["sgu_w_in_2"][0], k8, list(m(c)))
    for c in range(8):
        yield blocks(i["sgu_w_out_2"][0], k8, list(m(c)))
    yield from ffn(1)


def mod_tiles(i):
    for wt in (i["w_mod"][0], i["w_mod"][1], i["ada_w_2"][0], i["ada_w_2"][1]):
        for c in range(CH):
            yield blocks(wt, range(8), list(range(c * P, (c + 1) * P)))


def vector_table(i):
    pair = [2 * x for x in range(32)] + [2 * x + 1 for x in range(32)]
    turn = lambda v: v[pair]
    parts = [columns(i["b_mod"][0]), columns(i["b_mod"][1]), columns(i["ada_b_2"][0]),
             columns(i["ada_b_2"][1])]
    for name in ("norm1_g", "norm2_g"):
        parts += [columns(i[name][l]) for l in (0, 1)]
    parts.append(columns(i["final_norm_g"]))
    for name in ("q_norm_g", "kv_norm_g"):
        parts += [columns(i[name][l]) for l in (0, 1)]
    parts += [i["w_dw"][l].T[c * P:(c + 1) * P] for l in (0, 1) for c in (0, 1)]
    for name in ("b_dw", "conv_ln_g", "conv_ln_b"):
        parts += [columns(i[name][l]) for l in (0, 1)]
    for name in ("mix_norm_2", "ffn_norm_2"):
        parts += [columns(i[name][l]) for l in (0, 1)]
    parts.append(columns(i["final_norm_2"]))
    parts.append(columns(i["diff_subln_2"][0]))
    for name in ("gqa_q_norm_2", "gqa_k_norm_2"):
        half = turn(i[name][0])
        parts.append(np.concatenate([half, half])[:, None])
    parts.append(columns(i["sgu_v_norm_2"][0]))
    lam = np.stack([i[f"diff_{n}_2"][0] for n in ("lq1", "lq2", "lk1", "lk2")], 1)
    parts.append(np.concatenate([lam, lam]))
    order = [c + x for c in range(FFN_T) for x in (0, FFN_T)]
    for l in (0, 1):
        for tap in range(3):
            parts.append(columns(i["ffn_conv_w_2"][l, tap])[:, order])
    for l in (0, 1):
        parts.append(columns(i["ffn_conv_b_2"][l])[:, order])
    return np.concatenate(parts, 1)


def small_weights(i, l):
    wq = i["w_uq"][l]
    parts = []
    for h in range(HEADS):
        o = 96 * h
        r = list(range(o + 64, o + 96))
        parts.append(blocks(wq, range(2), list(range(o, o + 64)) + r + r[16:] + r[:16]).reshape(P, -1))
    wkv = i["w_ukv"][l].reshape(P, HEADS, 2, 64)
    parts += [wkv[:, :, 0].reshape(P, -1), wkv[:, :, 1].reshape(P, -1)]
    for name in ("w_fourier", "w_pw2"):
        for m in range(2):
            parts.append(blocks(i[name][l], range(2), list(range(m * P, (m + 1) * P))).reshape(P, -1))
    return np.concatenate(parts, 1)


def tokens(x):
    return x.T.reshape(KD, P, -1).transpose(1, 0, 2)


def shape_tables():
    t = np.arange(NX)
    row, col = t // GRID_W, t % GRID_W

    def angles(n):
        inv = 10000.0 ** (-np.arange(n, dtype=np.float32) / n)
        return np.concatenate([row[:, None] * inv, col[:, None] * inv], 1).T

    a1 = angles(8)
    c1, s1 = np.cos(a1), np.sin(a1)
    cos1, sin1 = np.concatenate([c1, c1]), np.concatenate([-s1, s1])
    a2 = angles(16)
    c2, s2 = np.cos(a2), np.sin(a2)
    cos2 = np.concatenate([c2] * 4)
    sin2 = np.concatenate([-s2, s2] * 2)
    half = np.eye(P).reshape(2, 2, 32, P)[:, ::-1].reshape(P, P)

    def dft(n):
        a = 2 * np.pi * np.outer(np.arange(n), np.arange(n)) / n
        return np.cos(a) / np.sqrt(n), np.sin(a) / np.sqrt(n)

    def positions(n):
        c, s = dft(n)
        return np.stack([c, -s]).reshape(2, n // P, P, n).transpose(2, 0, 1, 3).reshape(P, -1)

    c64, s64 = dft(64)
    chan = np.concatenate([np.kron(np.eye(2), c64), np.kron(np.eye(2), s64)], 1)
    out = dict(identity=np.eye(P), pair_swap=half, half_ones=np.kron(np.eye(2), np.ones((64, 64))),
               channel_dft=chan, rope1=np.concatenate([cos1, sin1] * 2),
               rope2=np.concatenate([cos2, sin2], 1), dft_x=positions(NX), dft_c=positions(NC_))
    return {k: np.ascontiguousarray(v, dtype=np.float32) for k, v in out.items()}


def layouts(i):
    conditions = np.concatenate(
        [np.stack([columns(i[c].reshape(-1)), columns(i[cc])], 2).reshape(P, -1)
         for c, cc in (("c", "c_ctx"), ("c_2", "c_ctx_2"))], 1)
    out = dict(
        stream=np.stack([b.reshape(P, 1024) for b in stream_tiles(i)]),
        mods=np.stack([b.reshape(P, 1024) for b in mod_tiles(i)]),
        vectors=vector_table(i), conditions=conditions,
        tokens=tokens(np.concatenate([i["ctx"][0], i["x"][0]])),
        context2=tokens(i["ctx_2"][0]),
        small_w=np.stack([small_weights(i, l) for l in (0, 1)]),
        w_s=i["sgu_w_s_2"][0].transpose(2, 0, 1).reshape(P, -1),
        b_s=np.tile(i["sgu_b_s_2"][0].reshape(1, -1), (P, 1)))
    out.update(shape_tables())
    return {k: np.ascontiguousarray(v) for k, v in out.items()}


def kernel(**inputs):
    import concourse.bacc as bacc
    from concourse.bass_utils import run_bass_kernel_spmd

    arrays = {f"{k}_dram": v for k, v in layouts({k: np.asarray(v) for k, v in inputs.items()}).items()}
    nc = bacc.Bacc("TRN2", target_bir_lowering=False, num_devices=1)
    aps = {k[:-5]: nc.dram_tensor(k, v.shape, mybir.dt.from_np(v.dtype), kind="ExternalInput").ap()
           for k, v in arrays.items()}
    aps["out"] = nc.dram_tensor("out_dram", (P, KD, NX), F32, kind="ExternalOutput").ap()
    two_towers(nc, aps)
    r = run_bass_kernel_spmd(nc, [arrays], core_ids=[0])
    got = r.results[0]["out_dram"]
    return np.ascontiguousarray(got.transpose(2, 1, 0).reshape(1, NX, D))
```

```python
from contextlib import ExitStack

import numpy as np

import concourse.bass as bass
from concourse import mybir

F32 = mybir.dt.float32
F32R = mybir.dt.float32r
ACT = mybir.ActivationFunctionType
ALU = mybir.AluOpType
AX = mybir.AxisListType

P = 128
D = 1024
KD = D // P
NC_, NX = 256, 512
T = NC_ + NX
CTX, LAT, ALL = (0, NC_), (NC_, T), (0, T)
EPS = 1e-6
GRID_W = 64
CH = 6 * KD
TAPS = 31
PAD = TAPS // 2
UW = PAD + NC_ + PAD + NX + PAD
CW = NC_ + PAD + NX
HEADS, NOPE, ROPE = 8, 64, 32
MLA_SCALE = (NOPE + ROPE) ** -0.5
HD = 64
GQA_SCALE = HD ** -0.5
QUARTERS, QK = 4, 8
FFN_T = 22
FFN_PARTS = (12, 10)
LAM_INIT = 0.2
SUB_AT, SUB_STEP = 33, 7

VEC_SIZES = [("bias", 4 * CH), ("norm1", 16), ("norm2", 16), ("fin1", 8), ("qn", 4), ("kvn", 2),
             ("dw", 4 * TAPS), ("bdw", 4), ("lng", 4), ("lnb", 4), ("mixn", 16), ("ffnn", 16),
             ("fin2", 8), ("subln", 1), ("gq", 1), ("gk", 1), ("vn", 8), ("lam", 4),
             ("fcw", 2 * 3 * 44), ("fcb", 2 * 44)]
VEC, _at = {}, 0
for _name, _size in VEC_SIZES:
    VEC[_name] = _at
    _at += _size
NVEC = _at

IN_TILES, OUT_TILES = 10, 8
MLP_STEPS = 16
QK_TILES, V_TILES = 13, 5
SGU_U, SGU_V = 8, 8
V_OUTS, SGU_V_OUTS = 3, 4
N_IN = [0, IN_TILES + OUT_TILES + QUARTERS * MLP_STEPS]
N_BLOCK2 = 2 * N_IN[1]
N_FFN = [N_BLOCK2 + QK_TILES + V_TILES + OUT_TILES]
FFN_TILES = sum(2 * k + k for k in FFN_PARTS)
N_SGU = N_FFN[0] + FFN_TILES
N_FFN.append(N_SGU + SGU_U + SGU_V + OUT_TILES)
N_TILES = N_FFN[1] + FFN_TILES
MOD_TILES = 4 * CH
RAW = 4
QK_ORDER = ([("q", 4 + i) for i in range(4)] + [("k", 4)] + [("q", i) for i in range(4)]
            + [("k", i) for i in range(4)])
N_NORMED = 5
NORMS = 10
MOD_GROUP = 2 * KD
MOD_RING = 2
MOD_IN, MOD_OUT = [16, 0], [16, 8]
MOD_QUARTER = [CH // QUARTERS, 16]
MOD_QK = MOD_ATT = 12
PAIR_LAG = 3


def two_towers(nc, a):
    ctx = ExitStack()
    with ctx:
        base = nc.sbuf_base
        base += -base % 32
        cursor = [base]

        def at(name, cols, dt=F32, offset=None):
            if offset is None:
                offset = cursor[0]
                cursor[0] += -(-4 * cols // 32) * 32
            return nc.alloc_sbuf_tensor_at(name, [P, cols], dt, offset=offset), offset

        res, _ = at("residual", KD * T)
        hi_f, o_hi = at("in_hi", KD * T, F32R)
        lo_f, o_lo = at("in_lo", KD * T, F32R)
        hid_hi_f, o_c = at("hidden_hi", QK * T, F32R)
        hid_lo_f, _ = at("hidden_lo", QK * T, F32R)
        raw, _ = at("w_raw", RAW * 1024)
        whi, _ = at("w_hi", 2 * 1024, F32R)
        wlo, _ = at("w_lo", 2 * 1024, F32R)
        mod_w, _ = at("mod_w", MOD_RING * 1024)
        small_w, _ = at("small_w", 4096)
        vec, _ = at("vectors", NVEC)
        mod, _ = at("modulation", 2 * MOD_TILES)
        cvec, _ = at("conditions", 2 * D)
        dots, _ = at("modulation_dots", 2 * MOD_GROUP)
        coef, _ = at("coefficients", 64)
        ident, _ = at("identity", P)
        ones, _ = at("ones", P)
        halves, _ = at("half_ones", P)
        swap, _ = at("pair_swap", P)
        chan_dft, _ = at("channel_dft", 256)
        rstd, _ = at("rstd", T)
        tmp, _ = at("scratch", 2 * T)
        rope, _ = at("rope", 2 * NX)
        rtmp, o_rtmp = at("rope_scratch", NX)
        tiny, _ = at("tiny", 64)
        rtmp_b = at("product_scratch", 2 * NX, mybir.dt.bfloat16, o_rtmp)[0][:, :]
        cbuf, _ = at("mixer_space", 2 * QK * T, F32, o_c)
        h_f, _ = at("in_hi_space", KD * T, F32, o_hi)
        l_f, _ = at("in_lo_space", KD * T, F32, o_lo)

        res3 = res[:, :].rearrange("p (k t) -> p k t", k=KD)
        hi3 = hi_f[:, :].rearrange("p (k t) -> p k t", k=KD)
        lo3 = lo_f[:, :].rearrange("p (k t) -> p k t", k=KD)
        hid_hi3 = hid_hi_f[:, :].rearrange("p (k t) -> p k t", k=QK)
        hid_lo3 = hid_lo_f[:, :].rearrange("p (k t) -> p k t", k=QK)
        tmp2 = tmp[:, :].rearrange("p (s t) -> p s t", s=2)
        raw3 = raw[:, :].rearrange("p (s n) -> p s n", s=RAW)
        whi3 = whi[:, :].rearrange("p (s k m) -> p s k m", s=2, k=8)
        wlo3 = wlo[:, :].rearrange("p (s k m) -> p s k m", s=2, k=8)
        mod3 = mod[:, :].rearrange("p (m v) -> p m v", v=2)
        rope3 = rope[:, :].rearrange("p (s t) -> p s t", s=2)
        uq = small_w[:, 0:2048].rearrange("p (h k m) -> p h k m", h=8, k=2)
        uk = small_w[:, 2048:2560].rearrange("p (h m) -> p h m", h=8)
        uv = small_w[:, 2560:3072]
        wf = small_w[:, 3072:3584].rearrange("p (m k c) -> p m k c", m=2, k=2)
        wp = small_w[:, 3584:4096].rearrange("p (m k c) -> p m k c", m=2, k=2)

        def region(first, k, width):
            return cbuf[:, first:first + k * width].rearrange("p (k t) -> p k t", k=k)

        cq = region(0, 2, T)
        ckv = region(1536, 1, T)
        u_pad = region(2304, 2, UW)
        conv = region(3930, 2, CW)
        sgate = region(3930, 2, T)
        v1 = region(5496, 6, 512)
        qbuf = region(8568, 2, T)
        kbuf = region(10104, 2, T)
        zf = qbuf
        tap_scratch = cbuf[:, 11640:12288]
        dft_x = h_f[:, 1536:1536 + 4096].rearrange("p (s k n) -> p s k n", s=2, k=4)
        dft_c = l_f[:, 4608:4608 + 1024].rearrange("p (s k n) -> p s k n", s=2, k=2)
        ab = l_f[:, 1536:1536 + 3072].rearrange("p (k n) -> p k n", k=6)
        pt1 = [h_f[:, 6 * T:8 * T].rearrange("p (k q) -> p k q", k=6),
               l_f[:, 6 * T:8 * T].rearrange("p (k q) -> p k q", k=6)]
        q2 = region(0, 8, NX)
        k2 = region(4096, 5, T)
        v2 = region(4096 + 3840, 6, 640)
        mix_hi = hi_f[:, 0:8 * NX].rearrange("p (k t) -> p k t", k=8)
        mix_lo = lo_f[:, 0:8 * NX].rearrange("p (k t) -> p k t", k=8)
        pt2 = [h_f[:, 8 * NX:8 * NX + 1536].rearrange("p (k q) -> p k q", k=6),
               l_f[:, 8 * NX:8 * NX + 1536].rearrange("p (k q) -> p k q", k=6)]
        diff_out = small_w[:, 0:2048].rearrange("p (k t) -> p k t", k=4)
        more_p = small_w[:, 2048:2048 + 2 * T].rearrange("p (s t) -> p s t", s=2)
        su = region(0, 8, NX)
        sv = region(4096, 4, 1024)
        ws = small_w[:, 0:512].rearrange("p (g c) -> p g c", g=4)
        bs = small_w[:, 512:1024].rearrange("p (g c) -> p g c", g=4)
        fh_hi = hid_hi_f[:, :].rearrange("p (k t) -> p k t", t=NX)
        fh_lo = hid_lo_f[:, :].rearrange("p (k t) -> p k t", t=NX)
        gates = small_w[:, 1024:2048].rearrange("p (s t) -> p s t", s=2)
        ups = small_w[:, 2048:3072].rearrange("p (s t) -> p s t", s=2)
        prods = tmp[:, 0:1024].rearrange("p (s t) -> p s t", s=2)

        psum = ctx.enter_context(nc.psum_tensor("psum", [P, 8, 512], F32))

        def bank(b, r0=0, r1=P, c0=0, c1=512):
            return psum[r0:r1, b, c0:c1]

        def V(name, i=0, n=1):
            return vec[:, VEC[name] + i:VEC[name] + i + n]

        def M(block, chunk, k, which):
            return mod3[:, block * CH + chunk * KD + k, which:which + 1]

        def both(layer_segs):
            return [(CTX, 0), (LAT, 1)] if layer_segs == ALL else [(LAT, 1)]

        def w(t):
            return t[1] - t[0]

        def sum_banks(cols):
            half = T // 2
            if cols == ALL:
                return [((0, half), bank(4, c1=half)), ((half, T), bank(5, c1=half))]
            return [(LAT, bank(5))]

        def sums(cols):
            return psum[:, 4:6, 0:T // 2] if cols == ALL else bank(5)

        gained_sum, r_final = small_w[:, 1024:1536], small_w[:, 1536:2048]
        gained = small_w[:, 0:1024].rearrange("p (s t) -> p s t", s=2)
        ctx_sum = rstd[:, 0:NC_]

        def sq(v):
            return v - (v > 5)

        def inverse(cols):
            return rstd[:, :].rearrange("p (b c) -> p b c", b=2) if cols == ALL else rstd[:, NC_:T]

        def sem(name):
            return ctx.enter_context(nc.semaphore(name))

        loaded = sem("constants_loaded")
        vec_landed, res_landed = sem("vectors_landed"), sem("tokens_landed")
        late = {n: sem(f"{n}_loaded") for n in ("dft", "small_w", "rope2", "context2", "sgu")}
        w_landed = [sem(f"w_landed{i}") for i in range(RAW)]
        m_landed = [sem(f"m_landed{i}") for i in range(MOD_RING)]
        m_first = [sem(f"first_modulation_landed{i}") for i in range(4)]
        hi_ready = sem("w_hi_ready")
        lo_ready = sem("w_lo_ready")
        tile_done = sem("tile_done")
        drained = [sem("drained_even"), sem("drained_odd")]
        mod_done = sem("mod_done")
        mod_half = sem("mod_context_done")
        pooled_first, summed_first = sem("first_products"), sem("first_sums")
        cond_landed = sem("conditions_landed")
        mod_drained = sem("mod_drained")
        silu_ready = sem("silu_ready")
        const_ready = sem("const_ready")
        sq_ready = sem("norm_squares")
        sq_added = sem("norm_squares_added")
        sq_ctx, sq_ctx_added = sem("context_squares"), sem("context_squares_added")
        sq_gain, sq_gain_added = sem("gained_squares"), sem("gained_squares_added")
        final_mean = sem("gained_mean")
        sum_ready = sem("norm_sums")
        rstd_ready = sem("rstd_ready")
        scaled = sem("norm_scaled")
        norm_hi = sem("norm_hi")
        norm_out = sem("norm_out")
        squared = sem("hid_squared")
        hid_hi = sem("hid_hi")
        hid_ready = sem("hid_ready")
        a_chain, d_chain, p_chain = sem("act_chain"), sem("dve_chain"), sem("pe_chain")
        out_done = sem("out_done")
        tapped, g_chain = sem("conv_taps_of_pool"), sem("pool_chain")

        class Chain:

            def __init__(self, eng, s):
                self.eng, self.s, self.n, self.plus = eng, s, 0, 0

            def mark(self, ins):
                ins.then_inc(self.s, 1)
                self.n += 1
                return self.n

            def wait(self, n=None):
                self.eng.wait_ge(self.s, (self.n if n is None else n) + self.plus)

        def per_layer(names):
            return [{n: sem(f"{n}_{i}") for n in names} for i in (0, 1)]

        m1 = per_layer(["ckv_in", "ckv_sum", "lora_sums", "lora_ready", "v_mm", "v_cp",
                        "ab_mm", "ab_cp", "y_mm", "y_cp", "f_mm", "f_hi", "f_lo",
                        "u_ready", "ln", "p_mm", "p_hi", "p_lo"])
        att_names = ["scores", "maxed", "exped", "p_ready", "turned", "ev",
                     "pv", "pv_hi", "pv_lo", "proj", "proj_act", "proj_dve"]
        att = [{n: sem(f"att{i}_{n}") for n in att_names} for i in range(3)]
        s2 = {n: sem("b2_" + n) for n in ["sq", "sum", "normed", "perm", "roped",
                                          "sub_sq", "sub_sum", "sub_r", "mixed", "mix_t", "mix_hi",
                                          "mix_lo", "g_ready", "prod", "f_hi", "f_lo", "sv",
                                          "lam"]}

        def mod_first(m):
            return (cbuf[:, m * 1024:(m + 1) * 1024] if m < 12
                    else l_f[:, (m - 12) * 1024:(m - 11) * 1024])

        def mla_plan(layer):
            steps, units = [], []
            for h in range(HEADS):
                chunks = ([(0, NC_)] if layer == 0 else []) + [(NC_, T), (NC_ + 256, T)]
                for q0, nk in chunks:
                    u = len(units)
                    units.append(dict(nk=nk, h=h, q0=q0, rows=(64 * (h % 2), 64 * (h % 2) + 64),
                                      lo=True))
                    for j in range(2):
                        steps.append(dict(unit=u, half=j, nk=nk, h=h, post="plain",
                                          q=qbuf[0:96, h % 2, q0 + j * P:q0 + (j + 1) * P],
                                          k=kbuf[0:96, h % 2, :], p=(0, 1, 4)[len(steps) % 3]))
            return steps, units

        def gqa_plan():
            steps, units = [], []
            for h in range(4):
                for q0 in (0, 256):
                    u = len(units)
                    units.append(dict(nk=T, h=h, q0=q0, rows=(0, P), lo=False, kind="diff"))
                    r = 64 * (h % 2)
                    for j in range(2):
                        for i, post in enumerate(("first", "second")):
                            qs = q2[r:r + 64, 2 * i + h // 2, q0 + j * P:q0 + (j + 1) * P]
                            steps.append(dict(unit=u, half=j, nk=T, h=h, post=post, q=qs,
                                              k=k2[r:r + 64, 2 * i + h // 2, :], p=len(steps) % 4))
            for h in range(8):
                for q0 in (0, 256):
                    u = len(units)
                    r = 64 * (h % 2)
                    units.append(dict(nk=T, h=h, q0=q0, rows=(r, r + 64), lo=True, kind="gqa"))
                    for j in range(2):
                        steps.append(dict(unit=u, half=j, nk=T, h=h, post="plain",
                                          q=q2[r:r + 64, 4 + h // 2, q0 + j * P:q0 + (j + 1) * P],
                                          k=k2[r:r + 64, 4, :], p=len(steps) % 4))
            return steps, units

        def index(steps, units):
            t = 0
            for s in steps:
                s["t"], s["t_before"] = None, t
                if s["post"] != "first":
                    s["t"] = t
                    t += 1
            lo = 0
            for u in units:
                u["lo_before"] = lo
                lo += u["lo"]
            for n, u in enumerate(units):
                u["t_end"] = [s for s in steps if s["unit"] == n][-1]["t"] + 1

        def unit_after(st):
            return st["t"] is not None and st["half"] == 0 and st["unit"] >= 1

        plans = [mla_plan(0), mla_plan(1), gqa_plan()]
        for pl in plans:
            index(*pl)

        def pieces_of(layer, h):
            keys, ctx_q = [("k", (0, 384)), ("k", (384, T))], [("q", CTX)] if layer == 0 else []
            return keys + ctx_q + [("q", LAT)] if h == 0 else [("q", LAT)] + keys + ctx_q

        def ln_stage(layer, i):
            per = len(plans[layer][0]) // HEADS
            at0 = (HEADS - 2) * per + len(pieces_of(layer, 0))
            g, stage = divmod(i - at0, 3)
            segs = [LAT, CTX] if layer == 0 else [LAT]
            return (g, segs[g], stage) if 0 <= g < len(segs) else (None, None, None)

        def conv_of(c, seg):
            o = 0 if seg == CTX else NC_ + PAD
            return conv[:, c, o:o + w(seg)]

        def p_slot(i):
            return tmp2[:, i, :] if i < 2 else more_p[:, i - 2, :] if i < 4 else rstd[:, :]

        def ffn_marks():
            marks, count = {}, 0
            for layer in (0, 1):
                for part, kk in enumerate(FFN_PARTS):
                    for m in range(8):
                        if (m + 1) * kk % 8:
                            count += 1
                            marks[layer, part, m] = count
            return marks

        marks = ffn_marks()
        block = ctx.enter_context(nc.Block())

        @block.sync
        def _(sp):
            stream, mods = a["stream"], a["mods"]

            def w_load(n, j):
                tile = stream[n:n + 1] if isinstance(n, int) else stream[bass.ds(n, 1)]
                sp.dma_start(raw3[:, j, :], tile.rearrange("a p n -> p (a n)"))\
                  .then_inc(w_landed[j], 16)

            def w_step(n, j):
                sp.wait_ge(lo_ready, n + 1)
                w_load(n + RAW, j)

            def w_steps(n0, count):
                count = min(count, N_TILES - RAW - n0)
                if count >= 8:
                    with sp.Fori(0, count // 4) as i:
                        for j in range(4):
                            w_step(i * 4 + (n0 + j), (n0 + j) % 4)
                for n in range(n0 + (count // 4 * 4 if count >= 8 else 0), n0 + count):
                    w_step(n, n % 4)

            def m_load(m, j):
                tile = mods[m:m + 1] if isinstance(m, int) else mods[bass.ds(m, 1)]
                sp.dma_start(mod_w[:, j * 1024:(j + 1) * 1024], tile.rearrange("a p n -> p (a n)"))\
                  .then_inc(m_landed[j], 16)

            def m_step(m, shift=0):
                sp.wait_ge(mod_done, shift + (m + 1))
                m_load(shift + (m + MOD_RING), m % MOD_RING)

            def m_steps(m0, count):
                for m in range(m0, min(m0 + count, MOD_TILES - MOD_RING)):
                    m_step(m)

            sp.dma_start(cvec[:, :], a["conditions"][0]).then_inc(cond_landed, 16)
            for m in range(MOD_GROUP):
                if m % 4 == 0 and m >= 8:
                    sp.wait_ge(m_first[m // 4 - 2], 16 * 4)
                sp.dma_start(mod_first(m), mods[m]).then_inc(m_first[m // 4], 16)
            sp.wait_ge(m_first[2], 16 * 4)
            for name, dst in (("identity", ident), ("pair_swap", swap), ("half_ones", halves),
                              ("channel_dft", chan_dft)):
                sp.dma_start(dst[:, :], a[name]).then_inc(loaded, 16)
            for n in range(RAW):
                w_load(n, n)
            for m in range(MOD_RING):
                m_load(MOD_GROUP + m, m)
            sp.dma_start(rope[:, 0:NX], a["rope1"]).then_inc(loaded, 16)
            sp.dma_start(small_w[:, :], a["small_w"][0]).then_inc(loaded, 16)
            m0 = MOD_GROUP
            for layer in (0, 1):
                n0 = N_IN[layer]
                for j in range(IN_TILES):
                    w_step(n0 + j, (n0 + j) % 4)
                    if j >= 2:
                        m_steps(m0, MOD_IN[layer] // 8)
                        m0 += MOD_IN[layer] // 8
                sp.wait_ge(tile_done, n0 + IN_TILES)
                if layer:
                    sp.dma_start(res3[:, :, 0:NC_], a["context2"]).then_inc(late["context2"], 16)
                sp.dma_start(h_f[:, 1536:1536 + 4096], a["dft_x"]).then_inc(late["dft"], 16)
                sp.dma_start(l_f[:, 4608:4608 + 1024], a["dft_c"]).then_inc(late["dft"], 16)
                for j in range(OUT_TILES):
                    w_step(n0 + IN_TILES + j, (n0 + IN_TILES + j) % 4)
                    m_steps(m0, MOD_OUT[layer] // 8)
                    m0 += MOD_OUT[layer] // 8
                sp.wait_ge(tile_done, n0 + IN_TILES + 1)
                if layer == 0:
                    sp.dma_start(small_w[:, :], a["small_w"][1]).then_inc(late["small_w"], 16)
                else:
                    sp.dma_start(rope[:, :], a["rope2"]).then_inc(late["rope2"], 16)
                n1 = n0 + IN_TILES + OUT_TILES
                per = MOD_QUARTER[layer]

                def quarter(i):
                    for j in range(MLP_STEPS):
                        w_step(i * MLP_STEPS + (n1 + j), (n1 + j) % 4)
                        if j < per:
                            m_step(m0 + j, i * per)

                with sp.Fori(0, QUARTERS) as i:
                    quarter(i)
                m0 += QUARTERS * per
                if layer == 0:
                    sp.wait_ge(mod_done, m0)
                    sp.dma_start(cvec[:, :], a["conditions"][1]).then_inc(cond_landed, 16)
            for j in range(QK_TILES + V_TILES):
                w_step(N_BLOCK2 + j, (N_BLOCK2 + j) % 4)
                if j < MOD_QK:
                    m_steps(m0 + j, 1)
            m_steps(m0 + MOD_QK, MOD_ATT)
            n = N_BLOCK2 + QK_TILES + V_TILES
            w_steps(n, N_SGU - n)
            sp.wait_ge(tile_done, N_FFN[0])
            sp.dma_start(small_w[:, 0:512], a["w_s"]).then_inc(late["sgu"], 16)
            sp.dma_start(small_w[:, 512:1024], a["b_s"]).then_inc(late["sgu"], 16)
            w_steps(N_SGU, N_TILES - N_SGU)
            sp.wait_ge(norm_out, KD * NORMS)
            sp.dma_start(a["out"], res3[:, :, NC_:T]).then_inc(out_done, 16)
            sp.wait_ge(out_done, 16)

        @block.gpsimd
        def _(pool):
            def w_low(n, j, free):
                pool.wait_ge(hi_ready, n + 1)
                if free:
                    pool.wait_ge(tile_done, n - 1)
                nc.gpsimd.tensor_tensor(wlo[:, (j % 2) * 1024:(j % 2 + 1) * 1024], raw3[:, j, :],
                                        whi[:, (j % 2) * 1024:(j % 2 + 1) * 1024].bitcast(F32),
                                        ALU.subtract).then_inc(lo_ready, 1)

            def w_lows(n0, n1):
                turns = (n1 - n0) // 4
                if turns >= 2:
                    with pool.Fori(0, turns) as i:
                        for j in range(4):
                            w_low(i * 4 + (n0 + j), (n0 + j) % 4, True)
                    n0 += 4 * turns
                for n in range(n0, n1):
                    w_low(n, n % 4, n >= 2)

            pooled = Chain(pool, g_chain)

            def tap(layer, k):
                x0 = NC_ + PAD if layer else 0
                parts = [(x0, CW)] if layer else [(0, CW // 2), (CW // 2, CW)]
                for a0, a1 in parts:
                    src = u_pad[:, 1, a0 + k:a1 + k]
                    wt = V("dw", (2 * layer + 1) * TAPS + k)
                    dst = conv[:, 1, a0:a1]
                    if k == 0:
                        pooled.mark(nc.gpsimd.tensor_scalar(dst, src, wt, V("bdw", 2 * layer + 1),
                                                            ALU.mult, ALU.add))
                        continue
                    pooled.wait()
                    prod = tap_scratch[:, 0:a1 - a0]
                    pooled.mark(nc.gpsimd.tensor_scalar(prod, src, wt, None, ALU.mult))
                    pooled.wait()
                    last = nc.gpsimd.tensor_tensor(dst, dst, prod, ALU.add)
                    if k == TAPS - 1 and a1 == CW:
                        last.then_inc(tapped, 1)
                    else:
                        pooled.mark(last)

            pool.wait_ge(silu_ready, 1)
            for i in range(12):
                m = i // 3 * 4 + i % 3
                pool.wait_ge(m_first[m // 4], 16 * 4)
                if i >= 6:
                    pool.wait_ge(summed_first, i - 5)
                nc.gpsimd.tensor_tensor(h_f[:, (i % 6) * 1024:(i % 6 + 1) * 1024], mod_first(m),
                                        cvec[:, D:2 * D], ALU.mult).then_inc(pooled_first, 1)
            for n in range(2):
                w_low(n, n, False)
            n = 2
            for layer in (0, 1):
                end = N_IN[layer] + IN_TILES + 2
                w_lows(n, end)
                n = end
                for i in (0, 1):
                    pool.wait_ge(drained[i], (layer * (IN_TILES + OUT_TILES + 64) + IN_TILES) // 2)
                for k in range(TAPS):
                    tap(layer, k)
            w_lows(n, N_TILES)

        @block.scalar
        def _(act):
            chain = Chain(act, a_chain)

            def split(n, shift=0):
                j = n % 4
                act.wait_ge(w_landed[j], shift * 4 + 16 * (n // 4 + 1))
                if n >= 2:
                    act.wait_ge(tile_done, shift + (n - 1))
                nc.scalar.activation(whi[:, (j % 2) * 1024:(j % 2 + 1) * 1024], raw3[:, j, :],
                                     ACT.Copy).then_inc(hi_ready, 1)

            def ahead(n, shift=0):
                if n + 2 < N_TILES:
                    split(n + 2, shift)

            def inv_sqrt(dst, src, n, rows=P):
                chain.mark(nc.scalar.activation(dst, src, ACT.Ln, bias=tiny[0:rows, 0:1], scale=1.0 / n))
                chain.wait()
                return nc.scalar.activation(dst, dst, ACT.Exp, scale=-0.5)

            def square(v, k, cols):
                if k >= 3:
                    act.wait_ge(sq_added, 7 * sq(v) + k - 2)
                dst = rstd[:, cols[0]:cols[1]] if k == 0 else tmp2[:, k % 2, cols[0]:cols[1]]
                nc.scalar.activation(dst, res3[:, k, cols[0]:cols[1]], ACT.Square).then_inc(sq_ready, 1)

            def squares(v, cols, t, m):
                act.wait_ge(drained[t % 2], t // 2 + 1)
                square(v, m, cols)

            def square_ctx(k):
                if k >= 3:
                    act.wait_ge(sq_ctx_added, k - 2)
                nc.scalar.activation(tmp2[:, k % 2, 0:NC_] if k else ctx_sum, res3[:, k, 0:NC_],
                                     ACT.Square).then_inc(sq_ctx, 1)

            def square_gained(k):
                if k >= 3:
                    act.wait_ge(sq_gain_added, k - 2)
                nc.scalar.activation(gained[:, k % 2, :] if k else gained_sum, res3[:, k, NC_:T],
                                     ACT.Square, scale=V("fin1", k)).then_inc(sq_gain, 1)

            def norm(v, cols, shifts):
                act.wait_ge(sum_ready, v + 1)
                chain.mark(nc.scalar.activation(inverse(cols), sums(cols), ACT.Ln, bias=tiny[:, 0:1],
                                                scale=1.0 / D))
                chain.wait()
                x = rstd[:, cols[0]:cols[1]]
                nc.scalar.activation(x, x, ACT.Exp, scale=-0.5).then_inc(rstd_ready, 1)
                if shifts is not None:
                    shifted(cols, shifts)

            def shifted(cols, shifts):
                segs = both(cols)
                for k in range(KD):
                    act.wait_ge(scaled, 8 * hi_v[0] + k + 1)
                    for (s0, s1), b in segs:
                        last = nc.scalar.activation(hi3[:, k, s0:s1], tmp2[:, k % 2, s0:s1],
                                                    ACT.Identity, bias=shifts(k, 1 - b))
                    last.then_inc(norm_hi, 1)
                hi_v[0] += 1

            hi_v = [0]

            def copy_out(t, dst, cols, func=ACT.Copy):
                segs = both(cols)
                for (s0, s1), b in segs:
                    last = nc.scalar.activation(dst(s0, s1), bank(2 * (t % 2) + b, c1=s1 - s0), func)
                last.then_inc(drained[t % 2], 1)

            def attention(s, plan, scale, hooks):
                steps, units = plan

                def exp(i):
                    st = steps[i]
                    nk, sl = st["nk"], i % 2
                    act.wait_ge(s["maxed"], i + 1)
                    back = len({x["p"] for x in steps})
                    if i >= back:
                        nt = steps[i - back]["t_before"] + 1
                        act.wait_ge(s["turned"], nt)
                    if nk > 384:
                        src = psum[:, 2 * sl:2 * sl + 2, 0:384]
                        dst = p_slot(st["p"])[:, 0:nk].rearrange("p (b c) -> p b c", b=2)
                    else:
                        src, dst = bank(2 * sl, c1=nk), p_slot(st["p"])[:, 0:nk]
                    nc.scalar.activation(dst, src, ACT.Exp, bias=tiny[:, 4 + i % 4:5 + i % 4],
                                         scale=scale, accum_out=tiny[:, 8 + i % 4:9 + i % 4])\
                      .then_inc(s["exped"], 1)

                def ev(i):
                    st = steps[i]
                    if st["t"] is None:
                        return
                    act.wait_ge(s["turned"], st["t"] + 1)
                    if st["unit"] >= 2:
                        act.wait_ge(s["pv"], st["unit"] - 1)
                    n = st["nk"] // P
                    pt = hooks["pt"][st["unit"] % 2][:, 0:n, st["half"] * P:(st["half"] + 1) * P]
                    if n > 3:
                        pt = pt.rearrange("p (b k) q -> p b k q", b=2)
                        src = psum[:, 4:6, 0:384].rearrange("p b (k q) -> p b k q", k=3)
                    else:
                        src = bank(4, c1=n * P).rearrange("p (k q) -> p k q", k=n)
                    nc.scalar.activation(pt, src, ACT.Copy).then_inc(s["ev"], 1)

                def pv_hi(u):
                    un = units[u]
                    r0, r1 = un["rows"]
                    act.wait_ge(s["pv"], u + 1)
                    nc.scalar.activation(hooks["hi"](un), bank(6, r0, r1, 0, 256), ACT.Copy)\
                      .then_inc(s["pv_hi"], 1)

                exp(0)
                for i in range(len(steps) + 1):
                    hooks["act"](i)
                    if i:
                        ev(i - 1)
                    if i + 1 < len(steps):
                        exp(i + 1)
                    if i:
                        if unit_after(steps[i - 1]):
                            pv_hi(steps[i - 1]["unit"] - 1)
                    if "act_end" in hooks:
                        hooks["act_end"](i)
                pv_hi(len(units) - 1)

            act.dma_start(vec[:, :], a["vectors"]).then_inc(vec_landed, 16)
            act.wait_ge(cond_landed, 16)
            nc.scalar.activation(cvec[:, :], cvec[:, :], ACT.Silu).then_inc(silu_ready, 1)
            act.wait_ge(m_first[0], 16 * 4)
            act.dma_start(res3, a["tokens"]).then_inc(res_landed, 16)
            def sum_product(i):
                x = h_f[:, (i % 6) * 1024:(i % 6 + 1) * 1024]
                act.wait_ge(pooled_first, i + 1)
                q = MOD_GROUP + i // 3 * 4 + i % 3
                nc.scalar.activation(x, x, ACT.Copy, accum_out=dots[:, q:q + 1]).then_inc(summed_first, 1)

            for i in range(6):
                sum_product(i)
            act.wait_ge(res_landed, 16)
            for i in range(6, 12):
                square(0, i - 6, ALL)
                sum_product(i)
            for k in (6, 7):
                square(0, k, ALL)
            act.wait_ge(const_ready, 1)
            split(0)
            split(1)
            v = 0
            for layer in (0, 1):
                s = m1[layer]
                n0 = N_IN[layer]
                t0 = layer * (IN_TILES + OUT_TILES + 64)
                cols = ALL if layer == 0 else LAT
                norm(v, ALL, lambda k, which: M(layer, 0, k, which))
                v += 1

                def at_step(j):
                    ahead(n0 + j)
                    act.wait_ge(tile_done, n0 + j + 1)

                at_step(0)
                if layer:
                    act.wait_ge(cond_landed, 32)
                    nc.scalar.activation(cvec[:, :], cvec[:, :], ACT.Silu).then_inc(silu_ready, 1)
                copy_out(t0, lambda x, y: ckv[:, 0, x:y], ALL)
                at_step(1)
                for k in range(2):
                    at_step(2 + k)
                    copy_out(t0 + 2 + k, lambda x, y: cq[:, k, x:y], cols)
                act.wait_ge(drained[0], (t0 + 2) // 2)
                act.wait_ge(norm_out, 8 * (2 * layer + 1))
                nc.scalar.activation(tmp2[:, 0, :], ckv[:, 0, :], ACT.Square).then_inc(s["ckv_in"], 1)
                for k in range(2):
                    at_step(4 + k)
                    copy_out(t0 + 4 + k, lambda x, y: zf[:, k, x:y], cols)
                act.wait_ge(s["ckv_sum"], 1)
                inv_sqrt(inverse(ALL), sums(ALL), P).then_inc(s["lora_sums"], 1)
                act.wait_ge(s["lora_ready"], 1)
                act.wait_ge(drained[1], (t0 + 4) // 2)
                for k in range(2):
                    nc.scalar.activation(tmp2[:, k, cols[0]:cols[1]], cq[:, k, cols[0]:cols[1]],
                                         ACT.Square).then_inc(s["ckv_in"], 1)
                for k in range(2):
                    at_step(6 + k)
                    copy_out(t0 + 6 + k, lambda x, y: sgate[:, k, x:y], cols, ACT.Sigmoid)
                act.wait_ge(s["ckv_sum"], 2)
                inv_sqrt(inverse(cols), sums(cols), 2 * P).then_inc(s["lora_sums"], 1)
                at_step(8)
                at_step(9)
                sa = att[layer]
                plan = plans[layer]
                per = len(plan[0]) // HEADS
                npc = len(pieces_of(layer, 0))

                def proj_ev(h, i):
                    kind, (x, y) = pieces_of(layer, h)[i]
                    act.wait_ge(sa["proj"], npc * h + i + 1)
                    r = 96 if kind == "q" else 64
                    dst = (qbuf if kind == "q" else kbuf)[0:r, h % 2, x:y]
                    if (kind, (x, y)) == ("q", LAT):
                        if h:
                            act.wait_ge(sa["proj_dve"], h)
                        nc.scalar.activation(rtmp[96:128, :], bank(7, 96, 128), ACT.Copy)
                    nc.scalar.activation(dst, bank(7, 0, r, 0, y - x), ACT.Copy)\
                      .then_inc(sa["proj_act"], 1)

                for c in range(2):
                    proj_ev(0, c)
                    act.wait_ge(s["y_mm"], c + 1)
                    for seg, b in both(cols):
                        last = nc.scalar.activation(zf[:, c, seg[0]:seg[1]],
                                                    bank(2 + c if b else 4 + c, c1=w(seg)), ACT.Copy)
                    last.then_inc(s["y_cp"], 1)
                for m in range(2):
                    act.wait_ge(s["f_mm"], m + 1)
                    for seg, b in both(cols):
                        last = nc.scalar.activation(hi3[:, m, seg[0]:seg[1]],
                                                    bank(m if b else 6 + m, c1=w(seg)), ACT.Copy)
                    last.then_inc(s["f_hi"], 1)

                for i in range(2, npc):
                    proj_ev(0, i)

                def act_hook(i):
                    h, j = divmod(i, per)
                    if h + 1 < HEADS and j < npc:
                        proj_ev(h + 1, j)

                def act_end(i):
                    g, seg, stage = ln_stage(layer, i)
                    if stage == 0:
                        act.wait_ge(s["ln"], 6 * g + 1)
                        for c in range(2):
                            last = nc.scalar.activation(u_pad[:, c, 0:w(seg)], conv_of(c, seg), ACT.Square)
                        last.then_inc(s["ln"], 1)
                    elif stage == 1:
                        act.wait_ge(s["ln"], 6 * g + 3)
                        inv_sqrt(ckv[:, 0, 0:w(seg)], bank(7, c1=w(seg)), 2 * P).then_inc(s["ln"], 1)
                    elif stage == 2:
                        act.wait_ge(s["ln"], 6 * g + 5)
                        for c in range(2):
                            last = nc.scalar.activation(conv_of(c, seg), conv_of(c, seg), ACT.Silu,
                                                        bias=V("lnb", 2 * layer + c))
                        last.then_inc(s["ln"], 1)

                attention(sa, plan, MLA_SCALE, dict(
                    pt=pt1, act=act_hook, act_end=act_end,
                    hi=lambda un: hi3[un["rows"][0]:un["rows"][1], 2 + un["h"] // 2,
                                      un["q0"]:un["q0"] + 256]))

                for m in range(2):
                    act.wait_ge(s["p_mm"], m + 1)
                    for seg, b in both(cols):
                        last = nc.scalar.activation(hi3[:, 6 + m, seg[0]:seg[1]],
                                                    bank(4 - 2 * m + b, c1=w(seg)), ACT.Copy)
                    last.then_inc(s["p_hi"], 1)
                for j in range(OUT_TILES):
                    ahead(n0 + IN_TILES + j)
                    if j:
                        squares(v, cols, t0 + IN_TILES + j - 1, j - 1)
                squares(v, cols, t0 + IN_TILES + 7, 7)
                n1, t1 = n0 + IN_TILES + OUT_TILES, t0 + IN_TILES + OUT_TILES
                norm(v, cols, lambda k, which: M(layer, 3, k, which))
                v += 1
                e0 = 32 * layer
                c0, c1 = cols
                def quarter(i, last_one=False):
                    for j in range(MLP_STEPS):
                        ahead(n1 + j, i * MLP_STEPS)
                        if last_one and j > 8:
                            squares(v, cols, t1 + MLP_STEPS * i + j - 1, j - 9)
                            if layer:
                                square_gained(j - 9)
                        if j < 8:
                            t = t1 + j
                            act.wait_ge(tile_done, i * MLP_STEPS + (n1 + j + 1))
                            if j >= 2:
                                act.wait_ge(hid_ready, i * 8 + (e0 + j - 1))
                            for (s0, s1), b in both(cols):
                                last = nc.scalar.activation(tmp2[:, j % 2, s0:s1],
                                                            bank(2 * (t % 2) + b, c1=s1 - s0), ACT.Relu)
                            last.then_inc(drained[t % 2], 1)
                            act.wait_ge(squared, i * 8 + (e0 + j + 1))
                            nc.scalar.activation(hid_hi3[:, j, c0:c1], tmp2[:, j % 2, c0:c1], ACT.Copy)\
                              .then_inc(hid_hi, 1)
                            if last_one and layer:
                                if j == 0:
                                    act.wait_ge(late["context2"], 16)
                                square_ctx(j)

                with act.Fori(0, QUARTERS - 1) as i:
                    quarter(i)
                quarter(QUARTERS - 1, last_one=True)
                squares(v, cols, t1 + QUARTERS * MLP_STEPS - 1, 7)
                if layer:
                    square_gained(7)
            t2 = 2 * (IN_TILES + OUT_TILES + 64)
            v = 5
            act.wait_ge(sum_ready, v)
            chain.mark(nc.scalar.activation(r_final, bank(5), ACT.Ln, bias=tiny[:, 0:1], scale=1.0 / D))
            act.wait_ge(sum_ready, v + 1)
            chain.mark(nc.scalar.activation(ctx_sum, bank(6, c1=NC_), ACT.Ln, bias=tiny[:, 0:1],
                                            scale=1.0 / D))
            chain.wait()
            nc.scalar.activation(r_final, r_final, ACT.Exp, scale=-0.5).then_inc(rstd_ready, 1)
            chain.mark(nc.scalar.activation(ctx_sum, ctx_sum, ACT.Exp, scale=-0.5))
            act.wait_ge(final_mean, 2)
            x = rstd[:, NC_:T]
            chain.mark(nc.scalar.activation(x, x, ACT.Ln, bias=tiny[:, 0:1], scale=1.0 / D))
            chain.wait()
            nc.scalar.activation(x, x, ACT.Exp, scale=-0.5).then_inc(rstd_ready, 1)
            n0 = N_BLOCK2
            shifted(ALL, lambda k, which: M(2, 0, k, which))
            v += 1
            for j in range(QK_TILES):
                ahead(n0 + j)
                act.wait_ge(tile_done, n0 + j + 1)
                name, idx = QK_ORDER[j]
                if name == "q":
                    nc.scalar.activation(q2[:, idx, :], bank(2 * ((t2 + j) % 2) + 1), ACT.Copy)\
                      .then_inc(drained[(t2 + j) % 2], 1)
                else:
                    copy_out(t2 + j, lambda x, y: k2[:, idx, x:y], ALL)
                if 1 <= j <= N_NORMED:
                    act.wait_ge(s2["sum"], j)
                    if j >= 2:
                        act.wait_ge(s2["normed"], j - 1)
                    sg = LAT if QK_ORDER[j - 1][0] == "q" else ALL
                    inv_sqrt(inverse(sg), sums(sg), HD).then_inc(s2["sub_r"], 1)
                if j < N_NORMED:
                    seg = LAT if name == "q" else ALL
                    act.wait_ge(drained[(t2 + j) % 2], (t2 + j) // 2 + 1)
                    src = q2[:, idx, :] if name == "q" else k2[:, idx, :]
                    nc.scalar.activation(tmp2[:, 0, seg[0]:seg[1]], src, ACT.Square)\
                      .then_inc(s2["sq"], 1)
            for c in range(V_TILES):
                j = QK_TILES + c
                ahead(n0 + j)
                act.wait_ge(tile_done, n0 + j + 1)
                if c in (0, 2):
                    continue
                t = t2 + QK_TILES + c // 2
                if c < 4:
                    b0 = 3 * (t % 2)
                    dst, src = v2[:, :, c // 2 * 256:c // 2 * 256 + 256], psum[:, b0:b0 + 3, :]
                    dst = dst.rearrange("p (b k) c -> p b k c", b=3)
                    src = src.rearrange("p b (k c) -> p b k c", k=2)
                else:
                    dst = v2[:, :, 512:640].rearrange("p (b k) c -> p b k c", b=2)
                    src = psum[:, 4:6, 0:384].rearrange("p b (k c) -> p b k c", k=3)
                nc.scalar.activation(dst, src, ACT.Copy).then_inc(drained[t % 2], 1)
            act.wait_ge(s2["lam"], 2)
            nc.scalar.activation(coef[:, 0:2], bank(7, c1=2), ACT.Exp).then_inc(s2["lam"], 1)

            def gqa_hi(un):
                if un["kind"] == "diff":
                    return diff_out[:, un["h"], un["q0"]:un["q0"] + 256]
                return mix_hi[un["rows"][0]:un["rows"][1], 4 + un["h"] // 2, un["q0"]:un["q0"] + 256]

            def act_hook(i):
                for h in range(4):
                    stage = i - SUB_AT - SUB_STEP * h
                    if stage == 0:
                        act.wait_ge(att[2]["pv_hi"], 2 * h + 2)
                        if h:
                            act.wait_ge(s2["sub_sum"], h)
                        nc.scalar.activation(rtmp[:, :], diff_out[:, h, :], ACT.Square)\
                          .then_inc(s2["sub_sq"], 1)
                    elif stage == 4:
                        act.wait_ge(s2["mix_t"], h + 1)
                        nc.scalar.activation(mix_hi[:, h, :], diff_out[:, h, :], ACT.Copy)\
                          .then_inc(s2["mix_hi"], 1)

            def act_end(i):
                for h in range(4):
                    if i - SUB_AT - SUB_STEP * h == 1:
                        act.wait_ge(s2["sub_sum"], h + 1)
                        if h:
                            act.wait_ge(s2["mix_t"], h)
                        inv_sqrt(rstd[:, 0:NX], bank(7), P).then_inc(s2["sub_r"], 1)
            attention(att[2], plans[2], GQA_SCALE, dict(pt=pt2, act=act_hook, act_end=act_end, hi=gqa_hi))
            for j in range(OUT_TILES):
                ahead(n0 + QK_TILES + V_TILES + j)
                if j:
                    squares(v, LAT, t2 + QK_TILES + V_OUTS + j - 1, j - 1)
            squares(v, LAT, t2 + QK_TILES + V_OUTS + 7, 7)
            t3 = t2 + QK_TILES + V_OUTS + OUT_TILES

            def ffn(layer, tb):
                nf = N_FFN[layer]
                pair0 = 0
                for part, kk in enumerate(FFN_PARTS):
                    nb = nf + sum(3 * x for x in FFN_PARTS[:part])
                    tb_part = tb + sum(2 * x + 8 for x in FFN_PARTS[:part])
                    e0 = layer * FFN_T + pair0
                    with act.Fori(0, kk // 2) as i:
                        for j in range(4):
                            ahead(nb + j, i * 4)
                            q, is_up = j // 2, j % 2
                            dst = (ups if is_up else gates)[:, q, :]
                            t = tb_part + j
                            col = layer * 44 * 3 + 44 + 2 * pair0 + j
                            act.wait_ge(tile_done, i * 4 + (nb + j + 1))
                            act.wait_ge(loaded, 16 * 6)
                            nc.scalar.activation(dst, bank(2 * (t % 2) + 1), ACT.Identity,
                                                 bias=vec[:, bass.ds(i * 4 + (VEC["fcb"] + layer * 44 + 2 * pair0 + j), 1)],
                                                 scale=vec[:, bass.ds(i * 4 + (VEC["fcw"] + col), 1)])\
                              .then_inc(s2["g_ready"], 1)
                            if is_up:
                                act.wait_ge(drained[(t - 1) % 2], i * 2 + ((t - 1) // 2 + 1))
                                nc.scalar.activation(gates[:, q, :], gates[:, q, :], ACT.Silu)\
                                  .then_inc(s2["f_hi"], 1)
                                act.wait_ge(s2["prod"], i * 2 + (e0 + q + 1))
                                act.wait_ge(loaded, 16 * 6)
                                nc.scalar.activation(
                                    hid_hi_f[:, bass.ds(i * 2 * NX + q * NX, NX)],
                                    prods[:, q, :], ACT.Copy).then_inc(hid_hi, 1)
                    m = 0
                    for j in range(kk):
                        ahead(nb + 2 * kk + j)
                        while part and (m + 1) * kk <= 8 * j:
                            squares(v, LAT, tb_part + 2 * kk + m, m)
                            m += 1
                    while part and m < 8:
                        squares(v, LAT, tb_part + 2 * kk + m, m)
                        m += 1
                    pair0 += kk

            norm(v, LAT, lambda k, which: M(2, 3, k, which))
            v += 1
            ffn(0, t3)
            t4 = t3 + 2 * FFN_T + 16
            norm(v, LAT, lambda k, which: M(3, 0, k, which))
            v += 1
            for j in range(SGU_U + SGU_V):
                ahead(N_SGU + j)
                act.wait_ge(tile_done, N_SGU + j + 1)
                if j >= SGU_U and (j - SGU_U) % 2 == 0:
                    continue
                t = t4 + (j if j < SGU_U else SGU_U + (j - SGU_U) // 2)
                if j < SGU_U:
                    dst, src = su[:, j, :], bank(2 * (t % 2) + 1)
                else:
                    c = (j - SGU_U) // 2
                    dst = sv[:, :, c * 256:(c + 1) * 256].rearrange("p (b k) c -> p b k c", b=2)
                    src = psum[:, 2 * (t % 2):2 * (t % 2) + 2, :].rearrange("p b (k c) -> p b k c", k=2)
                nc.scalar.activation(dst, src, ACT.Gelu).then_inc(drained[t % 2], 1)
            t5 = t4 + SGU_U + SGU_V_OUTS
            for i in (0, 1):
                act.wait_ge(drained[i], t5 // 2)
            for k in range(4):
                chain.mark(nc.scalar.activation(h_f[:, 5120:6144], sv[:, k, :], ACT.Square,
                                                accum_out=tiny[:, 16 + k:17 + k]))
                chain.wait()
            inv_sqrt(tiny[:, 20:24], tiny[:, 16:20], D).then_inc(s2["sv"], 1)
            for c in range(8):
                act.wait_ge(s2["mix_t"], 4 + c + 1)
                nc.scalar.activation(mix_hi[:, c, :], tmp2[:, c % 2, 0:NX], ACT.Copy)\
                  .then_inc(s2["mix_hi"], 1)
            for j in range(OUT_TILES):
                ahead(N_SGU + SGU_U + SGU_V + j)
                if j:
                    squares(v, LAT, t5 + j - 1, j - 1)
            squares(v, LAT, t5 + 7, 7)
            t6 = t5 + OUT_TILES
            norm(v, LAT, lambda k, which: M(3, 3, k, which))
            v += 1
            ffn(1, t6)
            norm(v, LAT, None)

        @block.tensor
        def _(pe):
            def tile(n, j, t, cols, rhs_hi, rhs_lo, per_k=None, first=True):
                pe.wait_ge(lo_ready, n + 1)
                if first:
                    slot_free(t)
                for k in range(8):
                    if per_k:
                        per_k(k)
                    for wt, x in ((whi3, rhs_hi), (whi3, rhs_lo), (wlo3, rhs_hi)):
                        for (s0, s1), b in both(cols):
                            mm = pe.matmul(bank(2 * (t % 2) + b, c1=s1 - s0), wt[:, j % 2, k, :],
                                           x(k, s0, s1), start=(k == 0 and wt is whi3 and x is rhs_hi),
                                           stop=(k == 7 and wt is wlo3))
                mm.then_inc(tile_done, 1)

            def pair(n, t, cols, ready):
                for k in range(8 + PAIR_LAG):
                    for i, kk in enumerate((k, k - PAIR_LAG)):
                        if not 0 <= kk < 8:
                            continue
                        if kk == 0:
                            pe.wait_ge(lo_ready, n + i + 1)
                            if t + i >= 2:
                                pe.wait_ge(drained[(t + i) % 2], (t + i) // 2)
                        if i == 0:
                            ready(kk)
                        for q, (wt, x) in enumerate(((whi3, hi3), (whi3, lo3), (wlo3, hi3))):
                            for (s0, s1), b in both(cols[i]):
                                mm = pe.matmul(bank(2 * ((t + i) % 2) + b, c1=s1 - s0),
                                               wt[:, (n + i) % 2, kk, :], x[:, kk, s0:s1],
                                               start=(kk == 0 and q == 0), stop=(kk == 7 and q == 2))
                        if kk == 7:
                            mm.then_inc(tile_done, 1)

            def token_major(n, toks, b0, off):
                for h in range(2):
                    pe.wait_ge(lo_ready, n + h + 1)
                    w_hi, w_lo = (x[:, (n + h) % 2].rearrange("p k m -> p (k m)")
                                  .rearrange("p (k m) -> p k m", k=4) for x in (whi3, wlo3))
                    for tok in range(toks):
                        for k in range(4):
                            kk = 4 * h + k
                            xs = slice(off + tok * P, off + (tok + 1) * P)
                            for q, (x, wt) in enumerate(((hi3, w_hi), (lo3, w_hi), (hi3, w_lo))):
                                mm = pe.matmul(bank(b0 + tok // 2, c0=256 * (tok % 2),
                                                    c1=256 * (tok % 2) + 256),
                                               x[:, kk, xs], wt[:, k, :],
                                               start=(kk == 0 and q == 0 and tok % 2 == 0),
                                               stop=(kk == 7 and q == 2 and tok % 2 == 1))
                    mm.then_inc(tile_done, 1)

            def slot_free(t):
                if t >= 2:
                    pe.wait_ge(drained[t % 2], t // 2)

            def norm(v, cols):
                pe.wait_ge(sq_added, 7 * sq(v) + 7)
                for (s0, s1), dst in sum_banks(cols):
                    mm = pe.matmul(dst, ones[:, :], rstd[:, s0:s1], start=True, stop=True)
                mm.then_inc(sum_ready, 1)

            def in_hi(k, x, y):
                return hi3[:, k, x:y]

            def in_lo(k, x, y):
                return lo3[:, k, x:y]

            def attention(s, plan, hooks):
                steps, units = plan

                def scores(i):
                    st = steps[i]
                    if i >= 2:
                        pe.wait_ge(s["exped"], i - 1)
                    hooks["ready"](i)
                    for b in range(0, st["nk"], 384):
                        e = min(st["nk"], b + 384)
                        mm = pe.matmul(bank(2 * (i % 2) + b // 384, c1=e - b), st["q"], st["k"][:, b:e],
                                       start=True, stop=True)
                    mm.then_inc(s["scores"], 1)

                def turn(i):
                    st = steps[i]
                    pe.wait_ge(s["p_ready"], i + 1)
                    if st["t"]:
                        pe.wait_ge(s["ev"], st["t"])
                    p = p_slot(st["p"])
                    n = st["nk"] // P
                    for k in range(n):
                        mm = pe.transpose(bank(4 + k // 3, c0=(k % 3) * P, c1=(k % 3 + 1) * P),
                                          p[:, k * P:(k + 1) * P], ident[:, :])
                    mm.then_inc(s["turned"], 1)

                def pv(u):
                    un = units[u]
                    r0, r1 = un["rows"]
                    pe.wait_ge(s["ev"], un["t_end"])
                    if u:
                        pe.wait_ge(s["pv_hi"], u)
                        if un["lo_before"]:
                            pe.wait_ge(s["pv_lo"], un["lo_before"])
                    n = un["nk"] // P
                    for k in range(n):
                        mm = pe.matmul(bank(6, r0, r1, 0, 256), hooks["v"](un, k),
                                       hooks["pt"][u % 2][:, k, :], start=(k == 0), stop=(k == n - 1))
                    mm.then_inc(s["pv"], 1)

                scores(0)
                for i in range(len(steps) + 1):
                    if i + 1 < len(steps):
                        scores(i + 1)
                    hooks["pe"](i)
                    if i and steps[i - 1]["t"] is not None:
                        if unit_after(steps[i - 1]):
                            pv(steps[i - 1]["unit"] - 1)
                        turn(i - 1)
                pv(len(units) - 1)

            pe.wait_ge(const_ready, 2)
            v = 0
            for layer in (0, 1):
                s = m1[layer]
                n0 = N_IN[layer]
                t0 = layer * (IN_TILES + OUT_TILES + 64)
                cols = ALL if layer == 0 else LAT
                norm(v, ALL)
                out_at = 8 * 2 * layer
                v += 1
                pair(n0, t0, (ALL, ALL), lambda k: pe.wait_ge(norm_out, out_at + k + 1))
                for j in range(2, IN_TILES):
                    tile(n0 + j, (n0 + j) % 4, t0 + j, cols, in_hi, in_lo)
                    if j == 4:
                        pe.wait_ge(s["ckv_in"], 1)
                        for (s0, s1), dst in sum_banks(ALL):
                            mm = pe.matmul(dst, ones[:, :], tmp2[:, 0, s0:s1], start=True, stop=True)
                        mm.then_inc(s["ckv_sum"], 1)
                    if j == 6:
                        pe.wait_ge(s["ckv_in"], 3)
                        for k in range(2):
                            for (s0, s1), dst in sum_banks(cols):
                                mm = pe.matmul(dst, ones[:, :], tmp2[:, k, s0:s1], start=(k == 0),
                                               stop=(k == 1))
                        mm.then_inc(s["ckv_sum"], 1)
                pe.wait_ge(s["lora_ready"], 1)
                if layer:
                    pe.wait_ge(late["small_w"], 16)
                for k in range(6):
                    if k >= 2:
                        pe.wait_ge(s["v_cp"], k - 1)
                    pe.matmul(bank(6 + k % 2), ckv[:, 0, k * P:(k + 1) * P], uv, start=True, stop=True)\
                      .then_inc(s["v_mm"], 1)
                toks = range(0 if layer == 0 else 2, 6)
                pe.wait_ge(drained[0], (t0 + 10) // 2)
                pe.wait_ge(drained[1], (t0 + 10) // 2)
                for i, k in enumerate(toks):
                    if i >= 2:
                        pe.wait_ge(s["ab_cp"], i - 1)
                    for c in range(2):
                        mm = pe.matmul(bank(i % 2, c0=256 * c, c1=256 * c + 256),
                                       zf[:, c, k * P:(k + 1) * P], chan_dft[:, :], start=True, stop=True)
                    mm.then_inc(s["ab_mm"], 1)
                sa = att[layer]
                plan = plans[layer]
                per = len(plan[0]) // HEADS
                npc = len(pieces_of(layer, 0))

                def project(h, i):
                    kind, (x, y) = pieces_of(layer, h)[i]
                    p = npc * h + i
                    if p:
                        pe.wait_ge(sa["proj_act"], p)
                    if kind == "q":
                        for k in range(2):
                            mm = pe.matmul(bank(7, c1=y - x), uq[:, h, k, :], cq[:, k, x:y],
                                           start=(k == 0), stop=(k == 1))
                    else:
                        mm = pe.matmul(bank(7, 0, 64, 0, y - x), uk[:, h, :], ckv[:, 0, x:y],
                                       start=True, stop=True)
                    mm.then_inc(sa["proj"], 1)

                pe.wait_ge(s["v_cp"], 6)
                pe.wait_ge(s["lora_ready"], 3)
                pe.wait_ge(s["ab_cp"], len(toks))
                pe.wait_ge(late["dft"], 32 * (layer + 1))
                for c in range(2):
                    project(0, c)
                    for seg, b in both(cols):
                        first, table = (0, dft_c) if seg == CTX else (2, dft_x)
                        nk = w(seg) // P
                        for k in range(nk):
                            for part in range(2):
                                mm = pe.matmul(bank(2 + c if b else 4 + c, c1=w(seg)),
                                               ab[:, first + k, 256 * c + 128 * part:
                                                  256 * c + 128 * part + 128],
                                               table[:, part, k, :], start=(k == 0 and part == 0),
                                               stop=(k == nk - 1 and part == 1))
                    mm.then_inc(s["y_mm"], 1)
                pe.wait_ge(s["y_cp"], 2)
                pe.wait_ge(sa["proj_act"], 2)
                for m in range(2):
                    for seg, b in both(cols):
                        for c in range(2):
                            mm = pe.matmul(bank(m if b else 6 + m, c1=w(seg)), wf[:, m, c, :],
                                           zf[:, c, seg[0]:seg[1]], start=(c == 0), stop=(c == 1))
                    mm.then_inc(s["f_mm"], 1)
                pe.wait_ge(s["f_lo"], 2)
                for i in range(2, npc):
                    project(0, i)

                def pe_hook(i):
                    h, j = divmod(i, per)
                    if h + 1 < HEADS and j < npc:
                        project(h + 1, j)
                    g, seg, stage = ln_stage(layer, i)
                    if stage == 0:
                        if g == 0:
                            pe.wait_ge(sa["proj_act"], npc * HEADS)
                            pe.wait_ge(tapped, layer + 1)
                            pe.wait_ge(s["u_ready"], 1)
                        else:
                            pe.wait_ge(s["ln"], 6 * g - 2)
                        for c in range(2):
                            mm = pe.matmul(bank(7, c1=w(seg)), ones[:, :], conv_of(c, seg),
                                           start=(c == 0), stop=(c == 1))
                        mm.then_inc(s["u_ready"], 1)
                    elif stage == 1:
                        pe.wait_ge(s["ln"], 6 * g + 2)
                        for c in range(2):
                            mm = pe.matmul(bank(7, c1=w(seg)), ones[:, :], u_pad[:, c, 0:w(seg)],
                                           start=(c == 0), stop=(c == 1))
                        mm.then_inc(s["ln"], 1)

                def head_ready(i):
                    h, j = divmod(i, per)
                    if j == 0:
                        pe.wait_ge(sa["proj_act"], npc * (h + 1))
                        pe.wait_ge(sa["proj_dve"], h + 1)

                attention(sa, plan, dict(pe=pe_hook, ready=head_ready, pt=pt1,
                                         v=lambda un, k: v1[:, k, 64 * un["h"]:64 * un["h"] + 64]))
                for m in range(2):
                    for seg, b in both(cols):
                        for c in range(2):
                            mm = pe.matmul(bank(4 - 2 * m + b, c1=w(seg)), wp[:, m, c, :],
                                           conv_of(c, seg), start=(c == 0), stop=(c == 1))
                    mm.then_inc(s["p_mm"], 1)
                units = len(plan[1])

                def mixed_ready(k):
                    if k == 2:
                        pe.wait_ge(sa["pv_lo"], units * 3 // 4)
                    if k == 5:
                        pe.wait_ge(sa["pv_lo"], units)
                    if k >= 6:
                        pe.wait_ge(s["p_lo"], k - 5)

                for j in range(OUT_TILES):
                    n = n0 + IN_TILES + j
                    tile(n, n % 4, t0 + IN_TILES + j, cols, in_hi, in_lo,
                         per_k=None if j else mixed_ready)
                n1, t1 = n0 + IN_TILES + OUT_TILES, t0 + IN_TILES + OUT_TILES
                norm(v, cols)
                v += 1
                e0 = 32 * layer
                def quarter(i, first=False):
                    if first:
                        pair(n1, t1, (cols, cols),
                             lambda k: pe.wait_ge(norm_out, 8 * (2 * layer + 1) + k + 1))
                    for j in range(2 if first else 0, MLP_STEPS):
                        n, t = n1 + j, t1 + j
                        pe.wait_ge(lo_ready, i * MLP_STEPS + (n + 1))
                        pe.wait_ge(drained[t % 2], i * 8 + t // 2)
                        hi_, lo_ = (hi3, lo3) if j < 8 else (hid_hi3, hid_lo3)
                        for k in range(8):
                            if j == 8:
                                pe.wait_ge(hid_ready, i * 8 + (e0 + k + 1))
                            for q, (wt, x) in enumerate(((whi3, hi_), (whi3, lo_), (wlo3, hi_))):
                                for (s0, s1), b in both(cols):
                                    mm = pe.matmul(bank(2 * (t % 2) + b, c1=s1 - s0), wt[:, n % 2, k, :],
                                                   x[:, k, s0:s1], start=(k == 0 and q == 0),
                                                   stop=(k == 7 and q == 2))
                        mm.then_inc(tile_done, 1)

                quarter(0, first=True)
                with pe.Fori(1, QUARTERS) as i:
                    quarter(i)

            norm(v, LAT)
            v += 1
            pe.wait_ge(sq_ctx_added, 7)
            pe.matmul(bank(6, c1=NC_), ones[:, :], ctx_sum, start=True, stop=True)
            pe.wait_ge(sq_gain_added, 7)
            pe.matmul(bank(4), ones[:, :], gained_sum, start=True, stop=True).then_inc(sum_ready, 1)
            v += 1
            n0 = N_BLOCK2
            t2 = 2 * (IN_TILES + OUT_TILES + 64)

            def block_sum(j):
                name, idx = QK_ORDER[j]
                pe.wait_ge(s2["sq"], j + 1)
                for (s0, s1), dst in sum_banks(LAT if name == "q" else ALL):
                    mm = pe.matmul(dst, halves[:, :], tmp2[:, 0, s0:s1], start=True, stop=True)
                mm.then_inc(s2["sum"], 1)

            def swap_pairs(j):
                name, idx = QK_ORDER[j]
                if j < N_NORMED:
                    pe.wait_ge(s2["normed"], j + 1)
                else:
                    t = t2 + j
                    pe.wait_ge(drained[t % 2], t // 2 + 1)
                if j >= 2:
                    pe.wait_ge(s2["roped"], j - 1)
                src = q2[:, idx, :] if name == "q" else k2[:, idx, NC_:T]
                pe.matmul(bank(6 + j % 2), swap[:, :], src, start=True, stop=True)\
                  .then_inc(s2["perm"], 1)

            pair(n0, t2, (LAT, LAT), lambda k: pe.wait_ge(norm_out, 8 * 5 + k + 1))
            for j in range(1, QK_TILES):
                name, idx = QK_ORDER[j]
                if j >= 2:
                    tile(n0 + j, (n0 + j) % 4, t2 + j, LAT if name == "q" else ALL, in_hi, in_lo)
                if 1 <= j <= N_NORMED:
                    block_sum(j - 1)
                if j >= 2:
                    swap_pairs(j - 2)
            for c in range(2):
                swap_pairs(QK_TILES - 2 + c)
                t = t2 + QK_TILES + c
                slot_free(t)
                token_major(n0 + QK_TILES + 2 * c, 6, 3 * (t % 2), 0)
            n, t = n0 + QK_TILES + 4, t2 + QK_TILES + 2
            pe.wait_ge(lo_ready, n + 1)
            slot_free(t)
            for tok in range(6):
                b, c0 = 4 + tok // 3, tok % 3 * P
                for k in range(8):
                    for q, (x, wt) in enumerate(((hi3, whi3), (lo3, whi3), (hi3, wlo3))):
                        mm = pe.matmul(bank(b, c0=c0, c1=c0 + P), x[:, k, tok * P:(tok + 1) * P],
                                       wt[:, n % 2, k, :], start=(k == 0 and q == 0),
                                       stop=(k == 7 and q == 2))
            mm.then_inc(tile_done, 1)
            pe.wait_ge(s2["lam"], 1)
            pe.wait_ge(s2["roped"], QK_TILES)
            pe.matmul(bank(7, c1=2), ones[0:HD, :], coef[0:HD, 2:4], start=True, stop=True)\
              .then_inc(s2["lam"], 1)
            for i in (0, 1):
                pe.wait_ge(drained[i], (t2 + QK_TILES + V_OUTS) // 2)
            pe.wait_ge(s2["lam"], 4)

            def gqa_v(un, k):
                if un["kind"] == "diff":
                    return v2[:, k, un["h"] * P:(un["h"] + 1) * P]
                g = un["h"] % 2
                return v2[:, k, 512 + 64 * g:512 + 64 * g + 64]

            def pe_hook(i):
                h, stage = divmod(i - SUB_AT, SUB_STEP)
                if stage == 1 and 0 <= h < 4:
                    pe.wait_ge(s2["sub_sq"], h + 1)
                    if h:
                        pe.wait_ge(s2["sub_r"], N_NORMED + h)
                    pe.matmul(bank(7), ones[:, :], rtmp[:, :], start=True, stop=True)\
                      .then_inc(s2["sub_sum"], 1)

            attention(att[2], plans[2], dict(pe=pe_hook, ready=lambda i: None, pt=pt2, v=gqa_v))
            t3 = t2 + QK_TILES + V_OUTS + OUT_TILES

            for j in range(OUT_TILES):
                n = n0 + QK_TILES + V_TILES + j
                if j == 0:
                    pe.wait_ge(s2["mix_lo"], 4)
                    pe.wait_ge(att[2]["pv_lo"], 16)
                tile(n, n % 4, t3 - OUT_TILES + j, LAT, lambda k, x, y: mix_hi[:, k, :],
                     lambda k, x, y: mix_lo[:, k, :])
            norm(v, LAT)
            v += 1

            def ffn(layer, tb, norm_at):
                nf = N_FFN[layer]
                pair0 = 0
                for part, kk in enumerate(FFN_PARTS):
                    nb = nf + sum(3 * x for x in FFN_PARTS[:part])
                    tb_part = tb + sum(2 * x + 8 for x in FFN_PARTS[:part])
                    def turn(i, first=False):
                        if first:
                            pair(nb, tb_part, (LAT, LAT), lambda k: pe.wait_ge(norm_out, norm_at + k + 1))
                        for j in range(2 if first else 0, 4):
                            n, t = nb + j, tb_part + j
                            pe.wait_ge(lo_ready, i * 4 + (n + 1))
                            pe.wait_ge(drained[t % 2], i * 2 + t // 2)
                            for k in range(8):
                                for q, (wt, x) in enumerate(((whi3, hi3), (whi3, lo3), (wlo3, hi3))):
                                    mm = pe.matmul(bank(2 * (t % 2) + 1), wt[:, n % 2, k, :],
                                                   x[:, k, NC_:T], start=(k == 0 and q == 0),
                                                   stop=(k == 7 and q == 2))
                            mm.then_inc(tile_done, 1)

                    if part == 0:
                        turn(0, first=True)
                    with pe.Fori(1 - part, kk // 2) as i:
                        turn(i)
                    n = nb + 2 * kk
                    block_no = 0
                    for m in range(8):
                        t = tb_part + 2 * kk + m
                        slot_free(t)
                        for k in range(kk):
                            if block_no % 8 == 0:
                                pe.wait_ge(lo_ready, n + 1)
                            if m == 0:
                                pe.wait_ge(hid_ready, 64 + layer * FFN_T + pair0 + k + 1)
                            for q, (wt, x) in enumerate(((whi3, fh_hi), (whi3, fh_lo), (wlo3, fh_hi))):
                                mm = pe.matmul(bank(2 * (t % 2) + 1), wt[:, n % 2, block_no % 8, :],
                                               x[:, k, :], start=(k == 0 and q == 0),
                                               stop=(k == kk - 1 and q == 2))
                            block_no += 1
                            if block_no % 8 == 0:
                                mm.then_inc(tile_done, 1)
                                n += 1
                        if block_no % 8:
                            mm.then_inc(p_chain, 1)
                    pair0 += kk

            ffn(0, t3, 8 * 6)
            t4 = t3 + 2 * FFN_T + 16
            norm(v, LAT)
            v += 1
            pair(N_SGU, t4, (LAT, LAT), lambda k: pe.wait_ge(norm_out, 8 * 7 + k + 1))
            for j in range(2, SGU_U):
                tile(N_SGU + j, (N_SGU + j) % 4, t4 + j, LAT, in_hi, in_lo)
            for c in range(SGU_V_OUTS):
                t = t4 + SGU_U + c
                slot_free(t)
                token_major(N_SGU + SGU_U + 2 * c, 4, 2 * (t % 2), NC_)
            pe.wait_ge(s2["sv"], 2)
            pe.wait_ge(late["sgu"], 32)
            for c in range(8):
                if c >= 2:
                    pe.wait_ge(s2["mix_t"], 4 + c - 1)
                for n in range(4):
                    mm = pe.matmul(bank(4 + c % 2, c0=n * P, c1=(n + 1) * P),
                                   sv[:, n, c * P:(c + 1) * P], ws[:, c // 2, :], start=True, stop=True)
                mm.then_inc(s2["mixed"], 1)
            t5 = t4 + SGU_U + SGU_V_OUTS
            for j in range(OUT_TILES):
                n = N_SGU + SGU_U + SGU_V + j
                tile(n, n % 4, t5 + j, LAT, lambda k, x, y: mix_hi[:, k, :],
                     lambda k, x, y: mix_lo[:, k, :],
                     per_k=(lambda k: pe.wait_ge(s2["mix_lo"], 4 + k + 1)) if j == 0 else None)
            norm(v, LAT)
            v += 1
            ffn(1, t5 + OUT_TILES, 8 * 8)
            norm(v, LAT)

        @block.vector
        def _(dve):
            chain = Chain(dve, d_chain)
            out_v = [0]

            def norm(v, cols, gains, shifts):
                segs = both(cols)
                o = out_v[0]
                dve.wait_ge(rstd_ready, v + 1)

                def low(k):
                    dve.wait_ge(norm_hi, 8 * o + k + 1)
                    for (s0, s1), b in segs:
                        last = nc.vector.scalar_tensor_tensor(
                            lo3[:, k, s0:s1], tmp2[:, k % 2, s0:s1], shifts(k, 1 - b),
                            hi3[:, k, s0:s1].bitcast(F32), ALU.add, ALU.subtract)
                    last.then_inc(norm_out, 1)

                for k in range(KD):
                    if k >= 2:
                        dve.wait_ge(norm_out, 8 * v + k - 1)
                    for (s0, s1), b in segs:
                        last = nc.vector.scalar_tensor_tensor(
                            tmp2[:, k % 2, s0:s1], res3[:, k, s0:s1], gains(k, 1 - b),
                            rstd[:, s0:s1], ALU.mult, ALU.mult)
                    last.then_inc(scaled, 1)
                    if k:
                        low(k - 1)
                low(KD - 1)
                out_v[0] += 1

            def add_square(v, k, cols):
                if k == 0:
                    return
                dve.wait_ge(sq_ready, 8 * sq(v) + k + 1)
                if k > 1:
                    dve.wait_ge(sq_added, 7 * sq(v) + k - 1)
                x = rstd[:, cols[0]:cols[1]]
                nc.vector.tensor_tensor(x, x, tmp2[:, k % 2, cols[0]:cols[1]], ALU.add)\
                  .then_inc(sq_added, 1)

            def add_beside(k, ready, added, x, slot):
                if k == 0:
                    return
                dve.wait_ge(ready, k + 1)
                if k > 1:
                    dve.wait_ge(added, k - 1)
                nc.vector.tensor_tensor(x, x, slot, ALU.add).then_inc(added, 1)

            def add_ctx(k):
                add_beside(k, sq_ctx, sq_ctx_added, ctx_sum, tmp2[:, k % 2, 0:NC_])

            def add_gained(k):
                add_beside(k, sq_gain, sq_gain_added, gained_sum, gained[:, k % 2, :])

            def final_norm(name, r):
                for k in range(KD):
                    nc.vector.scalar_tensor_tensor(
                        res3[:, k, NC_:T], res3[:, k, NC_:T], V(name, k), r,
                        ALU.mult, ALU.mult).then_inc(norm_out, 1)

            def gain_table(dst, name, i, block_, chunk, w_):
                for which in range(w_):
                    last = nc.vector.scalar_tensor_tensor(
                        coef[:, dst + 8 * which:dst + 8 * which + 8],
                        mod3[:, block_ * CH + chunk * KD:block_ * CH + chunk * KD + KD, which],
                        1.0, V(name, i, KD), ALU.add, ALU.mult)
                    chain.mark(last)
                chain.wait()

            def add_residual(t, m, cols, block_, chunk):
                for (s0, s1), b in both(cols):
                    last = nc.vector.scalar_tensor_tensor(
                        res3[:, m, s0:s1], bank(2 * (t % 2) + b, c1=s1 - s0),
                        M(block_, chunk, m, 1 - b), res3[:, m, s0:s1], ALU.mult, ALU.add)
                last.then_inc(drained[t % 2], 1)

            def mod_tile(m, q, both_, w_tile=None, shift=0):
                if w_tile is None:
                    j = m % MOD_RING
                    w_tile = mod_w[:, j * 1024:(j + 1) * 1024]
                    dve.wait_ge(m_landed[j], shift * 8 + 16 * ((m - MOD_GROUP) // MOD_RING + 1))
                else:
                    dve.wait_ge(m_first[m // 4], 16 * 4)
                    if m % 4 != 3:
                        both_ = False
                        dve.wait_ge(pooled_first, m // 4 * 3 + m % 4 + 1)
                if both_:
                    if half[0]:
                        dve.wait_ge(mod_half, half[0] + (half[1] if half[1] is not None else 0))
                    nc.vector.tensor_tensor_reduce(
                        rtmp_b, w_tile, cvec[:, D:2 * D], 1.0, 0.0, ALU.mult, ALU.add,
                        dots[:, MOD_GROUP + q:MOD_GROUP + q + 1]).then_inc(mod_half, 1)
                    half[0] += 1
                    dve.wait_ge(mod_half, half[0] + (half[1] if half[1] is not None else 0))
                nc.vector.tensor_tensor_reduce(
                    w_tile, w_tile, cvec[:, 0:D], 1.0, 0.0, ALU.mult, ALU.add,
                    dots[:, q:q + 1]).then_inc(mod_done, 1)

            half = [0, None]

            def mod_out(m, count, group, both_):
                dve.wait_ge(mod_done, m + count)
                for which in range(1 + both_):
                    last = nc.vector.tensor_tensor(
                        mod[:, bass.ds(m * 2, 2 * count)].rearrange("p (m v) -> p m v", v=2)[:, :, which],
                        dots[:, which * MOD_GROUP:which * MOD_GROUP + count],
                        vec[:, bass.ds(m + VEC["bias"], count)], ALU.add)
                last.then_inc(mod_drained, 1)
                dve.wait_ge(mod_drained, group + 1)

            def attention(s, plan, scale, hooks):
                steps, units = plan

                def maximum(i):
                    st = steps[i]
                    dve.wait_ge(s["scores"], i + 1)
                    c = tiny[:, 12 + i % 4:13 + i % 4]
                    if st["nk"] > 384:
                        last = nc.vector.tensor_reduce(c, psum[:, 2 * (i % 2):2 * (i % 2) + 2, 0:384],
                                                       AX.XY, ALU.max)
                    else:
                        last = nc.vector.tensor_reduce(c, bank(2 * (i % 2), c1=st["nk"]), AX.X, ALU.max)
                    chain.mark(last)
                    chain.wait()
                    nc.vector.tensor_scalar(tiny[:, 4 + i % 4:5 + i % 4], c, -scale, None, ALU.mult)\
                      .then_inc(s["maxed"], 1)

                def weigh(i):
                    st = steps[i]
                    dve.wait_ge(s["exped"], i + 1)
                    r = tiny[:, 24 + i % 4:25 + i % 4]
                    chain.mark(nc.vector.reciprocal(r, tiny[:, 8 + i % 4:9 + i % 4]))
                    chain.wait()
                    p = p_slot(st["p"])[:, 0:st["nk"]]
                    if st["post"] == "second":
                        chain.mark(nc.vector.tensor_tensor(r, r, coef[:, 4:5], ALU.mult))
                        chain.wait()
                        nc.vector.scalar_tensor_tensor(p, p, r, p_slot(steps[i - 1]["p"])[:, 0:st["nk"]],
                                                       ALU.mult, ALU.add).then_inc(s["p_ready"], 1)
                    else:
                        nc.vector.tensor_scalar(p, p, r, None, ALU.mult).then_inc(s["p_ready"], 1)
                        if st["post"] == "first":
                            dve.wait_ge(s["p_ready"], i + 1)

                def pv_lo(u):
                    un = units[u]
                    if not un["lo"]:
                        return
                    r0, r1 = un["rows"]
                    dve.wait_ge(s["pv_hi"], u + 1)
                    nc.vector.tensor_tensor(hooks["lo"](un), bank(6, r0, r1, 0, 256),
                                            hooks["hi"](un).bitcast(F32), ALU.subtract)\
                      .then_inc(s["pv_lo"], 1)

                maximum(0)
                for i in range(len(steps) + 1):
                    if i + 1 < len(steps):
                        maximum(i + 1)
                    if i < len(steps):
                        weigh(i)
                    hooks["dve"](i)
                    if i:
                        if unit_after(steps[i - 1]):
                            pv_lo(steps[i - 1]["unit"] - 1)
                pv_lo(len(units) - 1)

            nc.vector.memset(tiny[:, 0:1], EPS).then_inc(const_ready, 1)
            nc.vector.memset(ones[:, :], 1.0).then_inc(const_ready, 1)
            dve.wait_ge(silu_ready, 1)
            for m in range(MOD_GROUP):
                mod_tile(m, m, True, mod_first(m))
                if m >= MOD_GROUP - KD:
                    add_square(0, m - MOD_GROUP + KD, ALL)
            dve.wait_ge(vec_landed, 16)
            dve.wait_ge(summed_first, 12)
            mod_out(0, MOD_GROUP, 0, True)
            m0, group = MOD_GROUP, 1
            v = 0
            for layer in (0, 1):
                s = m1[layer]
                n0 = N_IN[layer]
                t0 = layer * (IN_TILES + OUT_TILES + 64)
                cols = ALL if layer == 0 else LAT
                gain_table(8, "norm1", 8 * layer, layer, 1, 2)
                norm(v, ALL, lambda k, which: coef[:, 8 + 8 * which + k:9 + 8 * which + k],
                     lambda k, which: M(layer, 0, k, which))
                v += 1
                if layer == 0:
                    dve.wait_ge(loaded, 16 * 6)
                t = t0 + 1
                dve.wait_ge(tile_done, n0 + 2)
                b = 2 * (t % 2)
                kx = kbuf[64:96, 0, NC_:T]
                chain.mark(nc.vector.tensor_tensor(kx, bank(b + 1, 0, 32), rope3[0:32, 0, :], ALU.mult))
                chain.mark(nc.vector.tensor_tensor(rtmp[64:96, :], bank(b + 1, 32, 64), rope3[32:64, 0, :],
                                                   ALU.mult))
                nc.vector.tensor_copy(kbuf[64:96, 0, 0:NC_], bank(b, 0, 32, 0, NC_))\
                  .then_inc(drained[t % 2], 1)
                chain.wait()
                dve.wait_ge(drained[t % 2], t // 2 + 1)
                chain.mark(nc.vector.tensor_tensor(kx, kx, rtmp[64:96, :], ALU.add))
                chain.wait()
                chain.mark(nc.vector.tensor_copy(kbuf[64:96, 1, :], kbuf[64:96, 0, :]))
                chain.mark(nc.vector.memset(u_pad, 0.0))
                chain.wait()
                for m in range(MOD_IN[layer] * 5 // 8):
                    mod_tile(m0 + m, m, True)
                dve.wait_ge(s["lora_sums"], 1)
                nc.vector.scalar_tensor_tensor(ckv[:, 0, :], ckv[:, 0, :], V("kvn", layer), rstd[:, :],
                                               ALU.mult, ALU.mult).then_inc(s["lora_ready"], 1)
                for m in range(MOD_IN[layer] * 5 // 8, MOD_IN[layer]):
                    mod_tile(m0 + m, m, True)
                dve.wait_ge(s["lora_sums"], 2)
                c0, c1 = cols
                for k in range(2):
                    nc.vector.scalar_tensor_tensor(cq[:, k, c0:c1], cq[:, k, c0:c1],
                                                   V("qn", 2 * layer + k), rstd[:, c0:c1],
                                                   ALU.mult, ALU.mult).then_inc(s["lora_ready"], 1)
                if MOD_IN[layer]:
                    mod_out(m0, MOD_IN[layer], group, True)
                    m0 += MOD_IN[layer]
                    group += 1
                chain.wait()
                for k in range(2):
                    t = t0 + 8 + k
                    dve.wait_ge(tile_done, n0 + 9 + k)
                    dve.wait_ge(drained[t % 2], t // 2)
                    for seg, b in both(cols):
                        o = PAD if seg == CTX else PAD + NC_ + PAD
                        last = nc.vector.tensor_tensor(u_pad[:, k, o:o + w(seg)],
                                                       bank(2 * (t % 2) + b, c1=w(seg)),
                                                       sgate[:, k, seg[0]:seg[1]], ALU.mult)
                    last.then_inc(drained[t % 2], 1)
                for k in range(6):
                    dve.wait_ge(s["v_mm"], k + 1)
                    nc.vector.tensor_copy(v1[:, k, :], bank(6 + k % 2)).then_inc(s["v_cp"], 1)
                toks = range(0 if layer == 0 else 2, 6)
                for i, k in enumerate(toks):
                    dve.wait_ge(s["ab_mm"], i + 1)
                    nc.vector.tensor_copy(ab[:, k, :], bank(i % 2)).then_inc(s["ab_cp"], 1)
                for m in range(2):
                    dve.wait_ge(s["f_hi"], m + 1)
                    for seg, b in both(cols):
                        last = nc.vector.tensor_tensor(lo3[:, m, seg[0]:seg[1]],
                                                       bank(m if b else 6 + m, c1=w(seg)),
                                                       hi3[:, m, seg[0]:seg[1]].bitcast(F32),
                                                       ALU.subtract)
                    last.then_inc(s["f_lo"], 1)

                sa = att[layer]
                plan = plans[layer]
                per = len(plan[0]) // HEADS
                npc = len(pieces_of(layer, 0))

                def rope_q(h):
                    dve.wait_ge(sa["proj_act"], npc * h + 1 if h else npc)
                    q = qbuf[64:96, h % 2, NC_:T]
                    chain.mark(nc.vector.tensor_tensor(q, q, rope3[64:96, 0, :], ALU.mult))
                    chain.mark(nc.vector.tensor_tensor(rtmp[64:96, :], rtmp[96:128, :],
                                                       rope3[96:128, 0, :], ALU.mult))
                    chain.wait()
                    nc.vector.tensor_tensor(q, q, rtmp[64:96, :], ALU.add).then_inc(sa["proj_dve"], 1)

                rope_q(0)
                x0 = 0 if layer == 0 else NC_ + PAD
                last_tap = [None]

                def tap(k):
                    if k:
                        chain.wait(last_tap[0])
                    dst = conv[:, 0, x0:CW]
                    src = u_pad[:, 0, x0 + k:CW + k]
                    wt = V("dw", 2 * layer * TAPS + k)
                    if k == 0:
                        ins = nc.vector.tensor_scalar(dst, src, wt, V("bdw", 2 * layer), ALU.mult, ALU.add)
                    else:
                        ins = nc.vector.scalar_tensor_tensor(dst, src, wt, dst, ALU.mult, ALU.add)
                    if k == TAPS - 1:
                        ins.then_inc(s["u_ready"], 1)
                    else:
                        last_tap[0] = chain.mark(ins)

                for i in (0, 1):
                    dve.wait_ge(drained[i], (t0 + 10) // 2)

                tap_steps = (HEADS - 2) * per + npc - 1

                def dve_hook(i):
                    h, j = divmod(i, per)
                    if h + 1 < HEADS and j == 1:
                        rope_q(h + 1)
                    for k in range(TAPS * i // tap_steps, min(TAPS, TAPS * (i + 1) // tap_steps)):
                        tap(k)
                    g, seg, stage = ln_stage(layer, i)
                    if stage == 0:
                        dve.wait_ge(s["u_ready"], g + 2)
                        for c in range(2):
                            last = nc.vector.scalar_tensor_tensor(
                                conv_of(c, seg), bank(7, c1=w(seg)), -1.0 / (2 * P), conv_of(c, seg),
                                ALU.mult, ALU.add)
                        last.then_inc(s["ln"], 1)
                    elif stage == 2:
                        dve.wait_ge(s["ln"], 6 * g + 4)
                        for c in range(2):
                            last = nc.vector.scalar_tensor_tensor(
                                conv_of(c, seg), conv_of(c, seg), V("lng", 2 * layer + c),
                                ckv[:, 0, 0:w(seg)], ALU.mult, ALU.mult)
                        last.then_inc(s["ln"], 1)

                attention(sa, plan, MLA_SCALE, dict(
                    pt=pt1, dve=dve_hook,
                    hi=lambda un: hi3[un["rows"][0]:un["rows"][1], 2 + un["h"] // 2,
                                      un["q0"]:un["q0"] + 256],
                    lo=lambda un: lo3[un["rows"][0]:un["rows"][1], 2 + un["h"] // 2,
                                      un["q0"]:un["q0"] + 256]))
                for m in range(2):
                    dve.wait_ge(s["p_hi"], m + 1)
                    for seg, b in both(cols):
                        last = nc.vector.tensor_tensor(lo3[:, 6 + m, seg[0]:seg[1]],
                                                       bank(4 - 2 * m + b, c1=w(seg)),
                                                       hi3[:, 6 + m, seg[0]:seg[1]].bitcast(F32),
                                                       ALU.subtract)
                    last.then_inc(s["p_lo"], 1)
                for j in range(OUT_TILES):
                    if layer and j == 0:
                        dve.wait_ge(silu_ready, 2)
                    for m in range(MOD_OUT[layer] * j // 8, MOD_OUT[layer] * (j + 1) // 8):
                        mod_tile(m0 + m, m, True)
                    if j == OUT_TILES - 1:
                        mod_out(m0, MOD_OUT[layer], group, True)
                        gain_table(8, "norm2", 8 * layer, layer, 4, 2)
                    dve.wait_ge(tile_done, n0 + IN_TILES + j + 1)
                    add_residual(t0 + IN_TILES + j, j, cols, layer, 2)
                    if j:
                        add_square(v, j - 1, cols)
                add_square(v, 7, cols)
                m0 += MOD_OUT[layer]
                group += 1
                n1, t1 = n0 + IN_TILES + OUT_TILES, t0 + IN_TILES + OUT_TILES
                for i in (0, 1):
                    dve.wait_ge(drained[i], t1 // 2)
                norm(v, cols, lambda k, which: coef[:, 8 + 8 * which + k:9 + 8 * which + k],
                     lambda k, which: M(layer, 3, k, which))
                v += 1
                e0 = 32 * layer
                per = MOD_QUARTER[layer]
                def quarter(i, last_one=False):
                    half[1] = i * per

                    def low(j):
                        dve.wait_ge(hid_hi, i * 8 + (e0 + j + 1))
                        nc.vector.tensor_tensor(hid_lo3[:, j, c0:c1], tmp2[:, j % 2, c0:c1],
                                                hid_hi3[:, j, c0:c1].bitcast(F32), ALU.subtract)\
                          .then_inc(hid_ready, 1)

                    for j in range(MLP_STEPS):
                        t = t1 + j
                        if j == 8:
                            low(7)
                            if last_one and layer:
                                add_ctx(7)
                        dve.wait_ge(tile_done, i * MLP_STEPS + (n1 + j + 1))
                        if j < 8:
                            dve.wait_ge(drained[t % 2], i * 8 + (t // 2 + 1))
                            x = tmp2[:, j % 2, c0:c1]
                            nc.vector.tensor_tensor(x, x, x, ALU.mult).then_inc(squared, 1)
                            if j:
                                low(j - 1)
                                if last_one and layer:
                                    add_ctx(j - 1)
                        else:
                            dve.wait_ge(drained[t % 2], i * 8 + (t // 2 - 3))
                            add_residual(t, j - 8, cols, layer, 5)
                            if last_one and j > 8:
                                add_square(v, j - 9, cols)
                                if layer:
                                    add_gained(j - 9)
                        if j < per:
                            mod_tile(m0 + j, j, True, shift=i * per)
                    if last_one:
                        add_square(v, 7, cols)
                        if layer:
                            add_gained(7)
                    mod_out(i * per + m0, per, i + group, True)

                half0 = half[0]
                with dve.Fori(0, QUARTERS - 1) as i:
                    quarter(i)
                half[0] = half0
                quarter(QUARTERS - 1, last_one=True)
                half[0] += (QUARTERS - 1) * per
                half[1] = None
                m0 += QUARTERS * per
                group += QUARTERS

            t2 = 2 * (IN_TILES + OUT_TILES + 64)
            for i in (0, 1):
                dve.wait_ge(drained[i], t2 // 2)
            gain_table(8, "mixn", 0, 2, 1, 2)
            dve.wait_ge(rstd_ready, v + 1)
            x = rstd[:, NC_:T]
            nc.vector.tensor_tensor(x, r_final, r_final, ALU.mult).then_inc(final_mean, 1)
            dve.wait_ge(final_mean, 1)
            nc.vector.tensor_tensor(x, bank(4), x, ALU.mult).then_inc(final_mean, 1)
            final_norm("fin1", r_final)
            v += 1
            dve.wait_ge(norm_out, 8 * 5)
            n0 = N_BLOCK2
            norm(v, ALL, lambda k, which: coef[:, 8 + 8 * which + k:9 + 8 * which + k],
                 lambda k, which: M(2, 0, k, which))
            v += 1
            nc.vector.tensor_tensor(coef[0:HD, 2:4], vec[0:HD, VEC["lam"]:VEC["lam"] + 2],
                                    vec[0:HD, VEC["lam"] + 2:VEC["lam"] + 4], ALU.mult)\
              .then_inc(s2["lam"], 1)

            def scale_heads(j):
                name, idx = QK_ORDER[j]
                dve.wait_ge(s2["sub_r"], j + 1)
                if name == "q":
                    x, r, g = q2[:, idx, :], rstd[:, NC_:T], V("gq")
                else:
                    x, r, g = k2[:, idx, :], rstd[:, :], V("gk")
                nc.vector.scalar_tensor_tensor(x, x, g, r, ALU.mult, ALU.mult).then_inc(s2["normed"], 1)

            def rope_tile(j):
                name, idx = QK_ORDER[j]
                dve.wait_ge(s2["perm"], j + 1)
                if j:
                    dve.wait_ge(s2["roped"], j)
                x = q2[:, idx, :] if name == "q" else k2[:, idx, NC_:T]
                chain.mark(nc.vector.tensor_tensor(rtmp[:, :], bank(6 + j % 2), rope3[:, 1, :], ALU.mult))
                chain.mark(nc.vector.tensor_tensor(x, x, rope3[:, 0, :], ALU.mult))
                chain.wait()
                nc.vector.tensor_tensor(x, x, rtmp[:, :], ALU.add).then_inc(s2["roped"], 1)

            dve.wait_ge(late["rope2"], 16)
            for j in range(QK_TILES):
                if 1 <= j <= N_NORMED:
                    scale_heads(j - 1)
                if j >= 2:
                    rope_tile(j - 2)
                if j < MOD_QK:
                    mod_tile(m0 + j, j, False)
            mod_out(m0, MOD_QK, group, False)
            m0 += MOD_QK
            group += 1
            rope_tile(QK_TILES - 2)
            rope_tile(QK_TILES - 1)
            dve.wait_ge(s2["lam"], 3)
            chain.mark(nc.vector.tensor_tensor(coef[:, 5:6], coef[:, 1:2], coef[:, 0:1], ALU.subtract))
            chain.wait()
            nc.vector.tensor_scalar(coef[:, 4:5], coef[:, 5:6], -LAM_INIT, None, ALU.add)\
              .then_inc(s2["lam"], 1)
            dve.wait_ge(s2["lam"], 4)
            chain.mark(nc.vector.tensor_scalar(coef[:, 6:7], V("subln"), 1.0 - LAM_INIT, None, ALU.mult))
            chain.wait()

            def dve_hook(i):
                if 2 <= i < 2 + 2 * MOD_ATT and i % 2 == 0:
                    mod_tile(m0 + i // 2 - 1, i // 2 - 1, False)
                if i == 2 + 2 * MOD_ATT:
                    mod_out(m0, MOD_ATT, group, False)
                for h in range(4):
                    stage = i - SUB_AT - SUB_STEP * h
                    if stage == 3:
                        dve.wait_ge(s2["sub_r"], N_NORMED + h + 1)
                        x = diff_out[:, h, :]
                        nc.vector.scalar_tensor_tensor(x, x, coef[:, 6:7], rstd[:, 0:NX],
                                                       ALU.mult, ALU.mult).then_inc(s2["mix_t"], 1)
                    elif stage == 5:
                        dve.wait_ge(s2["mix_hi"], h + 1)
                        nc.vector.tensor_tensor(mix_lo[:, h, :], diff_out[:, h, :],
                                                mix_hi[:, h, :].bitcast(F32), ALU.subtract)\
                          .then_inc(s2["mix_lo"], 1)

            attention(att[2], plans[2], GQA_SCALE, dict(
                pt=pt2, dve=dve_hook,
                hi=lambda un: mix_hi[un["rows"][0]:un["rows"][1], 4 + un["h"] // 2,
                                     un["q0"]:un["q0"] + 256],
                lo=lambda un: mix_lo[un["rows"][0]:un["rows"][1], 4 + un["h"] // 2,
                                     un["q0"]:un["q0"] + 256]))
            t3 = t2 + QK_TILES + V_OUTS + OUT_TILES
            gain_table(8, "ffnn", 0, 2, 4, 1)
            for j in range(OUT_TILES):
                dve.wait_ge(tile_done, n0 + QK_TILES + V_TILES + j + 1)
                add_residual(t3 - OUT_TILES + j, j, LAT, 2, 2)
                if j:
                    add_square(v, j - 1, LAT)
            add_square(v, 7, LAT)
            for i in (0, 1):
                dve.wait_ge(drained[i], t3 // 2)

            def norm_latents(v, block_, chunk):
                norm(v, LAT, lambda k, which: coef[:, 8 + 8 * which + k:9 + 8 * which + k],
                     lambda k, which: M(block_, chunk, k, which))

            norm_latents(v, 2, 3)
            v += 1

            def ffn(layer, tb):
                nf = N_FFN[layer]
                pair0 = 0
                for part, kk in enumerate(FFN_PARTS):
                    nb = nf + sum(3 * x for x in FFN_PARTS[:part])
                    tb_part = tb + sum(2 * x + 8 for x in FFN_PARTS[:part])
                    e0 = layer * FFN_T + pair0
                    with dve.Fori(0, kk // 2) as i:
                        for j in range(4):
                            q, is_up = j // 2, j % 2
                            x = (ups if is_up else gates)[:, q, :]
                            t = tb_part + j
                            col = VEC["fcw"] + layer * 132 + 2 * pair0 + j
                            dve.wait_ge(s2["g_ready"], i * 4 + (2 * e0 + j + 1))
                            side = nc.vector.scalar_tensor_tensor(
                                x[:, 1:NX], bank(2 * (t % 2) + 1, c1=NX - 1),
                                vec[:, bass.ds(i * 4 + col, 1)], x[:, 1:NX], ALU.mult, ALU.add)
                            side.then_inc(s2["f_lo"], 1)
                            dve.wait_ge(s2["f_lo"], i * 4 + (2 * e0 + j + 1))
                            nc.vector.scalar_tensor_tensor(
                                x[:, 0:NX - 1], bank(2 * (t % 2) + 1, c0=1, c1=NX),
                                vec[:, bass.ds(i * 4 + (col + 88), 1)], x[:, 0:NX - 1],
                                ALU.mult, ALU.add).then_inc(drained[t % 2], 1)
                            if is_up:
                                dve.wait_ge(s2["f_hi"], i * 2 + (e0 + q + 1))
                                dve.wait_ge(drained[t % 2], i * 2 + (t // 2 + 1))
                                nc.vector.tensor_tensor(prods[:, q, :], gates[:, q, :], ups[:, q, :],
                                                        ALU.mult).then_inc(s2["prod"], 1)
                                dve.wait_ge(hid_hi, i * 2 + (64 + e0 + q + 1))
                                nc.vector.tensor_tensor(
                                    hid_lo_f[:, bass.ds(i * 2 * NX + q * NX, NX)], prods[:, q, :],
                                    hid_hi_f[:, bass.ds(i * 2 * NX + q * NX, NX)].bitcast(F32),
                                    ALU.subtract).then_inc(hid_ready, 1)
                    for m in range(8):
                        t = tb_part + 2 * kk + m
                        end = (m + 1) * kk
                        if end % 8:
                            dve.wait_ge(p_chain, marks[layer, part, m])
                        else:
                            dve.wait_ge(tile_done, nb + 2 * kk + end // 8)
                        if part:
                            dve.wait_ge(drained[t % 2], t // 2 - 3)
                        add_residual(t, m, LAT, 2 + layer, 5)
                        if part and m:
                            add_square(v, m - 1, LAT)
                    pair0 += kk

            gain_table(8, "mixn", 8, 3, 1, 1)
            ffn(0, t3)
            add_square(v, 7, LAT)
            t4 = t3 + 2 * FFN_T + 16
            for i in (0, 1):
                dve.wait_ge(drained[i], t4 // 2)
            norm_latents(v, 3, 0)
            v += 1
            t5 = t4 + SGU_U + SGU_V_OUTS
            dve.wait_ge(s2["sv"], 1)
            for k in range(4):
                last = nc.vector.tensor_scalar(sv[:, k, :], sv[:, k, :], tiny[:, 20 + k:21 + k], None,
                                               ALU.mult)
                if k < 3:
                    chain.mark(last)
            last.then_inc(s2["sv"], 1)
            dve.wait_ge(late["sgu"], 32)

            def mix_low(c):
                dve.wait_ge(s2["mix_hi"], 4 + c + 1)
                nc.vector.tensor_tensor(mix_lo[:, c, :], tmp2[:, c % 2, 0:NX],
                                        mix_hi[:, c, :].bitcast(F32), ALU.subtract)\
                  .then_inc(s2["mix_lo"], 1)

            for c in range(8):
                dve.wait_ge(s2["mixed"], c + 1)
                if c >= 2:
                    dve.wait_ge(s2["mix_lo"], 4 + c - 1)
                for n in range(4):
                    chain.mark(nc.vector.scalar_tensor_tensor(
                        tmp2[:, c % 2, n * P:(n + 1) * P], bank(4 + c % 2, c0=n * P, c1=(n + 1) * P),
                        V("vn", c), bs[:, c // 2, :], ALU.mult, ALU.add))
                chain.wait()
                nc.vector.tensor_tensor(tmp2[:, c % 2, 0:NX], tmp2[:, c % 2, 0:NX], su[:, c, :],
                                        ALU.mult).then_inc(s2["mix_t"], 1)
                if c:
                    mix_low(c - 1)
            mix_low(7)
            gain_table(8, "ffnn", 8, 3, 4, 1)
            for j in range(OUT_TILES):
                dve.wait_ge(tile_done, N_SGU + SGU_U + SGU_V + j + 1)
                add_residual(t5 + j, j, LAT, 3, 2)
                if j:
                    add_square(v, j - 1, LAT)
            add_square(v, 7, LAT)
            t6 = t5 + OUT_TILES
            for i in (0, 1):
                dve.wait_ge(drained[i], t6 // 2)
            norm_latents(v, 3, 3)
            v += 1
            ffn(1, t6)
            add_square(v, 7, LAT)
            t7 = t6 + 2 * FFN_T + 16
            for i in (0, 1):
                dve.wait_ge(drained[i], t7 // 2)
            dve.wait_ge(rstd_ready, v + 1)
            final_norm("fin2", rstd[:, NC_:T])


def blocks(wt, ks, cols):
    return wt.reshape(-1, P, wt.shape[1])[np.asarray(ks)][:, :, np.asarray(cols)].transpose(1, 0, 2)


def columns(v):
    return v.reshape(-1, P).T


def stream_tiles(i):
    k8 = range(8)
    m = lambda c: range(c * P, (c + 1) * P)
    for l in (0, 1):
        wi = i["w_in"][l]
        f, q, kv, r = 256, 512, 640, 672
        kr = list(range(kv, r))
        turned = kr[16:] + kr[:16]
        for c in ([range(q, kv), kr + turned + kr + turned, range(f, f + P), range(f + P, q), m(0), m(1)]
                  + [range(r + o, r + o + P) for o in (256, 384, 0, 128)]):
            yield blocks(wi, k8, list(c))
        for c in range(8):
            yield blocks(i["w_o"][l], k8, list(m(c)))
        for part in range(QUARTERS):
            for c in range(8):
                yield blocks(i["w_mlp1"][l], k8, list(m(8 * part + c)))
            for c in range(8):
                yield blocks(i["w_mlp2"][l], range(8 * part, 8 * part + 8), list(m(c)))
    wi = i["attn_w_in_2"][0]
    pairs = lambda o: [o + 2 * x for x in range(32)] + [o + 2 * x + 1 for x in range(32)]
    q1, q2, k1, k2, va, qb, kb, vb = 0, 256, 512, 768, 1024, 1536, 2048, 2176
    for c in range(4):
        yield blocks(wi, k8, pairs(qb + 64 * c) + pairs(qb + 64 * (c + 4)))
    yield blocks(wi, k8, pairs(kb) + pairs(kb + 64))
    for o in (q1, q2, k1, k2):
        for c in range(2):
            yield blocks(wi, k8, pairs(o + 128 * c) + pairs(o + 128 * c + 64))
    for c in range(2):
        for half in (range(4), range(4, 8)):
            yield blocks(wi, half, list(range(va + 256 * c, va + 256 * (c + 1))))
    yield blocks(wi, k8, list(range(vb, vb + P)))
    wo = i["attn_w_out_2"][0]
    rows = list(range(512)) + [512 + 64 * h + x for c in range(4) for h in (c, c + 4) for x in range(64)]
    for c in range(8):
        yield blocks(wo[rows], k8, list(m(c)))

    def ffn(l):
        up, down = i["ffn_w_up_2"][l], i["ffn_w_down_2"][l]
        first = 0
        for kk in FFN_PARTS:
            for c in range(first, first + kk):
                yield blocks(up, k8, list(m(c)))
                yield blocks(up, k8, list(m(FFN_T + c)))
            flat = np.concatenate([blocks(down, range(first, first + kk), list(m(c))) for c in range(8)], 1)
            for b in range(0, 8 * kk, 8):
                yield flat[:, b:b + 8]
            first += kk

    yield from ffn(0)
    for c in range(8):
        yield blocks(i["sgu_w_in_2"][0], k8, list(m(c)))
    for c in range(4):
        for half in (range(4), range(4, 8)):
            yield blocks(i["sgu_w_in_2"][0], half, list(range(D + 256 * c, D + 256 * (c + 1))))
    for c in range(8):
        yield blocks(i["sgu_w_out_2"][0], k8, list(m(c)))
    yield from ffn(1)


def mod_tiles(i):
    for wt in (i["w_mod"][0], i["w_mod"][1], i["ada_w_2"][0], i["ada_w_2"][1]):
        for c in range(CH):
            yield wt[:, c * P:(c + 1) * P].T


def vector_table(i):
    pair = [2 * x for x in range(32)] + [2 * x + 1 for x in range(32)]
    turn = lambda v: v[pair]
    parts = [columns(i["b_mod"][0]), columns(i["b_mod"][1]), columns(i["ada_b_2"][0]),
             columns(i["ada_b_2"][1])]
    for name in ("norm1_g", "norm2_g"):
        parts += [columns(i[name][l]) for l in (0, 1)]
    parts.append(columns(i["final_norm_g"]))
    for name in ("q_norm_g", "kv_norm_g"):
        parts += [columns(i[name][l]) for l in (0, 1)]
    parts += [i["w_dw"][l].T[c * P:(c + 1) * P] for l in (0, 1) for c in (0, 1)]
    for name in ("b_dw", "conv_ln_g", "conv_ln_b"):
        parts += [columns(i[name][l]) for l in (0, 1)]
    for name in ("mix_norm_2", "ffn_norm_2"):
        parts += [columns(i[name][l]) for l in (0, 1)]
    parts.append(columns(i["final_norm_2"]))
    parts.append(columns(i["diff_subln_2"][0]))
    for name in ("gqa_q_norm_2", "gqa_k_norm_2"):
        half = turn(i[name][0])
        parts.append(np.concatenate([half, half])[:, None])
    parts.append(columns(i["sgu_v_norm_2"][0]))
    lam = np.stack([i[f"diff_{n}_2"][0] for n in ("lq1", "lq2", "lk1", "lk2")], 1)
    parts.append(np.concatenate([lam, lam]))
    order = [c + x for c in range(FFN_T) for x in (0, FFN_T)]
    for l in (0, 1):
        for tap in range(3):
            parts.append(columns(i["ffn_conv_w_2"][l, tap])[:, order])
    for l in (0, 1):
        parts.append(columns(i["ffn_conv_b_2"][l])[:, order])
    return np.concatenate(parts, 1)


def small_weights(i, l):
    wq = i["w_uq"][l]
    parts = []
    for h in range(HEADS):
        o = 96 * h
        r = list(range(o + 64, o + 96))
        parts.append(blocks(wq, range(2), list(range(o, o + 64)) + r + r[16:] + r[:16]).reshape(P, -1))
    wkv = i["w_ukv"][l].reshape(P, HEADS, 2, 64)
    parts += [wkv[:, :, 0].reshape(P, -1), wkv[:, :, 1].reshape(P, -1)]
    for name in ("w_fourier", "w_pw2"):
        for m in range(2):
            parts.append(blocks(i[name][l], range(2), list(range(m * P, (m + 1) * P))).reshape(P, -1))
    return np.concatenate(parts, 1)


def tokens(x):
    return x.T.reshape(KD, P, -1).transpose(1, 0, 2)


def shape_tables():
    t = np.arange(NX)
    row, col = t // GRID_W, t % GRID_W

    def angles(n):
        inv = 10000.0 ** (-np.arange(n, dtype=np.float32) / n)
        return np.concatenate([row[:, None] * inv, col[:, None] * inv], 1).T

    a1 = angles(8)
    c1, s1 = np.cos(a1), np.sin(a1)
    cos1, sin1 = np.concatenate([c1, c1]), np.concatenate([-s1, s1])
    a2 = angles(16)
    c2, s2 = np.cos(a2), np.sin(a2)
    cos2 = np.concatenate([c2] * 4)
    sin2 = np.concatenate([-s2, s2] * 2)
    half = np.eye(P).reshape(2, 2, 32, P)[:, ::-1].reshape(P, P)

    def dft(n):
        a = 2 * np.pi * np.outer(np.arange(n), np.arange(n)) / n
        return np.cos(a) / np.sqrt(n), np.sin(a) / np.sqrt(n)

    def positions(n):
        c, s = dft(n)
        return np.stack([c, -s]).reshape(2, n // P, P, n).transpose(2, 0, 1, 3).reshape(P, -1)

    c64, s64 = dft(64)
    chan = np.concatenate([np.kron(np.eye(2), c64), np.kron(np.eye(2), s64)], 1)
    out = dict(identity=np.eye(P), pair_swap=half, half_ones=np.kron(np.eye(2), np.ones((64, 64))),
               channel_dft=chan, rope1=np.concatenate([cos1, sin1] * 2),
               rope2=np.concatenate([cos2, sin2], 1), dft_x=positions(NX), dft_c=positions(NC_))
    return {k: np.ascontiguousarray(v, dtype=np.float32) for k, v in out.items()}


def layouts(i):
    conditions = np.stack([np.tile(np.concatenate([i[c].reshape(-1), i[cc].reshape(-1)]), (P, 1))
                           for c, cc in (("c", "c_ctx"), ("c_2", "c_ctx_2"))])
    out = dict(
        stream=np.stack([b.reshape(P, 1024) for b in stream_tiles(i)]),
        mods=np.stack(list(mod_tiles(i))),
        vectors=vector_table(i), conditions=conditions,
        tokens=tokens(np.concatenate([i["ctx"][0], i["x"][0]])),
        context2=tokens(i["ctx_2"][0]),
        small_w=np.stack([small_weights(i, l) for l in (0, 1)]),
        w_s=i["sgu_w_s_2"][0].transpose(2, 0, 1).reshape(P, -1),
        b_s=np.tile(i["sgu_b_s_2"][0].reshape(1, -1), (P, 1)))
    out.update(shape_tables())
    return {k: np.ascontiguousarray(v) for k, v in out.items()}


def kernel(**inputs):
    import concourse.bacc as bacc
    from concourse.bass_utils import run_bass_kernel_spmd

    arrays = {f"{k}_dram": v for k, v in layouts({k: np.asarray(v) for k, v in inputs.items()}).items()}
    nc = bacc.Bacc("TRN2", target_bir_lowering=False, num_devices=1)
    aps = {k[:-5]: nc.dram_tensor(k, v.shape, mybir.dt.from_np(v.dtype), kind="ExternalInput").ap()
           for k, v in arrays.items()}
    aps["out"] = nc.dram_tensor("out_dram", (P, KD, NX), F32, kind="ExternalOutput").ap()
    two_towers(nc, aps)
    r = run_bass_kernel_spmd(nc, [arrays], core_ids=[0])
    got = r.results[0]["out_dram"]
    return np.ascontiguousarray(got.transpose(2, 1, 0).reshape(1, NX, D))
```
